# Optimizing a Trainium2 kernel written in Bass

```python
import math
import jax, jax.numpy as jnp
from jax import lax
import numpy as np

D_MODEL = 1024
BATCH = 1
SEQ = 128
DEPTH = 1
DEC_BATCH = 1
DEC_SEQ = 512
PAST_LEN = 128

GRID_W = 64
MLSTM_WIDTH = 1024
MLSTM_HEADS = 4
MLSTM_HEAD_DIM = MLSTM_WIDTH // MLSTM_HEADS
MLSTM_CHUNK = 64
S5_WIDTH = 512
S5_GROUP = 16
S5_GROUPS = S5_WIDTH // S5_GROUP
S5_STATE = 64
N_EXPERTS = 16
EXPERT_FF = 1536
CAPACITY_FACTOR = 2
N_DIRS = 2
N_MOD = 6
EPS = 1e-6
IN_SPLITS = [MLSTM_WIDTH, 2 * MLSTM_WIDTH, 3 * MLSTM_WIDTH, 4 * MLSTM_WIDTH,
             4 * MLSTM_WIDTH + 4 * MLSTM_HEADS,
             4 * MLSTM_WIDTH + 4 * MLSTM_HEADS + S5_WIDTH,
             4 * MLSTM_WIDTH + 4 * MLSTM_HEADS + S5_WIDTH + D_MODEL]
IN_COLS = 4 * MLSTM_WIDTH + 4 * MLSTM_HEADS + S5_WIDTH + 2 * D_MODEL

kernel_name = "hybrid_mlstm_s5_ec_diffusion_step"

def rmsnorm(x, g):
    x32 = x.astype(jnp.float32)
    y = x32 * lax.rsqrt(jnp.mean(x32 * x32, axis=-1, keepdims=True) + EPS)
    return (y * g.astype(jnp.float32)).astype(x.dtype)

def adaln(cvec, w, b):
    m = jax.nn.silu(cvec) @ w + b
    return m.reshape(cvec.shape[0], N_MOD, D_MODEL)

def modulate(x, shift, scale):
    return x * (1 + scale[:, None]) + shift[:, None]

def pos2d(T, dtype):
    rows = T // GRID_W
    r, cl = jnp.meshgrid(jnp.arange(rows, dtype=jnp.float32), jnp.arange(GRID_W, dtype=jnp.float32), indexing='ij')
    r, cl = r.reshape(-1), cl.reshape(-1)
    quarter = D_MODEL // 4
    freqs = 1.0 / (10000.0 ** (jnp.arange(quarter, dtype=jnp.float32) / quarter))
    er, ec = r[:, None] * freqs, cl[:, None] * freqs
    return jnp.concatenate([jnp.sin(er), jnp.cos(er), jnp.sin(ec), jnp.cos(ec)], axis=-1).astype(dtype)

def mlstm_chunkwise(q, k, v, ig, lf, C0, n0, m0):
    B, H, T, dh = q.shape
    nc = T // MLSTM_CHUNK

    def chunks(a):
        return jnp.moveaxis(a.reshape(a.shape[:2] + (nc, MLSTM_CHUNK) + a.shape[3:]), 2, 0)

    causal = jnp.tril(jnp.ones((MLSTM_CHUNK, MLSTM_CHUNK), dtype=bool))

    def step(carry, inp):
        C, n, m = carry
        qc, kc, vc, ic, fc = inp
        b = jnp.cumsum(fc, axis=-1)
        dmat = jnp.where(causal, b[..., :, None] - b[..., None, :] + ic[..., None, :], -jnp.inf)
        m_inter = b + m[..., None]
        m_t = jnp.maximum(m_inter, jnp.max(dmat, axis=-1))
        w_inter = jnp.exp(m_inter - m_t)
        s = jnp.einsum('bhtd,bhsd->bhts', qc, kc) * jnp.exp(dmat - m_t[..., None])
        num = w_inter[..., None] * jnp.einsum('bhtd,bhde->bhte', qc, C) + jnp.einsum('bhts,bhse->bhte', s, vc)
        den = w_inter * jnp.einsum('bhtd,bhd->bht', qc, n) + jnp.sum(s, axis=-1)
        h = num / jnp.maximum(jnp.abs(den), jnp.exp(-m_t))[..., None]
        b_last = b[..., -1]
        g = b_last[..., None] - b + ic
        m_new = jnp.maximum(b_last + m, jnp.max(g, axis=-1))
        decay = jnp.exp(b_last + m - m_new)
        wk = jnp.exp(g - m_new[..., None])
        C_new = decay[..., None, None] * C + jnp.einsum('bhs,bhsd,bhse->bhde', wk, kc, vc)
        n_new = decay[..., None] * n + jnp.einsum('bhs,bhsd->bhd', wk, kc)
        return (C_new, n_new, m_new), h

    (C, n, m), hs = lax.scan(step, (C0, n0, m0), (chunks(q), chunks(k), chunks(v), chunks(ig), chunks(lf)))
    h = jnp.moveaxis(hs, 0, 2).reshape(B, H, T, dh)
    return h, C, n, m

def s5_scan(u, a_re, a_im, log_dt, b_c, c_c, x0):
    A = lax.complex(a_re.astype(jnp.float32), a_im.astype(jnp.float32))
    dt = jnp.exp(log_dt.astype(jnp.float32))[:, None]
    a_bar = jnp.exp(A * dt)
    b_bar = ((a_bar - 1.0) / A)[..., None] * b_c
    bu = jnp.einsum('gpc,btgc->btgp', b_bar, u.astype(jnp.complex64))
    bu = bu.at[:, 0].add(a_bar * x0)
    a = jnp.broadcast_to(a_bar, bu.shape)

    def combine(l, r):
        return (r[0] * l[0], r[0] * l[1] + r[1])

    _, xs = lax.associative_scan(combine, (a, bu), axis=1)
    y = jnp.real(jnp.einsum('gcp,btgp->btgc', c_c, xs))
    return y, xs[:, -1]

def mixer(h, C0, n0, m0, s0, p):
    B, T, _ = h.shape
    f32 = jnp.float32
    proj = h @ p['w_in']
    q, k, v, o, gates, u, ga, gb = jnp.split(proj, IN_SPLITS, axis=-1)

    def heads(a):
        return a.reshape(B, T, MLSTM_HEADS, MLSTM_HEAD_DIM).transpose(0, 2, 1, 3).astype(f32)

    def flip_t(a):
        return jnp.flip(a, axis=2)

    qh = heads(q) * (MLSTM_HEAD_DIM ** -0.5)
    kh, vh = heads(k), heads(v)
    gt = (gates.reshape(B, T, 4, MLSTM_HEADS).astype(f32) + p['b_gate'].astype(f32)).transpose(0, 2, 3, 1)
    hf, Cf, nf, mf = mlstm_chunkwise(qh, kh, vh, gt[:, 0], jax.nn.log_sigmoid(gt[:, 1]),
                                     C0[:, 0], n0[:, 0], m0[:, 0])
    hb, Cb, nb, mb = mlstm_chunkwise(flip_t(qh), flip_t(kh), flip_t(vh), flip_t(gt[:, 2]),
                                     flip_t(jax.nn.log_sigmoid(gt[:, 3])), C0[:, 1], n0[:, 1], m0[:, 1])
    hm = (hf + flip_t(hb)) * jax.nn.sigmoid(heads(o))
    hm = hm * lax.rsqrt(jnp.mean(hm * hm, axis=-1, keepdims=True) + EPS) * p['head_norm'].astype(f32)[None, :, None, :]
    h_a = hm.transpose(0, 2, 1, 3).reshape(B, T, MLSTM_WIDTH).astype(h.dtype)

    u32 = u.astype(f32).reshape(B, T, S5_GROUPS, S5_GROUP)
    b_c = lax.complex(p['s5_b_re'].astype(f32), p['s5_b_im'].astype(f32))
    c_c = lax.complex(p['s5_c_re'].astype(f32), p['s5_c_im'].astype(f32))
    yf, xf = s5_scan(u32, p['s5_a_re'][0], p['s5_a_im'][0], p['s5_log_dt'][0], b_c, c_c[0], s0[:, 0])
    yb, xb = s5_scan(jnp.flip(u32, axis=1), p['s5_a_re'][1], p['s5_a_im'][1], p['s5_log_dt'][1], b_c, c_c[1], s0[:, 1])
    z = (yf + jnp.flip(yb, axis=1)).reshape(B, T, S5_WIDTH) + p['s5_d'].astype(f32) * u32.reshape(B, T, S5_WIDTH)
    h_b = (jax.nn.gelu(z) * jax.nn.sigmoid(z @ p['w_glu'].astype(f32) + p['b_glu'].astype(f32))).astype(h.dtype)

    merged = jax.nn.sigmoid(ga) * (h_a @ p['w_pA']) + jax.nn.sigmoid(gb) * (h_b @ p['w_pB'])
    out = merged @ p['w_out']
    C = jnp.stack([Cf, Cb], axis=1)
    n = jnp.stack([nf, nb], axis=1)
    m = jnp.stack([mf, mb], axis=1)
    s = jnp.stack([xf, xb], axis=1)
    return out, C, n, m, s

def ec_moe(h, w_router, b_router, w1, w3, w2):
    B, T, D = h.shape
    cap = CAPACITY_FACTOR * T // N_EXPERTS
    aff = jax.nn.softmax((h @ w_router).astype(jnp.float32) + b_router.astype(jnp.float32), axis=-1)
    topv, topi = lax.top_k(jnp.swapaxes(aff, 1, 2), cap)
    xe = jax.vmap(lambda hb, ib: hb[ib])(h, topi)
    hid = jax.nn.silu(jnp.einsum('becd,edf->becf', xe, w1)) * jnp.einsum('becd,edf->becf', xe, w3)
    ye = jnp.einsum('becf,efd->becd', hid, w2) * topv[..., None].astype(h.dtype)
    return jax.vmap(lambda ib, yb: jnp.zeros((T, D), h.dtype).at[ib.reshape(-1)].add(yb.reshape(-1, D)))(topi, ye)

def layer_stream(x, mod, C0, n0, m0, s0, p):
    shift1, scale1, gate1, shift2, scale2, gate2 = (mod[:, i] for i in range(N_MOD))
    h = modulate(rmsnorm(x, p['norm_mix']), shift1, scale1)
    out, C, n, m, s = mixer(h, C0, n0, m0, s0, p)
    x = x + gate1[:, None] * out
    h = modulate(rmsnorm(x, p['norm_ffn']), shift2, scale2)
    x = x + gate2[:, None] * ec_moe(h, p['w_router'], p['b_router'], p['w_e1'], p['w_e3'], p['w_e2'])
    return x, C, n, m, s

def setup_inputs(seed: int = 0) -> dict:
    key = jax.random.key(seed)
    ks = jax.random.split(key, 40)
    f32 = jnp.float32

    def nrm(k, shape, s):
        return jax.random.normal(k, shape, f32) * s

    H, DH, G, P = MLSTM_HEADS, MLSTM_HEAD_DIM, S5_GROUPS, S5_STATE
    fbias = jnp.linspace(3.0, 6.0, H, dtype=f32)
    base_gate = jnp.stack([jnp.zeros((H,), f32), fbias, jnp.zeros((H,), f32), fbias])
    return {
        "x_prompt": nrm(ks[0], (BATCH, SEQ, D_MODEL), 1.0),
        "x_sample": nrm(ks[1], (DEC_BATCH, DEC_SEQ, D_MODEL), 1.0),
        "state_mlstm_C": nrm(ks[2], (DEC_BATCH, DEPTH, N_DIRS, H, DH, DH), 0.1),
        "state_mlstm_n": nrm(ks[3], (DEC_BATCH, DEPTH, N_DIRS, H, DH), 0.5),
        "state_mlstm_m": nrm(ks[4], (DEC_BATCH, DEPTH, N_DIRS, H), 1.0),
        "state_s5_re": nrm(ks[5], (DEC_BATCH, DEPTH, N_DIRS, G, P), 0.1),
        "state_s5_im": nrm(ks[6], (DEC_BATCH, DEPTH, N_DIRS, G, P), 0.1),
        "c": nrm(ks[7], (DEC_BATCH, D_MODEL), 1.0),
        "c_ctx": nrm(ks[8], (D_MODEL,), 1.0),
        "w_ada": nrm(ks[9], (DEPTH, D_MODEL, N_MOD * D_MODEL), D_MODEL ** -0.5),
        "b_ada": nrm(ks[10], (DEPTH, N_MOD * D_MODEL), 0.01),
        "norm_mix": 1.0 + nrm(ks[11], (DEPTH, D_MODEL), 0.02),
        "norm_ffn": 1.0 + nrm(ks[12], (DEPTH, D_MODEL), 0.02),
        "w_in": nrm(ks[13], (DEPTH, D_MODEL, IN_COLS), D_MODEL ** -0.5),
        "b_gate": base_gate[None] + nrm(ks[14], (DEPTH, 4, H), 0.1),
        "head_norm": 1.0 + nrm(ks[15], (DEPTH, H, DH), 0.02),
        "s5_a_re": -0.5 + nrm(ks[16], (DEPTH, N_DIRS, G, P), 0.01),
        "s5_a_im": jnp.pi * jnp.arange(P, dtype=f32) + nrm(ks[17], (DEPTH, N_DIRS, G, P), 0.01),
        "s5_log_dt": jax.random.uniform(ks[18], (DEPTH, N_DIRS, G), f32, math.log(1e-3), math.log(1e-1)),
        "s5_b_re": nrm(ks[19], (DEPTH, G, P, S5_GROUP), (2 * S5_GROUP) ** -0.5),
        "s5_b_im": nrm(ks[20], (DEPTH, G, P, S5_GROUP), (2 * S5_GROUP) ** -0.5),
        "s5_c_re": nrm(ks[21], (DEPTH, N_DIRS, G, S5_GROUP, P), (2 * P) ** -0.5),
        "s5_c_im": nrm(ks[22], (DEPTH, N_DIRS, G, S5_GROUP, P), (2 * P) ** -0.5),
        "s5_d": nrm(ks[23], (DEPTH, S5_WIDTH), 1.0),
        "w_glu": nrm(ks[24], (DEPTH, S5_WIDTH, S5_WIDTH), S5_WIDTH ** -0.5),
        "b_glu": nrm(ks[25], (DEPTH, S5_WIDTH), 0.01),
        "w_pA": nrm(ks[26], (DEPTH, MLSTM_WIDTH, D_MODEL), MLSTM_WIDTH ** -0.5),
        "w_pB": nrm(ks[27], (DEPTH, S5_WIDTH, D_MODEL), S5_WIDTH ** -0.5),
        "w_out": nrm(ks[28], (DEPTH, D_MODEL, D_MODEL), D_MODEL ** -0.5),
        "w_router": nrm(ks[29], (DEPTH, D_MODEL, N_EXPERTS), D_MODEL ** -0.5),
        "b_router": nrm(ks[30], (DEPTH, N_EXPERTS), 0.01),
        "w_e1": nrm(ks[31], (DEPTH, N_EXPERTS, D_MODEL, EXPERT_FF), D_MODEL ** -0.5),
        "w_e3": nrm(ks[32], (DEPTH, N_EXPERTS, D_MODEL, EXPERT_FF), D_MODEL ** -0.5),
        "w_e2": nrm(ks[33], (DEPTH, N_EXPERTS, EXPERT_FF, D_MODEL), EXPERT_FF ** -0.5),
        "norm_final": 1.0 + nrm(ks[34], (D_MODEL,), 0.02),
    }

def reference(x_prompt, x_sample, state_mlstm_C, state_mlstm_n, state_mlstm_m, state_s5_re, state_s5_im,
              c, c_ctx, w_ada, b_ada, norm_mix, norm_ffn, w_in, b_gate, head_norm,
              s5_a_re, s5_a_im, s5_log_dt, s5_b_re, s5_b_im, s5_c_re, s5_c_im, s5_d, w_glu, b_glu,
              w_pA, w_pB, w_out, w_router, b_router, w_e1, w_e3, w_e2, norm_final):
    f32 = jnp.float32
    Bp = x_prompt.shape[0]
    xp = x_prompt
    xs = x_sample + pos2d(x_sample.shape[1], x_sample.dtype)[None]
    new_C, new_n, new_m, new_re, new_im = [], [], [], [], []
    for l in range(DEPTH):
        p = {"norm_mix": norm_mix[l], "norm_ffn": norm_ffn[l], "w_in": w_in[l], "b_gate": b_gate[l],
             "head_norm": head_norm[l], "s5_a_re": s5_a_re[l], "s5_a_im": s5_a_im[l],
             "s5_log_dt": s5_log_dt[l], "s5_b_re": s5_b_re[l], "s5_b_im": s5_b_im[l],
             "s5_c_re": s5_c_re[l], "s5_c_im": s5_c_im[l], "s5_d": s5_d[l], "w_glu": w_glu[l],
             "b_glu": b_glu[l], "w_pA": w_pA[l], "w_pB": w_pB[l], "w_out": w_out[l],
             "w_router": w_router[l], "b_router": b_router[l], "w_e1": w_e1[l], "w_e3": w_e3[l],
             "w_e2": w_e2[l]}
        mod_ctx = adaln(c_ctx[None], w_ada[l], b_ada[l])
        mod_lat = adaln(c, w_ada[l], b_ada[l])
        z_C = jnp.zeros((Bp, N_DIRS, MLSTM_HEADS, MLSTM_HEAD_DIM, MLSTM_HEAD_DIM), f32)
        z_n = jnp.zeros((Bp, N_DIRS, MLSTM_HEADS, MLSTM_HEAD_DIM), f32)
        z_m = jnp.zeros((Bp, N_DIRS, MLSTM_HEADS), f32)
        z_s = jnp.zeros((Bp, N_DIRS, S5_GROUPS, S5_STATE), jnp.complex64)
        xp, C_l, n_l, m_l, s_l = layer_stream(xp, mod_ctx, z_C, z_n, z_m, z_s, p)
        new_C.append(C_l)
        new_n.append(n_l)
        new_m.append(m_l)
        new_re.append(jnp.real(s_l))
        new_im.append(jnp.imag(s_l))
        s0 = lax.complex(state_s5_re[:, l].astype(f32), state_s5_im[:, l].astype(f32))
        xs, _, _, _, _ = layer_stream(xs, mod_lat, state_mlstm_C[:, l].astype(f32),
                                      state_mlstm_n[:, l].astype(f32), state_mlstm_m[:, l].astype(f32), s0, p)
    y_prompt = rmsnorm(xp, norm_final)
    y_sample = rmsnorm(xs, norm_final)
    dt = x_prompt.dtype
    out_C = jnp.stack(new_C, axis=1).astype(dt)
    out_n = jnp.stack(new_n, axis=1).astype(dt)
    out_m = jnp.stack(new_m, axis=1).astype(dt)
    out_re = jnp.stack(new_re, axis=1).astype(dt)
    out_im = jnp.stack(new_im, axis=1).astype(dt)
    return (y_prompt, y_sample, out_C, out_n, out_m, out_re, out_im)


_drawn_inputs = setup_inputs


def setup_inputs(seed=0):
    import zlib

    import numpy as np

    out = dict(_drawn_inputs(seed))
    spreads = {}
    factors = {'state_mlstm_C': 8.0,
     'state_mlstm_n': 8.0,
     'state_mlstm_m': 8.0,
     'state_s5_re': 8.0,
     'state_s5_im': 5.119,
     'norm_ffn': 3.379,
     'head_norm': 5.061,
     's5_a_re': 4.637,
     's5_c_re': 3.251,
     's5_c_im': 3.138,
     'b_glu': 8.0,
     'b_router': 4.693,
     'norm_final': 2.841}
    for name, (base, spread) in spreads.items():
        noise = np.random.default_rng([zlib.crc32(name.encode()), seed]).standard_normal(out[name].shape)
        drawn = base * np.exp(spread * noise) if base else spread * noise
        out[name] = __import__('jax').numpy.asarray(drawn.astype(out[name].dtype))
    for name, factor in factors.items():
        out[name] = (out[name] * factor).astype(out[name].dtype)
    return out
```

```python
from contextlib import ExitStack

import numpy as np
import concourse.bass as bass
from concourse import mybir

F32 = mybir.dt.float32
U32 = mybir.dt.uint32
I32 = mybir.dt.int32
ALU = mybir.AluOpType
ACT = mybir.ActivationFunctionType
AX = mybir.AxisListType

P = 128
D = 1024
KD = D // P
LAT, CTX = 512, 128
TOK = LAT + CTX
NT = TOK // P
H, DH = 4, 256
MW = H * DH
SW, GC, GN, SP_ = 512, 16, 32, 64
L = 8
JL, JC = LAT // L, CTX // L
J = JL + JC
NS_ = (JL + 1) + (JC + 1)
QG = 8
NQ = GN // QG
E, FF = 16, 1536
CAPL, CAPC = 2 * LAT // E, 2 * CTX // E
CAP = CAPL + CAPC
FG = 4
FT = FF // P // FG
EPS = 1e-6
IN_COLS = 4 * MW + 4 * H + SW + 2 * D
C_Q, C_K, C_V, C_O, C_G = 0, MW, 2 * MW, 3 * MW, 4 * MW
C_U = C_G + 4 * H
C_GA = C_U + SW
C_GB = C_GA + D
NSLOT = 3

PC_C, PC_BADA, PC_NMIX, PC_NFFN, PC_NFIN, PC_HN, PC_BGLU, PC_BR = 0, 16, 64, 72, 80, 88, 96, 100
PC_N = 116


def bc(ap, shape):
    return ap.to_broadcast(shape)


class Chain:

    def __init__(self, eng, sem):
        self.eng, self.sem, self.n = eng, sem, 0

    def __call__(self, ins):
        self.n += 1
        ins.then_inc(self.sem, 1)
        self.eng.wait_ge(self.sem, self.n)


def program(nc, ar, out):
    with ExitStack() as ctx:
        def sb(name, shape, dt=F32, stack=None):
            return (stack or ctx).enter_context(nc.sbuf_tensor(name, shape, dt))

        sems = {}

        def sem(name):
            if name not in sems:
                sems[name] = ctx.enter_context(nc.semaphore(name))
            return sems[name]

        chains = {}

        def chain(eng, name):
            if name not in chains:
                chains[name] = Chain(eng, sem("order_" + name))
            chains[name].eng = eng
            return chains[name]

        PS = [ctx.enter_context(nc.psum_tensor(f"bank{i}", [P, 512], F32)) for i in range(8)]

        par = sb("par", [P, PC_N])
        consts = sb("consts", [P, 3, P])
        ident, mask_f, mask_b = consts[:, 0, :], consts[:, 1, :], consts[:, 2, :]
        meanw = sb("meanw", [P, P])
        modT = sb("modT", [P, 48, 2])
        gain = sb("gain", [P, 2, KD, 2])
        xT = sb("xT", [P, KD, TOK])
        rsb = sb("rsb", [P, TOK])
        sq = sb("sq", [P, 2, TOK])
        gpar = sb("gpar", [H, 6])
        hT = sb("hT", [P, KD, TOK])
        acts = ctx.enter_context(ExitStack())
        W = sb("W", [P, NSLOT, 4096], F32, acts)
        hbT = sb("hbT", [P, 4, TOK], F32, acts)
        colT = sb("colT", [P, NT, 6, H], F32, acts)
        negM = sb("negM", [H, 2, TOK], F32, acts)

        w_in = ar["w_in"][0].rearrange("(k p) n -> p k n", p=P)
        w_ada = ar["w_ada"][0].rearrange("(k p) n -> p k n", p=P)
        w_pA = ar["w_pA"][0].rearrange("(k p) n -> p k n", p=P)
        w_pB = ar["w_pB"][0].rearrange("(k p) n -> p k n", p=P)
        w_out = ar["w_out"][0].rearrange("(k p) n -> p k n", p=P)
        w_glu = ar["w_glu"][0].rearrange("(k p) n -> p k n", p=P)
        plan = []
        for c in range(12):
            plan.append(([(8, 0, w_ada[:, :, 512 * c:512 * c + 512])], "ada_done", c + 1))
        CH_U = len(plan)
        plan.append(([(8, 0, w_in[:, :, C_U:C_U + SW])], "u_done", L))
        CH_H = len(plan)
        for h in range(H):
            o = h * DH
            plan.append(([(8, 0, w_in[:, :, C_Q + o:C_Q + o + DH]), (8, DH, w_in[:, :, C_K + o:C_K + o + DH])],
                         "qk_done", 5 * (h + 1)))
            plan.append(([(8, 0, w_in[:, :, C_V + o:C_V + o + DH]), (8, DH, w_in[:, :, C_O + o:C_O + o + DH])],
                         "vo_done", NT * (h + 1)))
        CH_M = len(plan)
        for m in range(4):
            o = 256 * m
            plan.append(([(8, 0, w_in[:, :, C_GA + o:C_GA + o + 256]), (8, 256, w_in[:, :, C_GB + o:C_GB + o + 256])],
                         "merge_done", 4 * (2 * m + 1) + 2))
            plan.append(([(8, 0, w_pA[:, :, o:o + 256]), (4, 256, w_pB[:, :, o:o + 256])],
                         "merge_done", 4 * (2 * m + 1) + 4))
        CH_O = len(plan)
        for m in range(2):
            plan.append(([(8, 0, w_out[:, :, 512 * m:512 * m + 512])], "out_done", 4 * (m + 1)))
        landed, per_slot = [], [0] * NSLOT
        for c, (parts, _, _) in enumerate(plan):
            per_slot[c % NSLOT] += 16 * len(parts)
            landed.append(per_slot[c % NSLOT])
        issued = [0]

        def wslot(c, kt=8):
            return W[:, c % NSLOT, 0:kt * 512].rearrange("p (k n) -> p k n", k=kt)

        def load_weights(eng, upto):
            while issued[0] < min(upto, len(plan)):
                c = issued[0]
                if c >= NSLOT:
                    eng.wait_ge(sem(plan[c - NSLOT][1]), plan[c - NSLOT][2])
                for kt, at, src in plan[c][0]:
                    n = src.shape[2]
                    eng.dma_start(wslot(c, kt)[:, :, at:at + n], src).then_inc(sem(f"ring{c % NSLOT}"), 16)
                issued[0] += 1

        def have_weights(eng, c):
            eng.wait_ge(sem(f"ring{c % NSLOT}"), landed[c])

        def pe_mean_square(pe, n):
            for k in range(KD):
                pe.wait_ge(sem("squares"), 8 * n + k + 1)
                pe.matmul(PS[6][:, 0:LAT], meanw[:], sq[:, k % 2, 0:LAT], start=(k == 0), stop=(k == 7))
                pe.matmul(PS[7][:, 0:CTX], meanw[:], sq[:, k % 2, LAT:TOK], start=(k == 0),
                          stop=(k == 7)).then_inc(sem("squares_summed"), 1)

        def act_square(act, n, k):
            if k >= 2:
                act.wait_ge(sem("squares_summed"), 8 * n + k - 1)
            act.activation(sq[:, k % 2, :], xT[:, k, :], ACT.Square).then_inc(sem("squares"), 1)

        def dve_inverse_mean(dve, v, n, tmp):
            dve.wait_ge(sem("squares_summed"), 8 * n + 8)
            v(dve.tensor_scalar(tmp[:, 0:LAT], PS[6][:, 0:LAT], EPS, None, ALU.add))
            v(dve.tensor_scalar(tmp[:, LAT:TOK], PS[7][:, 0:CTX], EPS, None, ALU.add))
            dve.reciprocal(tmp[:], tmp[:]).then_inc(sem("inverse_mean"), 1)

        def act_rms(act, n, tmp):
            act.wait_ge(sem("inverse_mean"), n + 1)
            act.activation(rsb[:], tmp[:], ACT.Sqrt).then_inc(sem("rms"), 1)

        def dve_normalise(dve, n):
            dve.wait_ge(sem("rms"), n + 1)
            for k in range(KD):
                if k >= 2:
                    dve.wait_ge(sem("modulated"), 8 * n + k - 1)
                dve.tensor_tensor(sq[:, k % 2, :], xT[:, k, :], rsb[:], ALU.mult).then_inc(sem("normalised"), 1)

        def act_modulate(act, n, dst):
            for k in range(KD):
                act.wait_ge(sem("normalised"), 8 * n + k + 1)
                act.activation(dst[:, k, 0:LAT], sq[:, k % 2, 0:LAT], ACT.Identity,
                               scale=gain[:, n, k, 0:1], bias=modT[:, 24 * n + k, 0:1])
                act.activation(dst[:, k, LAT:TOK], sq[:, k % 2, LAT:TOK], ACT.Identity,
                               scale=gain[:, n, k, 1:2],
                               bias=modT[:, 24 * n + k, 1:2]).then_inc(sem("modulated"), 1)

        s5 = ctx.enter_context(ExitStack())
        s5p = sb("s5p", [P, 5, GN], F32, s5)
        s5bc = sb("s5bc", [P, 4, GN, GC], F32, s5)
        s5d = sb("s5d", [GC, GN], F32, s5)
        bb = sb("bb", [P, 2, GN, GC], F32, s5)
        pw = sb("pw", [P, 2, L + 1, GN], F32, s5)
        pwc = sb("pwc", [P, 2, L + 1, GN], F32, s5)
        pwd = sb("pwd", [P, 2, L, GN], F32, s5)
        ph = sb("ph", [P, 2, GN], F32, s5)
        rho = sb("rho", [P, GN], F32, s5)
        uC = sb("uC", [J, GN, L, GC], F32, s5)
        zC = sb("zC", [J, L, SW], F32, s5)

        with ExitStack() as st:
            cs = sb("cs", [P, KD, 2], F32, st)
            posT = sb("posT", [P, KD, LAT], F32, st)
            t5 = sb("t5", [P, 12, GN], F32, st)
            tmp = sb("tmp", [P, TOK], F32, st)
            tp = sb("tp", [P, 4, 4, GN], F32, st)
            tb = sb("tb", [P, 2, GN, GC], F32, st)
            zero = sb("zero", [P, D], F32, st)
            block = st.enter_context(nc.Block())

            @block.sync
            def _(sp):
                sp.dma_start(par[:], ar["par"]).then_inc(sem("par_in"), 16)
                sp.dma_start(s5p[:], ar["s5p"]).then_inc(sem("s5p_in"), 16)
                load_weights(sp, 2)
                sp.dma_start(xT[:], ar["xT"]).then_inc(sem("x_in"), 16)
                sp.dma_start(posT[:], ar["posT"]).then_inc(sem("x_in"), 16)
                sp.dma_start(s5bc[:], ar["s5bc"]).then_inc(sem("s5bc_in"), 16)
                sp.dma_start(consts[:], ar["consts"]).then_inc(sem("consts_in"), 16)
                sp.dma_start(s5d[:], ar["s5d"]).then_inc(sem("consts_in"), 16)
                sp.dma_start(gpar[:], ar["gpar"]).then_inc(sem("consts_in"), 16)
                load_weights(sp, CH_U + 1)
                sp.wait_ge(sem("consts_in"), 48)

            @block.gpsimd
            def _(pool):
                pool.memset(meanw[:], 1.0 / D).then_inc(sem("meanw_set"), 1)
                pool.memset(zero[:], 0.0).then_inc(sem("zero_set"), 1)
                pool.wait_ge(sem("zero_set"), 1)
                for t in range(NT):
                    pool.dma_start(ar["moe"][t * P:(t + 1) * P, :], zero[:]).then_inc(sem("moe_zero"), 16)
                pool.wait_ge(sem("moe_zero"), 16 * NT)

            @block.scalar
            def _(act):
                a = chain(act, "act")
                act.wait_ge(sem("par_in"), 16)
                act.activation(cs[:].rearrange("p k s -> p (k s)"), par[:, PC_C:PC_C + 16],
                               ACT.Silu).then_inc(sem("c_silu"), 1)
                act.wait_ge(sem("s5p_in"), 16)
                a(act.activation(t5[:, 0, :], s5p[:, 2, :], ACT.Exp))
                act.wait_ge(sem("s5_z"), 1)
                a(act.activation(t5[:, 3, :], t5[:, 1, :], ACT.Exp))
                act.activation(rho[:], t5[:, 1, :], ACT.Exp, scale=float(L)).then_inc(sem("s5_mag"), 1)
                act.wait_ge(sem("s5_angle"), 1)
                a(act.activation(t5[:, 4, :], t5[:, 2, :], ACT.Sin))
                act.activation(t5[:, 5, :], t5[:, 2, :], ACT.Sin, scale=0.5).then_inc(sem("s5_sin"), 1)
                act.wait_ge(sem("x_pos"), 1)
                for k in range(KD):
                    act_square(act, 0, k)
                act_rms(act, 0, tmp)
                act.wait_ge(sem("mod_ready"), 1)
                act_modulate(act, 0, hT)

            @block.tensor
            def _(pe):
                pe.wait_ge(sem("c_silu"), 1)
                for c in range(12):
                    have_weights(pe, c)
                    for n in range(4):
                        for k in range(KD):
                            mm = pe.matmul(PS[0][:, 2 * (4 * c + n):2 * (4 * c + n) + 2],
                                           wslot(c)[:, k, n * P:(n + 1) * P], cs[:, k, :],
                                           start=(k == 0), stop=(k == 7))
                    mm.then_inc(sem("ada_done"), 1)
                pe.wait_ge(sem("meanw_set"), 1)
                pe_mean_square(pe, 0)

            @block.vector
            def _(dve):
                v = chain(dve, "dve")
                dve.wait_ge(sem("s5p_in"), 16)
                dve.wait_ge(sem("order_act"), 1)
                are, aim = s5p[:, 0, :], s5p[:, 1, :]
                v(dve.tensor_tensor(t5[:, 6, :], aim, t5[:, 0, :], ALU.mult))
                dve.tensor_tensor(t5[:, 1, :], are, t5[:, 0, :], ALU.mult).then_inc(sem("s5_z"), 1)
                MAGIC = 1.5 * 2.0 ** 23
                v(dve.tensor_scalar(t5[:, 7, :], t5[:, 6, :], float(1 / (2 * np.pi)), MAGIC, ALU.mult, ALU.add))
                v(dve.tensor_scalar(t5[:, 7, :], t5[:, 7, :], MAGIC, None, ALU.subtract))
                c1 = 6.28125
                c2 = float(np.float32(2 * np.pi - c1))
                c3 = float(np.float32(2 * np.pi - c1 - float(c2)))
                for cc in (c1, c2, c3):
                    v(dve.scalar_tensor_tensor(t5[:, 6, :], t5[:, 7, :], -cc, t5[:, 6, :], ALU.mult, ALU.add))
                dve.tensor_scalar(t5[:, 2, :], t5[:, 6, :], 3.1415925, -3.1415925, ALU.min,
                                  ALU.max).then_inc(sem("s5_angle"), 1)
                dve.wait_ge(sem("s5_mag"), 1)
                dve.wait_ge(sem("s5_sin"), 1)
                v(dve.tensor_tensor(t5[:, 7, :], t5[:, 5, :], t5[:, 5, :], ALU.mult))
                v(dve.tensor_scalar(ph[:, 0, :], t5[:, 7, :], -2.0, 1.0, ALU.mult, ALU.add))
                v(dve.tensor_copy(ph[:, 1, :], t5[:, 4, :]))
                v(dve.tensor_tensor(pw[:, 0, 1, :], t5[:, 3, :], ph[:, 0, :], ALU.mult))
                v(dve.tensor_tensor(pw[:, 1, 1, :], t5[:, 3, :], ph[:, 1, :], ALU.mult))
                v(dve.memset(pw[:, 0, 0, :], 1.0))
                v(dve.memset(pw[:, 1, 0, :], 0.0))

                def cmul(dr, di, ar_, ai_, br_, bi_, t):
                    dve.tensor_tensor(t[0], ar_, br_, ALU.mult)
                    dve.tensor_tensor(t[1], ai_, bi_, ALU.mult)
                    dve.tensor_tensor(t[2], ar_, bi_, ALU.mult)
                    v(dve.tensor_tensor(t[3], ai_, br_, ALU.mult))
                    dve.tensor_tensor(dr, t[0], t[1], ALU.subtract)
                    v(dve.tensor_tensor(di, t[2], t[3], ALU.add))

                def t4(n):
                    return [tp[:, x, 0:n, :] for x in range(4)]

                for _ in range(3):
                    cmul(ph[:, 0, :], ph[:, 1, :], ph[:, 0, :], ph[:, 1, :], ph[:, 0, :], ph[:, 1, :],
                         [tp[:, x, 0, :] for x in range(4)])
                for m in (1, 2, 4):
                    cmul(pw[:, 0, m + 1:2 * m + 1, :], pw[:, 1, m + 1:2 * m + 1, :],
                         pw[:, 0, 1:m + 1, :], pw[:, 1, 1:m + 1, :],
                         bc(pw[:, 0, m:m + 1, :], [P, m, GN]), bc(pw[:, 1, m:m + 1, :], [P, m, GN]), t4(m))
                F, B = slice(0, SP_), slice(SP_, P)
                for r in range(2):
                    v(dve.tensor_copy(pwc[F, r, :, :], pw[F, r, :, :]))
                    v(dve.tensor_copy(pwc[B, r, :, :], pw[B, r, ::-1, :]))
                    v(dve.tensor_copy(pwd[F, r, :, :], pw[F, r, L - 1::-1, :]))
                    v(dve.tensor_copy(pwd[B, r, :, :], pw[B, r, 0:L, :]))
                v(dve.tensor_tensor(t5[:, 8, :], are, are, ALU.mult))
                v(dve.tensor_tensor(t5[:, 9, :], aim, aim, ALU.mult))
                v(dve.tensor_tensor(t5[:, 8, :], t5[:, 8, :], t5[:, 9, :], ALU.add))
                v(dve.reciprocal(t5[:, 8, :], t5[:, 8, :]))
                v(dve.tensor_tensor(t5[:, 9, :], are, t5[:, 8, :], ALU.mult))
                v(dve.scalar_tensor_tensor(t5[:, 10, :], aim, -1.0, t5[:, 8, :], ALU.mult, ALU.mult))
                v(dve.tensor_scalar(t5[:, 11, :], pw[:, 0, 1, :], 1.0, None, ALU.subtract))
                cmul(t5[:, 7, :], t5[:, 8, :], t5[:, 11, :], pw[:, 1, 1, :], t5[:, 9, :], t5[:, 10, :],
                     [tp[:, x, 0, :] for x in range(4)])
                dve.wait_ge(sem("s5bc_in"), 16)
                wr = bc(t5[:, 7, :].unsqueeze(2), [P, GN, GC])
                wi = bc(t5[:, 8, :].unsqueeze(2), [P, GN, GC])
                v(dve.tensor_tensor(tb[:, 0], s5bc[:, 0], wr, ALU.mult))
                v(dve.tensor_tensor(tb[:, 1], s5bc[:, 1], wi, ALU.mult))
                v(dve.tensor_tensor(bb[:, 0], tb[:, 0], tb[:, 1], ALU.subtract))
                v(dve.tensor_tensor(tb[:, 0], s5bc[:, 0], wi, ALU.mult))
                v(dve.tensor_tensor(tb[:, 1], s5bc[:, 1], wr, ALU.mult))
                v(dve.tensor_tensor(bb[:, 1], tb[:, 0], tb[:, 1], ALU.add))
                dve.wait_ge(sem("x_in"), 32)
                dve.tensor_tensor(xT[:, :, 0:LAT], xT[:, :, 0:LAT], posT[:], ALU.add).then_inc(sem("x_pos"), 1)
                dve_inverse_mean(dve, v, 0, tmp)
                dve.wait_ge(sem("ada_done"), 12)
                v(dve.tensor_tensor(modT[:], PS[0][:, 0:96].rearrange("p (n s) -> p n s", s=2),
                                    bc(par[:, PC_BADA:PC_BADA + 48].unsqueeze(2), [P, 48, 2]), ALU.add))
                for n, pc in ((0, PC_NMIX), (1, PC_NFFN)):
                    ins = dve.scalar_tensor_tensor(gain[:, n], modT[:, 24 * n + 8:24 * n + 16, :], 1.0,
                                                   bc(par[:, pc:pc + 8].unsqueeze(2), [P, KD, 2]),
                                                   ALU.add, ALU.mult)
                    if n == 0:
                        v(ins)
                    else:
                        ins.then_inc(sem("mod_ready"), 1)
                dve_normalise(dve, 0)

        with ExitStack() as st:
            wg = sb("wg", [P, KD, 16], F32, st)
            gtok = sb("gtok", [P, NT, 16], F32, st)
            G = W[0:H, 2, 0:4 * TOK].rearrange("h (g t) -> h g t", g=4)
            gt = W[0:H, 2, 4 * TOK:6 * TOK].rearrange("h (g t) -> h g t", g=2)
            hb2 = hbT[:].rearrange("p a b -> p (a b)")
            lf = hb2[0:H, 0:2 * TOK].rearrange("h (g t) -> h g t", g=2)
            cum = hb2[0:H, 2 * TOK:4 * TOK].rearrange("h (g t) -> h g t", g=2)
            R = zC[:].rearrange("p a b -> p (a b)")[0:H, 0:6 * TOK].rearrange("h (x t) -> h x t", x=6)
            Mx = sb("Mx", [H, 2, TOK], F32, st)
            ones4 = sb("ones4", [H, TOK], F32, st)
            mrow = sb("mrow", [H, 2], F32, st)
            block = st.enter_context(nc.Block())

            @block.sync
            def _(sp):
                sp.dma_start(wg[:], w_in[:, :, C_G:C_G + 16]).then_inc(sem("wg_in"), 16)
                load_weights(sp, CH_H + 1)
                sp.wait_ge(sem("m_ready"), 1)
                with nc.allow_non_contiguous_dma(reason="eight values"):
                    sp.dma_start(out["m"].rearrange("d h -> h d"), mrow[:]).then_inc(sem("m_out"), 16)
                sp.wait_ge(sem("m_out"), 16)

            @block.tensor
            def _(pe):
                pe.wait_ge(sem("wg_in"), 16)
                for t in range(NT):
                    for k in range(KD):
                        mm = pe.matmul(PS[0][:, 16 * t:16 * t + 16], hT[:, k, t * P:(t + 1) * P], wg[:, k, :],
                                       start=(k == 0), stop=(k == 7))
                mm.then_inc(sem("gates_done"), 1)
                have_weights(pe, CH_U)
                for i in range(L):
                    if i >= 2:
                        pe.wait_ge(sem("u_copied"), i - 1)
                    for k in range(KD):
                        mm = pe.matmul(PS[1 + i % 2][0:J, :], hT[:, k, i:TOK:L], wslot(CH_U)[:, k, :],
                                       start=(k == 0), stop=(k == 7))
                    mm.then_inc(sem("u_done"), 1)
                    if i == 1:
                        pe.wait_ge(sem("gates_copied"), 1)
                        for g in range(4):
                            for t in range(NT):
                                dst = PS[3 + g][0:H, t * P:(t + 1) * P] if t < 4 else PS[7][0:H, g * P:(g + 1) * P]
                                mm = pe.transpose(dst, gtok[:, t, 4 * g:4 * g + 4], ident)
                        mm.then_inc(sem("gates_turned"), 1)
                pe.wait_ge(sem("rows_ready"), 1)
                for t in range(NT):
                    for x in range(6):
                        if t < 4 or x not in (2, 3):
                            c = (t * 6 + x) * H
                            mm = pe.transpose(PS[0][:, c:c + H], R[:, x, t * P:(t + 1) * P], ident[0:H, 0:H])
                mm.then_inc(sem("rows_turned"), 1)

            @block.scalar
            def _(act):
                a = chain(act, "act")
                for i in range(L):
                    act.wait_ge(sem("u_done"), i + 1)
                    act.activation(uC[:, :, i, :], PS[1 + i % 2][0:J, :].rearrange("p (g c) -> p g c", c=GC),
                                   ACT.Copy).then_inc(sem("u_copied"), 1)
                act.wait_ge(sem("gate_abs"), 1)
                a(act.activation(gt, gt, ACT.Exp, scale=-1.0))
                act.activation(gt, gt, ACT.Ln, bias=1.0).then_inc(sem("gate_ln"), 1)
                act.wait_ge(sem("m_ready"), 1)
                for d in range(2):
                    act.activation(R[:, 2 + d, 0:LAT], Mx[:, d, 0:LAT], ACT.Exp, scale=-1.0, bias=gpar[:, 4 + d:5 + d])
                    ins = act.activation(R[:, 4 + d, :], cum[:, d, :], ACT.Exp, scale=-1.0)
                ins.then_inc(sem("rows_ready"), 1)

            @block.vector
            def _(dve):
                v = chain(dve, "dve")
                dve.wait_ge(sem("gates_done"), 1)
                dve.tensor_copy(gtok[:].rearrange("p t g -> p (t g)"), PS[0][:, 0:80]).then_inc(sem("gates_copied"), 1)
                v(dve.memset(ones4[:], 1.0))
                dve.wait_ge(sem("gates_turned"), 1)
                for g in range(4):
                    dve.tensor_scalar(G[:, g, 0:LAT], PS[3 + g][0:H, :], gpar[:, g:g + 1], None, ALU.add)
                    v(dve.tensor_scalar(G[:, g, LAT:TOK], PS[7][0:H, g * P:(g + 1) * P], gpar[:, g:g + 1], None,
                                        ALU.add))
                x = G[:, 1:4:2, :]
                dve.scalar_tensor_tensor(gt, x, -1.0, x, ALU.mult, ALU.max).then_inc(sem("gate_abs"), 1)
                dve.wait_ge(sem("gate_ln"), 1)
                v(dve.scalar_tensor_tensor(lf, x, 0.0, gt, ALU.min, ALU.subtract))

                def part(tile, d, s):
                    ap = tile[:, d, 0:LAT] if s == 0 else tile[:, d, LAT:TOK]
                    return ap[:, ::-1] if d else ap

                for d in range(2):
                    for s in range(2):
                        n = LAT if s == 0 else CTX
                        v(dve.tensor_tensor_scan(part(cum, d, s), ones4[:, 0:n], part(lf, d, s), 0.0,
                                                 ALU.mult, ALU.add))
                v(dve.tensor_tensor(R[:, 0:2, :], G[:, 0:4:2, :], cum, ALU.subtract))
                for d in range(2):
                    for s in range(2):
                        v(dve.tensor_tensor_scan(part(Mx, d, s), part(R, d, s), part(R, d, s),
                                                 gpar[:, 4 + d:5 + d] if s == 0 else 0.0, ALU.max, ALU.max))
                v(dve.tensor_scalar(negM[:], Mx[:], -1.0, None, ALU.mult))
                v(dve.tensor_tensor(cum, cum, Mx[:], ALU.add))
                v(dve.tensor_copy(mrow[:, 0:1], cum[:, 0, TOK - 1:TOK]))
                dve.tensor_copy(mrow[:, 1:2], cum[:, 1, LAT:LAT + 1]).then_inc(sem("m_ready"), 1)
                dve.wait_ge(sem("rows_turned"), 1)
                c4 = PS[0][:, 0:NT * 24].rearrange("p (t x h) -> p t x h", t=NT, x=6)
                dve.tensor_copy(colT[:, 0:4], c4[:, 0:4])
                dve.tensor_copy(colT[:, 4, 0:2], c4[:, 4, 0:2])
                dve.tensor_copy(colT[:, 4, 4:6], c4[:, 4, 4:6])

        with ExitStack() as st:
            half0, half1 = W[:, 0, 0:2048], W[:, 0, 2048:4096]
            CB = half0.rearrange("p (r g x) -> p r g x", r=2, g=QG)
            CT = half1.rearrange("p (r g x) -> p r g x", r=2, g=QG)
            n3 = 2 * QG * NS_
            Et, V, Z = (W[:, 2, x * n3:(x + 1) * n3].rearrange("p (r g n) -> p r g n", r=2, g=QG) for x in range(3))
            t8 = hbT[:].rearrange("p a b -> p (a b)")[:, 0:2 * QG * (L + 1) * GC].rearrange("p (x g m) -> p x g m", x=2, g=QG)
            Xp = sq[:].rearrange("p a b -> p (a b)").rearrange("p (r g j) -> p r g j", r=2, g=QG)
            CA = sb("CA", [P, 2, QG, L + 1, GC], F32, st)
            bbz = sb("bbz", [P, 2, 2, QG, GC], F32, st)
            U = sb("U", [P, QG, J], F32, st)
            Kt = sb("Kt", [GC, QG, (2 * L - 1) * GC], F32, st)
            kd = sb("kd", [GC, QG, GC], F32, st)
            T = sb("T", [P, QG, P], F32, st)
            rt = sb("rt", [P, QG, NS_], F32, st)
            tz = sb("tz", [P, 4, QG, NS_], F32, st)
            xfin = sb("xfin", [P, 2, GN], F32, st)
            CAo = CB
            block = st.enter_context(nc.Block())

            @block.sync
            def _(sp):
                for q in range(NQ):
                    sp.wait_ge(sem("lags_ready"), q + 1)
                    if q:
                        sp.wait_ge(sem("s5_y_done"), 2 * q)
                    for i in range(L):
                        sp.dma_start(T[GC * i:GC * i + GC, :, :],
                                     Kt[:, :, (L - 1 - i) * GC:(2 * L - 1 - i) * GC]).then_inc(sem("toeplitz_in"), 16)
                sp.wait_ge(sem("xfin_ready"), NQ)
                for r in range(2):
                    sp.dma_start(out["s5"][r], xfin[:, r, :]).then_inc(sem("s5_out"), 16)
                sp.wait_ge(sem("s5_out"), 32)

            @block.gpsimd
            def _(pool):
                p = chain(pool, "pool")
                for q in range(NQ):
                    g = slice(QG * q, QG * q + QG)
                    s = [P, QG, L, GC]
                    if q:
                        pool.wait_ge(sem("cb_turned"), 4 * q)
                        pool.wait_ge(sem("s5_lag_done"), 4 * q)
                        pool.wait_ge(sem("s5_y_done"), 2 * q)
                    pr, pi = (bc(pwd[:, r, :, g].rearrange("p i g -> p g i").unsqueeze(3), s) for r in range(2))
                    br, bi = (bc(bb[:, r, g, :].unsqueeze(2), s) for r in range(2))
                    ta, tb_ = (t8[:, x, :, 0:P].rearrange("p g (i c) -> p g i c", c=GC) for x in range(2))
                    cr, ci = (CB[:, r].rearrange("p g (i c) -> p g i c", c=GC) for r in range(2))
                    pool.tensor_tensor(ta, pr, br, ALU.mult)
                    p(pool.tensor_tensor(tb_, pi, bi, ALU.mult))
                    p(pool.tensor_tensor(cr, ta, tb_, ALU.subtract))
                    pool.tensor_tensor(ta, pr, bi, ALU.mult)
                    p(pool.tensor_tensor(tb_, pi, br, ALU.mult))
                    pool.tensor_tensor(ci, ta, tb_, ALU.add).then_inc(sem("cb_ready"), 1)
                    pool.wait_ge(sem("cb_ready"), q + 1)
                    s = [P, QG, L + 1, GC]
                    pr, pi = (bc(pwc[:, r, :, g].rearrange("p i g -> p g i").unsqueeze(3), s) for r in range(2))
                    br, bi = (bc(s5bc[:, 2 + r, g, :].unsqueeze(2), s) for r in range(2))
                    ta, tb_ = (t8[:, x].rearrange("p g (i c) -> p g i c", c=GC) for x in range(2))
                    pool.tensor_tensor(ta, pr, br, ALU.mult)
                    p(pool.tensor_tensor(tb_, pi, bi, ALU.mult))
                    p(pool.tensor_tensor(CA[:, 0], ta, tb_, ALU.subtract))
                    pool.tensor_tensor(ta, pr, bi, ALU.mult)
                    p(pool.tensor_tensor(tb_, pi, br, ALU.mult))
                    p(pool.tensor_tensor(CA[:, 1], ta, tb_, ALU.add))
                    pool.tensor_scalar(CA[:, 1], CA[:, 1], -1.0, 1.0, ALU.mult, ALU.mult).then_inc(sem("ca_ready"), 1)
                    pool.wait_ge(sem("ca_ready"), q + 1)

            @block.tensor
            def _(pe):
                for q in range(NQ):
                    if q:
                        pe.wait_ge(sem("z_copied"), 2 * q)
                        pe.wait_ge(sem("lags_copied"), 4 * q)
                    for g in range(QG):
                        mm = pe.transpose(PS[g // 4][:, (g % 4) * J:(g % 4 + 1) * J], uC[:, QG * q + g, :, :],
                                          ident[0:J, 0:J])
                        if g % 4 == 3:
                            mm.then_inc(sem("u_turned"), 1)
                    pe.wait_ge(sem("cb_ready"), q + 1)
                    for r in range(2):
                        for g in range(QG):
                            mm = pe.transpose(PS[2 + 2 * r + g // 4][:, (g % 4) * P:(g % 4 + 1) * P], CB[:, r, g, :],
                                              ident)
                            if g % 4 == 3:
                                mm.then_inc(sem("cb_turned"), 1)
                    pe.wait_ge(sem("u_sliced"), 2 * q + 2)
                    for r in range(2):
                        for g in range(QG):
                            if g % 4 == 0:
                                pe.wait_ge(sem("ct_copied"), 4 * q + 2 * r + g // 4 + 1)
                            mm = pe.matmul(PS[2 + 2 * r + g // 4][:, (g % 4) * J:(g % 4 + 1) * J], CT[:, r, g, :],
                                           U[:, g, :], start=True, stop=True)
                            if g % 4 == 3:
                                mm.then_inc(sem("s5_v_done"), 1)
                    pe.wait_ge(sem("ca_ready"), q + 1)
                    pe.wait_ge(sem("bbz_ready"), q + 1)
                    FW, BW = (L - 1) * GC, 0
                    for g in range(QG):
                        bank = (6, 7, 0, 1)[g // 2]
                        o = (g % 2) * (2 * L - 1) * GC
                        k = 0
                        for d, (at, m0) in enumerate(((FW, 0), (BW, 1))):
                            for r in range(2):
                                mm = pe.matmul(PS[bank][0:GC, o + at:o + at + P], bbz[:, d, r, g, :],
                                               CA[:, r, g, m0:m0 + L, :], start=(k == 0 and g % 2 == 0), stop=(k == 3),
                                               skip_group_check=True)
                                k += 1
                        if g % 2 == 1:
                            mm.then_inc(sem("s5_lag_done"), 1)
                    pe.wait_ge(sem("xp_copied"), q + 1)
                    pe.wait_ge(sem("cao_ready"), q + 1)
                    pe.wait_ge(sem("toeplitz_in"), 128 * (q + 1))
                    pe.wait_ge(sem("v_copied"), 4 * q + 4)
                    for g in range(QG):
                        dst = PS[2 + g // 4][0:J, (g % 4) * P:(g % 4 + 1) * P]
                        pe.matmul(dst, U[:, g, :], T[:, g, :], start=True, stop=False)
                        for r in range(2):
                            mm = pe.matmul(dst, Xp[:, r, g, :], CAo[:, r, g, :], start=False, stop=(r == 1))
                        if g % 4 == 3:
                            mm.then_inc(sem("s5_y_done"), 1)

            @block.scalar
            def _(act):
                a = chain(act, "act")
                for q in range(NQ):
                    for b in range(2):
                        act.wait_ge(sem("u_turned"), 2 * q + b + 1)
                        act.activation(U[:, 4 * b:4 * b + 4, :].rearrange("p g j -> p (g j)"), PS[b][:, 0:4 * J],
                                       ACT.Copy).then_inc(sem("u_sliced"), 1)
                    for b in range(4):
                        act.wait_ge(sem("cb_turned"), 4 * q + b + 1)
                        act.activation(CT[:, b // 2, 4 * (b % 2):4 * (b % 2) + 4, :].rearrange("p g j -> p (g j)"),
                                       PS[2 + b][:], ACT.Copy).then_inc(sem("ct_copied"), 1)
                    act.wait_ge(sem("ca_ready"), q + 1)
                    act.wait_ge(sem("cb_turned"), 4 * q + 4)
                    for r in range(2):
                        dst = CB[:, r].rearrange("p g (i c) -> p g i c", c=GC)
                        act.activation(dst[0:SP_], CA[0:SP_, r, :, 1:L + 1, :], ACT.Copy)
                        ins = act.activation(dst[SP_:P], CA[SP_:P, r, :, 0:L, :], ACT.Copy)
                    ins.then_inc(sem("cao_ready"), 1)
                    for b in range(4):
                        act.wait_ge(sem("s5_lag_done"), 4 * q + b + 1)
                        act.activation(Kt[:, 2 * b:2 * b + 2, :].rearrange("p g x -> p (g x)"),
                                       PS[(6, 7, 0, 1)[b]][0:GC, 0:2 * (2 * L - 1) * GC],
                                       ACT.Copy).then_inc(sem("lags_copied"), 1)
                    for b in range(2):
                        act.wait_ge(sem("s5_y_done"), 2 * q + b + 1)
                        c0 = (QG * q + 4 * b) * GC
                        act.activation(zC[:, :, c0:c0 + 4 * GC].rearrange("p i (g c) -> p g i c", c=GC),
                                       PS[2 + b][0:J, :].rearrange("p (g i c) -> p g i c", g=4, i=L),
                                       ACT.Copy).then_inc(sem("z_copied"), 1)

            @block.vector
            def _(dve):
                v = chain(dve, "dve")
                F, B = slice(0, SP_), slice(SP_, P)
                lat, cx = slice(0, JL + 1), slice(JL + 1, NS_)
                for q in range(NQ):
                    g = slice(QG * q, QG * q + QG)
                    if q:
                        dve.wait_ge(sem("s5_lag_done"), 4 * q)
                    for d, (own, other) in enumerate(((F, B), (B, F))):
                        for r in range(2):
                            dve.tensor_copy(bbz[own, d, r], bb[own, r, g, :])
                            ins = dve.memset(bbz[other, d, r], 0.0)
                    ins.then_inc(sem("bbz_ready"), 1)
                    v(dve.memset(Et[:, 0, :, 0:1], 1.0))
                    v(dve.memset(Et[:, 1, :, 0:1], 0.0))
                    for r in range(2):
                        v(dve.tensor_copy(Et[:, r, :, 1:2], ph[:, r, g].unsqueeze(2)))
                    m = 1
                    while m < JL:
                        x, y = slice(1, m + 1), slice(m + 1, 2 * m + 1)
                        er, ei = (bc(Et[:, r, :, m:m + 1], [P, QG, m]) for r in range(2))
                        dve.tensor_tensor(tz[:, 0, :, 0:m], Et[:, 0, :, x], er, ALU.mult)
                        dve.tensor_tensor(tz[:, 1, :, 0:m], Et[:, 1, :, x], ei, ALU.mult)
                        dve.tensor_tensor(tz[:, 2, :, 0:m], Et[:, 0, :, x], ei, ALU.mult)
                        v(dve.tensor_tensor(tz[:, 3, :, 0:m], Et[:, 1, :, x], er, ALU.mult))
                        dve.tensor_tensor(Et[:, 0, :, y], tz[:, 0, :, 0:m], tz[:, 1, :, 0:m], ALU.subtract)
                        v(dve.tensor_tensor(Et[:, 1, :, y], tz[:, 2, :, 0:m], tz[:, 3, :, 0:m], ALU.add))
                        m *= 2
                    v(dve.tensor_copy(Et[:, :, :, cx], Et[:, :, :, 0:JC + 1]))
                    v(dve.tensor_copy(rt[:], bc(rho[:, g].unsqueeze(2), [P, QG, NS_])))
                    v(dve.memset(rt[:, :, 0:1], 0.0))
                    v(dve.memset(rt[:, :, JL + 1:JL + 2], 0.0))
                    for r in range(2):
                        v(dve.tensor_copy(V[:, r, :, 0:1], s5p[:, 3 + r, g].unsqueeze(2)))
                        v(dve.memset(V[:, r, :, JL + 1:JL + 2], 0.0))
                        for b in range(2):
                            dve.wait_ge(sem("s5_v_done"), 4 * q + 2 * r + b + 1)
                            src = PS[2 + 2 * r + b][:, 0:4 * J].rearrange("p (g j) -> p g j", g=4)
                            gg = slice(4 * b, 4 * b + 4)
                            dve.tensor_copy(V[F, r, gg, 1:JL + 1], src[F, :, 0:JL])
                            dve.tensor_copy(V[F, r, gg, JL + 2:NS_], src[F, :, JL:J])
                            dve.tensor_copy(V[B, r, gg, 1:JL + 1], src[B, :, 0:JL][:, :, ::-1])
                            dve.tensor_copy(V[B, r, gg, JL + 2:NS_],
                                            src[B, :, JL:J][:, :, ::-1]).then_inc(sem("v_copied"), 1)
                            dve.wait_ge(sem("v_copied"), 4 * q + 2 * r + b + 1)
                    dve.tensor_tensor(tz[:, 0], V[:, 0], Et[:, 0], ALU.mult)
                    dve.tensor_tensor(tz[:, 1], V[:, 1], Et[:, 1], ALU.mult)
                    dve.tensor_tensor(tz[:, 2], V[:, 1], Et[:, 0], ALU.mult)
                    v(dve.tensor_tensor(tz[:, 3], V[:, 0], Et[:, 1], ALU.mult))
                    dve.tensor_tensor(V[:, 0], tz[:, 0], tz[:, 1], ALU.add)
                    v(dve.tensor_tensor(V[:, 1], tz[:, 2], tz[:, 3], ALU.subtract))
                    for r in range(2):
                        v(dve.tensor_tensor_scan(Z[:, r].rearrange("p g n -> p (g n)"),
                                                 rt[:].rearrange("p g n -> p (g n)"),
                                                 V[:, r].rearrange("p g n -> p (g n)"), 0.0, ALU.mult, ALU.add))
                    dve.tensor_tensor(tz[:, 0], Z[:, 0], Et[:, 0], ALU.mult)
                    dve.tensor_tensor(tz[:, 1], Z[:, 1], Et[:, 1], ALU.mult)
                    dve.tensor_tensor(tz[:, 2], Z[:, 1], Et[:, 0], ALU.mult)
                    v(dve.tensor_tensor(tz[:, 3], Z[:, 0], Et[:, 1], ALU.mult))
                    dve.tensor_tensor(V[:, 0], tz[:, 0], tz[:, 1], ALU.subtract)
                    v(dve.tensor_tensor(V[:, 1], tz[:, 2], tz[:, 3], ALU.add))
                    dve.tensor_copy(xfin[:, :, g], V[:, :, :, NS_ - 1]).then_inc(sem("xfin_ready"), 1)
                    if q:
                        dve.wait_ge(sem("s5_y_done"), 2 * q)
                    for r in range(2):
                        dve.tensor_copy(Xp[F, r, :, 0:JL], V[F, r, :, 0:JL])
                        dve.tensor_copy(Xp[F, r, :, JL:J], V[F, r, :, JL + 1:NS_ - 1])
                        dve.tensor_copy(Xp[B, r, :, 0:JL], V[B, r, :, 0:JL][:, :, ::-1])
                        ins = dve.tensor_copy(Xp[B, r, :, JL:J], V[B, r, :, JL + 1:NS_ - 1][:, :, ::-1])
                    ins.then_inc(sem("xp_copied"), 1)
                    v(dve.tensor_tensor(kd[:], bc(s5d[:, g].unsqueeze(2), [GC, QG, GC]),
                                        bc(ident[0:GC, 0:GC].unsqueeze(1), [GC, QG, GC]), ALU.mult))
                    dve.wait_ge(sem("lags_copied"), 4 * q + 4)
                    k0 = Kt[:, :, (L - 1) * GC:L * GC]
                    dve.tensor_tensor(k0, k0, kd[:], ALU.add).then_inc(sem("lags_ready"), 1)


        with ExitStack() as st:
            zT = sb("zT", [P, 4, TOK], F32, st)
            gz = sb("gz", [P, 4, TOK], F32, st)
            sg = sb("sg", [P, 2, TOK], F32, st)
            wgl = sb("wgl", [P, 4, SW], F32, st)
            block = st.enter_context(nc.Block())

            @block.sync
            def _(sp):
                sp.dma_start(wgl[:], w_glu).then_inc(sem("wglu_in"), 16)
                load_weights(sp, CH_H + NSLOT)

            @block.tensor
            def _(pe):
                for b in range(8):
                    if b >= 4:
                        pe.wait_ge(sem("z_in"), b - 3)
                    for i in range(4):
                        mm = pe.transpose(PS[b % 4][:, i * J:(i + 1) * J],
                                          zC[:, 4 * (b % 2) + i, (b // 2) * P:(b // 2 + 1) * P], ident[0:J, 0:J])
                    mm.then_inc(sem("z_turned"), 1)
                pe.wait_ge(sem("wglu_in"), 16)
                pe.wait_ge(sem("z_in"), 8)
                for m in range(4):
                    if m >= 2:
                        pe.wait_ge(sem("glu_sig"), m - 1)
                    for k in range(4):
                        w = wgl[:, k, m * P:(m + 1) * P]
                        pe.matmul(PS[4 + m % 2][:, :], w, zT[:, k, 0:LAT], start=(k == 0), stop=(k == 3))
                        mm = pe.matmul(PS[6 + m % 2][:, 0:CTX], w, zT[:, k, LAT:TOK], start=(k == 0), stop=(k == 3))
                    mm.then_inc(sem("glu_done"), 1)

            @block.scalar
            def _(act):
                act.wait_ge(sem("z_in"), 8)
                for m in range(4):
                    act.activation(gz[:, m, :], zT[:, m, :], ACT.Gelu_apprx_tanh).then_inc(sem("gelu"), 1)
                for m in range(4):
                    act.wait_ge(sem("glu_done"), m + 1)
                    if m >= 2:
                        act.wait_ge(sem("hb_ready"), m - 1)
                    b = par[:, PC_BGLU + m:PC_BGLU + m + 1]
                    act.activation(sg[:, m % 2, 0:LAT], PS[4 + m % 2][:, :], ACT.Sigmoid, bias=b)
                    act.activation(sg[:, m % 2, LAT:TOK], PS[6 + m % 2][:, 0:CTX], ACT.Sigmoid,
                                   bias=b).then_inc(sem("glu_sig"), 1)

            @block.vector
            def _(dve):
                for b in range(8):
                    dve.wait_ge(sem("z_turned"), b + 1)
                    dst = zT[:, b // 2, :].rearrange("p (j i) -> p i j", i=L)[:, 4 * (b % 2):4 * (b % 2) + 4, :]
                    dve.tensor_copy(dst, PS[b % 4][:, 0:4 * J].rearrange("p (i j) -> p i j", i=4)
                                    ).then_inc(sem("z_in"), 1)
                dve.wait_ge(sem("gelu"), 4)
                for m in range(4):
                    dve.wait_ge(sem("glu_sig"), m + 1)
                    dve.tensor_tensor(hbT[:, m, :], gz[:, m, :], sg[:, m % 2, :], ALU.mult).then_inc(sem("hb_ready"), 1)

        s5.close()

        haT = sb("haT", [P, KD, TOK], F32, acts)
        with ExitStack() as st:
            qk = sb("qk", [P, 2, 4, TOK], F32, st)
            vt = sb("vt", [P, 2, NT, DH + 1], F32, st)
            og = sb("og", [P, 2, NT, DH], F32, st)
            PW = LAT * 5 // 2 + CTX
            Pm = sb("Pm", [P, 2, PW], F32, st)
            negMd = sq
            Qs = rsb[:, 0:2 * (DH + 1)].rearrange("p (b n) -> p b n", b=2)
            nd = sb("nd", [P, 2, DH + 1], F32, st)
            rr = sb("rr", [P, 2], F32, st)
            hacc = sb("hacc", [P, NT, DH], F32, st)
            junk = sb("junk", [P, DH], F32, st)
            ssq = sb("ssq", [P, NT], F32, st)
            rs5 = sb("rs5", [P, NT], F32, st)
            C0 = sb("C0", [P, 4, DH + 1], F32, st)
            wk = sb("wk", [P, 2], F32, st)
            kw = sb("kw", [P, 2, DH], F32, st)
            Co = sb("Co", [P, 4, DH + 1], F32, st)
            selH = sb("selH", [H, H, P], F32, st)
            block = st.enter_context(nc.Block())
            Cn = ar["Cn"].rearrange("d h (k p) n -> h d p k n", p=P)
            Cout = out["Cn"].rearrange("d h (k p) n -> h d p k n", p=P)
            OFF = {0: [0, 512, 896, 1152], 1: [0, 128, 384, 768]}

            @block.sync
            def _(sp):
                for h in range(H):
                    if h:
                        sp.wait_ge(sem("pv_done"), 10 * h)
                    for d in range(2):
                        sp.dma_start(C0[:, 2 * d:2 * d + 2, :], Cn[h, d]).then_inc(sem("c0_in"), 16)
                    load_weights(sp, CH_H + 2 * h + 4)
                load_weights(sp, CH_M + NSLOT)

            @block.gpsimd
            def _(pool):
                for h in range(H):
                    pool.wait_ge(sem("co_ready"), 4 * (h + 1))
                    for d in range(2):
                        pool.dma_start(Cout[h, d], Co[:, 2 * d:2 * d + 2, :]).then_inc(sem("c_out"), 16)
                pool.wait_ge(sem("c_out"), 32 * H)

            @block.tensor
            def _(pe):
                def proj_wait(u):
                    if u >= 2:
                        pe.wait_ge(sem("proj_copied"), u - 1 + (u - 2 + 5) // 9)

                def proj_qk(h):
                    c = CH_H + 2 * h
                    have_weights(pe, c)
                    for m in range(4):
                        u = 9 * h + m
                        proj_wait(u)
                        for k in range(KD):
                            w = wslot(c)[:, k, m * P:(m + 1) * P]
                            mm = pe.matmul(PS[u % 2][:, :], w, hT[:, k, 0:LAT], start=(k == 0), stop=(k == 7))
                        mm.then_inc(sem("qk_done"), 1)
                    for m in range(4):
                        for k in range(KD):
                            mm = pe.matmul(PS[2][:, m * P:(m + 1) * P], wslot(c)[:, k, m * P:(m + 1) * P],
                                           hT[:, k, LAT:TOK], start=(k == 0), stop=(k == 7))
                    mm.then_inc(sem("qk_done"), 1)

                def proj_vo(h):
                    c = CH_H + 2 * h + 1
                    have_weights(pe, c)
                    for t in range(NT):
                        u = 9 * h + 4 + t
                        proj_wait(u)
                        for k in range(KD):
                            mm = pe.matmul(PS[u % 2][:, :], hT[:, k, t * P:(t + 1) * P], wslot(c)[:, k, :],
                                           start=(k == 0), stop=(k == 7))
                        mm.then_inc(sem("vo_done"), 1)

                def scores(h):
                    b = h % 2
                    if h:
                        pe.wait_ge(sem("co_ready"), 4 * h)
                        pe.wait_ge(sem("ha_ready"), 3 * h)
                    else:
                        pe.wait_ge(sem("sel_ready"), 1)
                    for d in range(2):
                        pe.matmul(PS[3 + d][:, :], selH[:, h, :], negM[:, d, 0:LAT], start=True, stop=True)
                        mm = pe.matmul(PS[5][:, d * P:(d + 1) * P], selH[:, h, :], negM[:, d, LAT:TOK], start=True,
                                       stop=True)
                    mm.then_inc(sem("m_spread"), 1)
                    pe.wait_ge(sem("proj_copied"), 10 * h + 5)
                    for s in range(NT):
                        if s == 4:
                            pe.wait_ge(sem("negmd_ready"), h + 1)
                        if 2 <= s < 4:
                            pe.wait_ge(sem("p_ready"), NT * h + s - 1)
                        for k in range(2):
                            if s < 4:
                                mm = pe.matmul(PS[6 + s % 2][:, :], qk[:, b, 2 + k, s * P:(s + 1) * P],
                                               qk[:, b, k, 0:LAT], start=(k == 0), stop=(k == 1))
                            else:
                                mm = pe.matmul(PS[5][:, 2 * P:3 * P], qk[:, b, 2 + k, LAT:TOK],
                                               qk[:, b, k, LAT:TOK], start=(k == 0), stop=(k == 1))
                        mm.then_inc(sem("scores_done"), 1)

                def values(h):
                    b = h % 2
                    pe.wait_ge(sem("p_ready"), NT * (h + 1))
                    pe.wait_ge(sem("proj_copied"), 10 * h + 10)
                    if h == 0:
                        pe.wait_ge(sem("ones_set"), 1)
                    pe.wait_ge(sem("c0_in"), 32 * (h + 1))
                    for n in range(10):
                        t, d = n // 2, n % 2
                        if n >= 2:
                            pe.wait_ge(sem("nd_ready"), 10 * h + n - 1)
                        if t < 4:
                            for k in range(2):
                                pe.matmul(PS[6 + d][:, 0:DH + 1], qk[:, b, k, t * P:(t + 1) * P],
                                          C0[:, 2 * d + k, :], start=(k == 0), stop=(k == 1))
                            ss = range(t + 1) if d == 0 else range(t, 4)
                        else:
                            ss = (4,)
                        for s in ss:
                            if t == 4:
                                o = PW - CTX
                            else:
                                o = OFF[d][s] + (t - s if d == 0 else t) * P
                            mm = pe.matmul(PS[3 + d][:, 0:DH + 1], Pm[:, d, o:o + P], vt[:, b, s, :],
                                           start=(s == ss[0]), stop=(s == ss[-1]))
                        mm.then_inc(sem("pv_done"), 1)

                def turn(h):
                    b = h % 2
                    pe.wait_ge(sem("hn_ready"), h + 1)
                    for r, bank in enumerate((5, 3, 4)):
                        n = 2 if r < 2 else 1
                        for f in range(2):
                            for t in range(n):
                                o = (f * n + t) * P
                                mm = pe.transpose(PS[bank][:, o:o + P], hacc[:, 2 * r + t, f * P:(f + 1) * P], ident)
                        if r == 2:
                            for k in range(2):
                                o = (2 + k) * P
                                mm = pe.transpose(PS[bank][:, o:o + P], qk[:, b, 2 + k, LAT:TOK], ident)
                        mm.then_inc(sem("h_turned"), 1)
                    pe.wait_ge(sem("kw_ready"), h + 1)
                    for n in range(4):
                        d, k = n // 2, n % 2
                        if n >= 2:
                            pe.wait_ge(sem("co_ready"), 4 * h + n - 1)
                        pe.matmul(PS[6 + k][:, 0:DH + 1], kw[:, d, k * P:(k + 1) * P], vt[:, b, 4, :], start=True,
                                  stop=True).then_inc(sem("c_done"), 1)

                proj_qk(0)
                proj_vo(0)
                for h in range(H):
                    scores(h)
                    if h + 1 < H:
                        proj_qk(h + 1)
                    values(h)
                    if h + 1 < H:
                        proj_vo(h + 1)
                    turn(h)

            @block.scalar
            def _(act):
                a = chain(act, "act")

                def out_qk(h):
                    for m in range(4):
                        u = 9 * h + m
                        act.wait_ge(sem("qk_done"), 5 * h + m + 1)
                        act.activation(qk[:, h % 2, m, 0:LAT], PS[u % 2][:, :], ACT.Copy,
                                       scale=DH ** -0.5 if m < 2 else 1.0).then_inc(sem("proj_copied"), 1)
                    act.wait_ge(sem("qk_done"), 5 * h + 5)
                    for x in range(2):
                        ins = act.activation(qk[:, h % 2, 2 * x:2 * x + 2, LAT:TOK],
                                             PS[2][:, 256 * x:256 * x + 256].rearrange("p (m t) -> p m t", m=2),
                                             ACT.Copy, scale=1.0 if x else DH ** -0.5)
                    ins.then_inc(sem("proj_copied"), 1)

                def out_vo(h):
                    for t in range(NT):
                        u = 9 * h + 4 + t
                        act.wait_ge(sem("vo_done"), NT * h + t + 1)
                        act.activation(vt[:, h % 2, t, 0:DH], PS[u % 2][:, 0:DH], ACT.Copy)
                        act.activation(og[:, h % 2, t, :], PS[u % 2][:, DH:2 * DH],
                                       ACT.Sigmoid).then_inc(sem("proj_copied"), 1)

                def decays(h):
                    act.wait_ge(sem("negmd_ready"), h + 1)
                    for s in range(NT):
                        for d in range(2):
                            col = colT[:, s, d, h:h + 1]
                            if s == 4:
                                act.activation(Pm[:, d, PW - CTX:PW], negMd[:, d, LAT:TOK], ACT.Exp, bias=col)
                                at = TOK - 1 if d == 0 else LAT
                                ins = act.activation(wk[:, d:d + 1], negMd[:, d, at:at + 1], ACT.Exp, bias=col)
                                continue
                            o = OFF[d][s]
                            dg = o if d == 0 else o + s * P
                            ins = act.activation(Pm[:, d, dg:dg + P], negMd[:, d, s * P:(s + 1) * P], ACT.Exp, bias=col)
                            if d == 0 and s < 3:
                                ins = act.activation(Pm[:, d, o + P:o + (4 - s) * P], PS[3][:, (s + 1) * P:LAT],
                                                     ACT.Exp, bias=col)
                            if d == 1 and s > 0:
                                ins = act.activation(Pm[:, d, o:o + s * P], PS[4][:, 0:s * P], ACT.Exp, bias=col)
                        ins.then_inc(sem("decay_ready"), 1)

                def inter(h):
                    for n in range(8):
                        t, d = n // 2, n % 2
                        act.wait_ge(sem("pv_done"), 10 * h + n + 1)
                        if n >= 2:
                            act.wait_ge(sem("nd_ready"), 10 * h + n - 1)
                        act.activation(Qs[:, d, :], PS[6 + d][:, 0:DH + 1], ACT.Copy,
                                       scale=colT[:, t, 2 + d, h:h + 1]).then_inc(sem("inter_ready"), 1)

                def finish(h):
                    act.wait_ge(sem("ms_inv"), h + 1)
                    act.activation(rs5[:], ssq[:], ACT.Sqrt).then_inc(sem("rs_ready"), 1)
                    for r, bank in enumerate((5, 3, 4)):
                        act.wait_ge(sem("h_turned"), 3 * h + r + 1)
                        w = 256 if r < 2 else P
                        for f in range(2):
                            ins = act.activation(haT[:, 2 * h + f, r * 256:r * 256 + w], PS[bank][:, f * w:(f + 1) * w],
                                                 ACT.Copy, scale=par[:, PC_HN + 2 * h + f:PC_HN + 2 * h + f + 1])
                        ins.then_inc(sem("ha_ready"), 1)
                    if h:
                        act.wait_ge(sem("c_out"), 32 * h)
                    for n in range(4):
                        act.wait_ge(sem("c_done"), 4 * h + n + 1)
                        act.activation(Co[:, n, :], PS[6 + n % 2][:, 0:DH + 1], ACT.Copy).then_inc(sem("co_ready"), 1)

                out_qk(0)
                out_vo(0)
                for h in range(H):
                    decays(h)
                    if h + 1 < H:
                        out_qk(h + 1)
                    inter(h)
                    if h + 1 < H:
                        out_vo(h + 1)
                    finish(h)

            @block.vector
            def _(dve):
                v = chain(dve, "dve")

                def weigh(h):
                    dve.wait_ge(sem("m_spread"), h + 1)
                    for d, mask in enumerate((mask_f, mask_b)):
                        dve.tensor_tensor(negMd[:, d, 0:LAT].rearrange("p (s t) -> p s t", s=4),
                                          PS[3 + d][:, :].rearrange("p (s t) -> p s t", s=4),
                                          bc(mask.unsqueeze(1), [P, 4, P]), ALU.add)
                        ins = dve.tensor_tensor(negMd[:, d, LAT:TOK], PS[5][:, d * P:(d + 1) * P], mask, ALU.add)
                    ins.then_inc(sem("negmd_ready"), 1)
                    for s in range(NT):
                        dve.wait_ge(sem("scores_done"), NT * h + s + 1)
                        dve.wait_ge(sem("decay_ready"), NT * h + s + 1)
                        for d in range(2):
                            if s == 4:
                                x, sc = Pm[:, d, PW - CTX:PW], PS[5][:, 2 * P:3 * P]
                            elif d == 0:
                                x, sc = Pm[:, 0, OFF[0][s]:OFF[0][s] + (4 - s) * P], PS[6 + s % 2][:, s * P:LAT]
                            else:
                                x, sc = Pm[:, 1, OFF[1][s]:OFF[1][s] + (s + 1) * P], PS[6 + s % 2][:, 0:(s + 1) * P]
                            ins = dve.tensor_tensor(x, x, sc, ALU.mult)
                        ins.then_inc(sem("p_ready"), 1)

                def combine(h):
                    for n in range(10):
                        t, d = n // 2, n % 2
                        dve.wait_ge(sem("pv_done"), 10 * h + n + 1)
                        if t < 4:
                            dve.wait_ge(sem("inter_ready"), 8 * h + n + 1)
                            dve.tensor_tensor(nd[:, d, :], PS[3 + d][:, 0:DH + 1], Qs[:, d, :],
                                              ALU.add).then_inc(sem("nd_ready"), 1)
                        else:
                            dve.tensor_copy(nd[:, d, :], PS[3 + d][:, 0:DH + 1]).then_inc(sem("nd_ready"), 1)
                        if d == 0:
                            continue
                        dve.wait_ge(sem("nd_ready"), 10 * h + n + 1)
                        v(dve.scalar_tensor_tensor(rr[:], nd[:, :, DH], -1.0, nd[:, :, DH], ALU.mult, ALU.max))
                        v(dve.tensor_tensor(rr[:], rr[:], colT[:, t, 4:6, h], ALU.max))
                        v(dve.reciprocal(rr[:], rr[:]))
                        x = hacc[:, t, :]
                        v(dve.tensor_scalar(x, nd[:, 0, 0:DH], rr[:, 0:1], None, ALU.mult))
                        v(dve.scalar_tensor_tensor(x, nd[:, 1, 0:DH], rr[:, 1:2], x, ALU.mult, ALU.add))
                        dve.wait_ge(sem("proj_copied"), 10 * h + 5 + t + 1)
                        v(dve.tensor_tensor(x, x, og[:, h % 2, t, :], ALU.mult))
                        v(dve.scalar_tensor_tensor(junk[:], x, 1.0, x, ALU.mult, ALU.mult, accum_out=ssq[:, t:t + 1]))

                def finish(h):
                    v(dve.tensor_scalar(ssq[:], ssq[:], 1.0 / DH, EPS, ALU.mult, ALU.add))
                    dve.reciprocal(ssq[:], ssq[:]).then_inc(sem("ms_inv"), 1)
                    dve.wait_ge(sem("rs_ready"), h + 1)
                    for t in range(NT):
                        ins = dve.tensor_scalar(hacc[:, t, :], hacc[:, t, :], rs5[:, t:t + 1], None, ALU.mult)
                    ins.then_inc(sem("hn_ready"), 1)
                    dve.wait_ge(sem("ha_ready"), 3 * h + 3)
                    for d in range(2):
                        ins = dve.tensor_scalar(kw[:, d, :], PS[4][:, 2 * P:4 * P], wk[:, d:d + 1], None, ALU.mult)
                    ins.then_inc(sem("kw_ready"), 1)

                dve.tensor_copy(selH[:], bc(ident[0:H, 0:H].unsqueeze(2), [H, H, P])).then_inc(sem("sel_ready"), 1)
                dve.memset(vt[:, :, :, DH:DH + 1], 1.0).then_inc(sem("ones_set"), 1)
                for h in range(H):
                    weigh(h)
                    combine(h)
                    finish(h)

        with ExitStack() as st:
            mg = sb("mg", [P, KD, TOK], F32, st)
            sg = sb("sg2", [P, 2, TOK], F32, st)
            tm = sb("tm", [P, 2, TOK], F32, st)
            tmp = sb("tmp6", [P, TOK], F32, st)
            block = st.enter_context(nc.Block())

            @block.sync
            def _(sp):
                load_weights(sp, len(plan))

            @block.tensor
            def _(pe):
                for m in range(KD):
                    cg, cp = CH_M + 2 * (m // 2), CH_M + 2 * (m // 2) + 1
                    for x in range(4):
                        if m >= 1:
                            pe.wait_ge(sem("gate_sig" if x < 2 else "branch_used"), 2 * (m - 1) + x % 2 + 1)
                        c = cg if x < 2 else cp
                        have_weights(pe, c)
                        src = (hT, hT, haT, hbT)[x]
                        kt = 4 if x == 3 else 8
                        o = 256 * (x % 2) + (m % 2) * P
                        for k in range(kt):
                            w = wslot(c)[:, k, o:o + P]
                            pe.matmul(PS[x][:, :], w, src[:, k, 0:LAT], start=(k == 0), stop=(k == kt - 1))
                            mm = pe.matmul(PS[4 + x][:, 0:CTX], w, src[:, k, LAT:TOK],
                                           start=(k == 0), stop=(k == kt - 1))
                        mm.then_inc(sem("merge_done"), 1)
                pe.wait_ge(sem("mg_ready"), KD)
                for m in range(KD):
                    c = CH_O + m // 4
                    have_weights(pe, c)
                    if m >= 2:
                        pe.wait_ge(sem("x2_ready"), m - 1)
                    for k in range(KD):
                        w = wslot(c)[:, k, (m % 4) * P:(m % 4 + 1) * P]
                        pe.matmul(PS[m % 2][:, :], w, mg[:, k, 0:LAT], start=(k == 0), stop=(k == 7))
                        mm = pe.matmul(PS[2 + m % 2][:, 0:CTX], w, mg[:, k, LAT:TOK], start=(k == 0), stop=(k == 7))
                    mm.then_inc(sem("out_done"), 1)
                pe_mean_square(pe, 1)

            @block.scalar
            def _(act):
                for m in range(KD):
                    for x in range(2):
                        act.wait_ge(sem("merge_done"), 4 * m + x + 1)
                        if m:
                            act.wait_ge(sem("branch_used"), 2 * (m - 1) + x + 1)
                        act.activation(sg[:, x, 0:LAT], PS[x][:, :], ACT.Sigmoid)
                        act.activation(sg[:, x, LAT:TOK], PS[4 + x][:, 0:CTX],
                                       ACT.Sigmoid).then_inc(sem("gate_sig"), 1)
                for k in range(KD):
                    act.wait_ge(sem("x2_ready"), k + 1)
                    act_square(act, 1, k)
                act_rms(act, 1, tmp)
                act_modulate(act, 1, hT)

            @block.vector
            def _(dve):
                v = chain(dve, "dve")
                for m in range(KD):
                    if m:
                        dve.wait_ge(sem("mg_ready"), m)
                    for x in range(2):
                        dve.wait_ge(sem("gate_sig"), 2 * m + x + 1)
                        dve.wait_ge(sem("merge_done"), 4 * m + 2 + x + 1)
                        dve.tensor_tensor(tm[:, x, 0:LAT], sg[:, x, 0:LAT], PS[2 + x][:, :], ALU.mult)
                        dve.tensor_tensor(tm[:, x, LAT:TOK], sg[:, x, LAT:TOK], PS[6 + x][:, 0:CTX],
                                          ALU.mult).then_inc(sem("branch_used"), 1)
                    dve.wait_ge(sem("branch_used"), 2 * m + 2)
                    dve.tensor_tensor(mg[:, m, :], tm[:, 0, :], tm[:, 1, :], ALU.add).then_inc(sem("mg_ready"), 1)
                for m in range(KD):
                    dve.wait_ge(sem("out_done"), m + 1)
                    dve.scalar_tensor_tensor(xT[:, m, 0:LAT], PS[m % 2][:, :], modT[:, 16 + m, 0:1], xT[:, m, 0:LAT],
                                             ALU.mult, ALU.add)
                    dve.scalar_tensor_tensor(xT[:, m, LAT:TOK], PS[2 + m % 2][:, 0:CTX], modT[:, 16 + m, 1:2],
                                             xT[:, m, LAT:TOK], ALU.mult, ALU.add).then_inc(sem("x2_ready"), 1)
                dve_inverse_mean(dve, v, 1, tmp)
                dve_normalise(dve, 1)
        acts.close()

        moe = ctx.enter_context(ExitStack())
        w13 = sb("w13", [P, FG, 2, KD, FT * P], F32, moe)
        w2 = sb("w2", [P, FG, FT, D], F32, moe)
        gval = sb("gval", [CAP, E], F32, moe)
        gidx = sb("gidx", [CAP, E], I32, moe)
        we1 = ar["w_e1"][0].rearrange("e (k p) f -> p e k f", p=P)
        we3 = ar["w_e3"][0].rearrange("e (k p) f -> p e k f", p=P)
        we2 = ar["w_e2"][0].rearrange("e (t p) d -> p e t d", p=P)

        def load_w13(sp, e, q):
            c = q * FT * P
            for x, src in enumerate((we1, we3)):
                sp.dma_start(w13[:, q, x], src[:, bass.ds(e, 1), :, c:c + FT * P].rearrange("p e k f -> p (e k) f")
                             ).then_inc(sem(f"w13_in{q}"), 16)

        def load_w2(sp, e, q):
            sp.dma_start(w2[:, q], we2[:, bass.ds(e, 1), q * FT:(q + 1) * FT, :].rearrange("p e t d -> p (e t) d")
                         ).then_inc(sem(f"w2_in{q}"), 16)

        with ExitStack() as st:
            wr = sb("wr", [P, KD, E], F32, st)
            htok = sb("htok", [P, 2, D], F32, st)
            lg = sb("lg", [P, NT, E], F32, st)
            mx = sb("mx", [P, NT], F32, st)
            af = sb("af", [E, TOK], F32, st)
            topv = sb("topv", [E, CAP], F32, st)
            topi = sb("topi", [E, CAP], U32, st)
            topf = sb("topf", [E, CAP], F32, st)
            block = st.enter_context(nc.Block())

            @block.sync
            def _(sp):
                with nc.allow_non_contiguous_dma(reason="small"):
                    sp.dma_start(wr[:], ar["w_router"][0].rearrange("(k p) e -> p k e", p=P)).then_inc(sem("wr_in"), 16)
                for q in range(FG):
                    load_w13(sp, 0, q)
                    load_w2(sp, 0, q)
                for t in range(NT):
                    sp.wait_ge(sem("htok_ready"), t + 1)
                    sp.dma_start(ar["h2"][t * P:(t + 1) * P, :], htok[:, t % 2, :]).then_inc(sem(f"h2_out{t % 2}"), 16)
                sp.wait_ge(sem("h2_out0"), 48)
                sp.wait_ge(sem("h2_out1"), 32)

            @block.tensor
            def _(pe):
                pe.wait_ge(sem("wr_in"), 16)
                for t in range(NT):
                    for k in range(KD):
                        mm = pe.matmul(PS[0][:, E * t:E * t + E], hT[:, k, t * P:(t + 1) * P], wr[:, k, :],
                                       start=(k == 0), stop=(k == 7))
                mm.then_inc(sem("logits_done"), 1)
                for t in range(NT):
                    if t >= 2:
                        pe.wait_ge(sem("htok_ready"), t - 1)
                    for k in range(KD):
                        mm = pe.transpose(PS[1 + 2 * (t % 2) + k // 4][:, (k % 4) * P:(k % 4 + 1) * P],
                                          hT[:, k, t * P:(t + 1) * P], ident)
                    mm.then_inc(sem("h2_turned"), 1)
                pe.wait_ge(sem("aff_ready"), 1)
                for t in range(NT):
                    mm = pe.transpose(PS[5 + t // 4][0:E, (t % 4) * P:(t % 4 + 1) * P], lg[:, t, :], ident)
                mm.then_inc(sem("aff_turned"), 1)
                pe.wait_ge(sem("top_ready"), 1)
                pe.transpose(PS[7][0:CAP, 0:E], topv[:], ident[0:E, 0:E])
                pe.transpose(PS[7][0:CAP, E:2 * E], topf[:], ident[0:E, 0:E]).then_inc(sem("top_turned"), 1)

            @block.scalar
            def _(act):
                act.wait_ge(sem("lg_shifted"), 1)
                act.activation(lg[:], lg[:], ACT.Exp).then_inc(sem("lg_exp"), 1)
                for t in range(NT):
                    act.wait_ge(sem("h2_turned"), t + 1)
                    if t >= 2:
                        act.wait_ge(sem(f"h2_out{t % 2}"), 16 * (t // 2))
                    for x in range(2):
                        ins = act.activation(htok[:, t % 2, x * 512:(x + 1) * 512], PS[1 + 2 * (t % 2) + x][:, :],
                                             ACT.Copy)
                    ins.then_inc(sem("htok_ready"), 1)

            @block.vector
            def _(dve):
                v = chain(dve, "dve")
                dve.wait_ge(sem("logits_done"), 1)
                v(dve.tensor_tensor(lg[:], PS[0][:, 0:NT * E].rearrange("p (t e) -> p t e", t=NT),
                                    bc(par[:, PC_BR:PC_BR + E].unsqueeze(1), [P, NT, E]), ALU.add))
                v(dve.tensor_reduce(mx[:], lg[:], AX.X, ALU.max))
                dve.tensor_tensor(lg[:], lg[:], bc(mx[:].unsqueeze(2), [P, NT, E]),
                                  ALU.subtract).then_inc(sem("lg_shifted"), 1)
                dve.wait_ge(sem("lg_exp"), 1)
                v(dve.tensor_reduce(mx[:], lg[:], AX.X, ALU.add))
                v(dve.reciprocal(mx[:], mx[:]))
                dve.tensor_tensor(lg[:], lg[:], bc(mx[:].unsqueeze(2), [P, NT, E]),
                                  ALU.mult).then_inc(sem("aff_ready"), 1)
                dve.wait_ge(sem("aff_turned"), 1)
                dve.tensor_copy(af[:, 0:LAT], PS[5][0:E, :])
                v(dve.tensor_copy(af[:, LAT:TOK], PS[6][0:E, 0:CTX]))
                for lo, hi, at, cap in ((0, LAT, 0, CAPL), (LAT, TOK, CAPL, CAPC)):
                    for o in range(at, at + cap, 8):
                        v(dve.max(topv[:, o:o + 8], af[:, lo:hi]))
                        v(dve.max_index(topi[:, o:o + 8], topv[:, o:o + 8], af[:, lo:hi]))
                        if o + 8 < at + cap:
                            v(dve.match_replace(af[:, lo:hi], topv[:, o:o + 8], af[:, lo:hi], -1.0))
                v(dve.tensor_copy(topf[:], topi[:]))
                dve.tensor_scalar(topf[:, CAPL:CAP], topf[:, CAPL:CAP], float(LAT), None,
                                  ALU.add).then_inc(sem("top_ready"), 1)
                dve.wait_ge(sem("top_turned"), 1)
                dve.tensor_copy(gval[:], PS[7][0:CAP, 0:E])
                dve.tensor_copy(gidx[:], PS[7][0:CAP, E:2 * E])

        with ExitStack() as st:
            rows = hT[:].rearrange("p k t -> p (k t)")
            xe = rows[0:CAP, 0:2 * D].rearrange("p (b d) -> p b d", b=2)
            ys = rows[0:CAP, 2 * D:4 * D].rearrange("p (b d) -> p b d", b=2)
            xeT = sb("xeT", [P, 2, KD, CAP], F32, st)
            sl = sb("sl", [P, 2, FT * CAP], F32, st)
            hid = sb("hid", [P, 2, FT * CAP], F32, st)
            block = st.enter_context(nc.Block())
            HC = FT * CAP

            @block.sync
            def _(sp):
                with sp.Fori(1, E) as e:
                    for q in range(FG):
                        sp.wait_ge(sem("hidden_done"), 4 * e + (q - 3))
                        load_w13(sp, e, q)
                        sp.wait_ge(sem("down_done"), 4 * e + (q - 3))
                        load_w2(sp, e, q)

            @block.gpsimd
            def _(pool):
                def gather(e):
                    if e >= 2:
                        pool.wait_ge(sem("x_turned"), e - 1)
                    pool.indirect_dma_start(out=xe[:, e % 2, :], out_offset=None, in_=ar["h2"][:, :],
                                            in_offset=bass.IndirectOffsetOnAxis(ap=gidx[:, e:e + 1], axis=0)
                                            ).then_inc(sem(f"xe_in{e % 2}"), 16)

                def scatter(e):
                    pool.wait_ge(sem("y_ready"), e + 1)
                    if e:
                        pool.wait_ge(sem(f"y_out{(e - 1) % 2}"), 16 * ((e - 1) // 2 + 1))
                    pool.indirect_dma_start(out=ar["moe"][:, :],
                                            out_offset=bass.IndirectOffsetOnAxis(ap=gidx[:, e:e + 1], axis=0),
                                            in_=ys[:, e % 2, :], in_offset=None, compute_op=ALU.add
                                            ).then_inc(sem(f"y_out{e % 2}"), 16)

                gather(0)
                for e in range(E):
                    if e + 1 < E:
                        gather(e + 1)
                    scatter(e)
                pool.wait_ge(sem("y_out0"), 16 * E // 2)
                pool.wait_ge(sem("y_out1"), 16 * E // 2)

            def pairs(eng, body):
                body(0, 0)
                body(0, 1)
                with eng.Fori(1, E // 2) as i:
                    body(i, 0)
                    body(i, 1)

            def is_first(i, u):
                return isinstance(i, int) and i == 0 and u == 0

            @block.tensor
            def _(pe):
                def down(i, u, q):
                    n = 8 * i + 4 * u + q
                    pe.wait_ge(sem("hid_ready"), n + 1)
                    pe.wait_ge(sem(f"w2_in{q}"), 32 * i + 16 * u + 16)
                    for t in range(FT):
                        for x in range(2):
                            mm = pe.matmul(PS[2 + x][0:CAP, :], hid[:, q % 2, t * CAP:(t + 1) * CAP],
                                           w2[:, q, t, x * 512:(x + 1) * 512], start=(q == 0 and t == 0),
                                           stop=(q == FG - 1 and t == FT - 1))
                    mm.then_inc(sem("down_done"), 1)

                def body(i, u):
                    first = is_first(i, u)
                    pe.wait_ge(sem(f"xe_in{u}"), 16 * i + 16)
                    for k in range(KD):
                        mm = pe.transpose(PS[4 + k // 4][:, (k % 4) * CAP:(k % 4 + 1) * CAP],
                                          xe[:, u, k * P:(k + 1) * P], ident[0:CAP, 0:CAP])
                    mm.then_inc(sem("x_turned"), 1)
                    if not first:
                        down(i if u else i - 1, 1 - u, FG - 1)
                    pe.wait_ge(sem("xt_ready"), 2 * i + u + 1)
                    for q in range(FG):
                        if not (first and q < 2):
                            pe.wait_ge(sem("hid_ready"), 8 * i + (4 * u + q - 1))
                        pe.wait_ge(sem(f"w13_in{q}"), 64 * i + 32 * u + 32)
                        for x in range(2):
                            for t in range(FT):
                                o = x * HC + t * CAP
                                for k in range(KD):
                                    mm = pe.matmul(PS[q % 2][:, o:o + CAP], w13[:, q, x, k, t * P:(t + 1) * P],
                                                   xeT[:, u, k, :], start=(k == 0), stop=(k == 7))
                        mm.then_inc(sem("hidden_done"), 1)
                        if q == 1 and not first:
                            pe.wait_ge(sem("y_ready"), 2 * i + u)
                        if q >= 1:
                            down(i, u, q - 1)

                pairs(pe, body)
                down(E // 2 - 1, 1, FG - 1)

            @block.scalar
            def _(act):
                def body(i, u):
                    act.wait_ge(sem("x_turned"), 2 * i + u + 1)
                    for x in range(2):
                        ins = act.activation(xeT[:, u, 4 * x:4 * x + 4, :].rearrange("p k c -> p (k c)"),
                                             PS[4 + x][:, 0:4 * CAP], ACT.Copy)
                    ins.then_inc(sem("xt_ready"), 1)
                    for q in range(FG):
                        act.wait_ge(sem("hidden_done"), 8 * i + 4 * u + q + 1)
                        if not (is_first(i, u) and q < 2):
                            act.wait_ge(sem("hid_ready"), 8 * i + (4 * u + q - 1))
                        act.activation(sl[:, q % 2, :], PS[q % 2][:, 0:HC], ACT.Silu).then_inc(sem("silu_ready"), 1)

                pairs(act, body)

            @block.vector
            def _(dve):
                def take_y(i, u):
                    dve.wait_ge(sem("down_done"), 8 * i + 4 * u + 4)
                    if not (isinstance(i, int) and i == 0):
                        dve.wait_ge(sem(f"y_out{u}"), 16 * i)
                    g = gval[:, bass.ds(2 * i + u, 1)]
                    dve.tensor_scalar(ys[:, u, 0:512], PS[2][0:CAP, :], g, None, ALU.mult)
                    dve.tensor_scalar(ys[:, u, 512:D], PS[3][0:CAP, :], g, None, ALU.mult).then_inc(sem("y_ready"), 1)

                def body(i, u):
                    first = is_first(i, u)
                    if not first:
                        take_y(i if u else i - 1, 1 - u)
                    for q in range(FG):
                        dve.wait_ge(sem("silu_ready"), 8 * i + 4 * u + q + 1)
                        if not (first and q < 2):
                            dve.wait_ge(sem("down_done"), 8 * i + (4 * u + q - 1))
                        dve.tensor_tensor(hid[:, q % 2, :], sl[:, q % 2, :], PS[q % 2][:, HC:2 * HC],
                                          ALU.mult).then_inc(sem("hid_ready"), 1)

                pairs(dve, body)
                take_y(E // 2 - 1, 1)
        moe.close()

        with ExitStack() as st:
            mt = sb("mt", [P, NT, D], F32, st)
            yT = sb("yT", [P, KD, TOK], F32, st)
            tmp = sb("tmp9", [P, TOK], F32, st)
            block = st.enter_context(nc.Block())

            @block.sync
            def _(sp):
                for t in range(NT):
                    sp.dma_start(mt[:, t, :], ar["moe"][t * P:(t + 1) * P, :]).then_inc(sem(f"mt_in{t}"), 16)
                for k in range(KD):
                    sp.wait_ge(sem("y_done"), k + 1)
                    sp.dma_start(out["yT"][:, k, :], yT[:, k, :]).then_inc(sem("yT_out"), 16)
                sp.wait_ge(sem("yT_out"), 16 * KD)

            @block.tensor
            def _(pe):
                for k in range(KD):
                    if k >= 2:
                        pe.wait_ge(sem("x3_ready"), k - 1)
                    for t in range(NT):
                        if k == 0:
                            pe.wait_ge(sem(f"mt_in{t}"), 16)
                        dst = PS[k % 2][:, t * P:(t + 1) * P] if t < 4 else PS[2 + k % 2][:, 0:CTX]
                        mm = pe.transpose(dst, mt[:, t, k * P:(k + 1) * P], ident)
                    mm.then_inc(sem("moe_turned"), 1)
                pe_mean_square(pe, 2)

            @block.scalar
            def _(act):
                for k in range(KD):
                    act.wait_ge(sem("x3_ready"), k + 1)
                    act_square(act, 2, k)
                act_rms(act, 2, tmp)
                for k in range(KD):
                    act.wait_ge(sem("normalised"), 16 + k + 1)
                    act.activation(yT[:, k, :], sq[:, k % 2, :], ACT.Copy,
                                   scale=par[:, PC_NFIN + k:PC_NFIN + k + 1]).then_inc(sem("y_done"), 1)

            @block.vector
            def _(dve):
                v = chain(dve, "dve")
                for k in range(KD):
                    dve.wait_ge(sem("moe_turned"), k + 1)
                    dve.scalar_tensor_tensor(xT[:, k, 0:LAT], PS[k % 2][:, :], modT[:, 40 + k, 0:1], xT[:, k, 0:LAT],
                                             ALU.mult, ALU.add)
                    dve.scalar_tensor_tensor(xT[:, k, LAT:TOK], PS[2 + k % 2][:, 0:CTX], modT[:, 40 + k, 1:2],
                                             xT[:, k, LAT:TOK], ALU.mult, ALU.add).then_inc(sem("x3_ready"), 1)
                dve_inverse_mean(dve, v, 2, tmp)
                dve.wait_ge(sem("rms"), 3)
                for k in range(KD):
                    if k >= 2:
                        dve.wait_ge(sem("y_done"), k - 1)
                    dve.tensor_tensor(sq[:, k % 2, :], xT[:, k, :], rsb[:], ALU.mult).then_inc(sem("normalised"), 1)


def _positions():
    q = D // 4
    n = np.arange(LAT)
    r, c = (n // 64).astype(np.float32), (n % 64).astype(np.float32)
    fr = (1.0 / (np.float32(10000.0) ** (np.arange(q, dtype=np.float32) / np.float32(q)))).astype(np.float32)
    er, ec = r[:, None] * fr, c[:, None] * fr
    return np.concatenate([np.sin(er), np.cos(er), np.sin(ec), np.cos(ec)], -1).astype(np.float32)


def _feature_major(a):
    return np.ascontiguousarray(np.asarray(a).reshape(a.shape[0], -1, P).transpose(2, 1, 0))


def kernel(**inputs):
    import concourse.bacc as bacc
    from concourse.bass_utils import run_bass_kernel_spmd

    i = {k: np.asarray(v) for k, v in inputs.items()}
    col = lambda a, n: np.asarray(a).reshape(n, P).T
    both = lambda a: np.concatenate([a, a], 0)
    dirp = lambda a: np.asarray(a).reshape(2, GN, SP_).transpose(0, 2, 1).reshape(P, GN)
    c2 = np.stack([i["c"][0], i["c_ctx"]])
    arrays = {}
    arrays["par"] = np.concatenate([
        _feature_major(c2).reshape(P, 16), col(i["b_ada"][0], 48), col(i["norm_mix"][0], 8), col(i["norm_ffn"][0], 8),
        col(i["norm_final"], 8), col(i["head_norm"][0].reshape(-1), 8), col(i["b_glu"][0], 4),
        np.broadcast_to(i["b_router"][0][None], (P, E))], 1)
    arrays["consts"] = np.stack([np.eye(P), np.where(np.arange(P)[None] >= np.arange(P)[:, None], 0, -1e30),
                                 np.where(np.arange(P)[None] <= np.arange(P)[:, None], 0, -1e30)],
                                1).astype(np.float32)
    arrays["xT"] = _feature_major(np.concatenate([i["x_sample"][0], i["x_prompt"][0]], 0))
    arrays["posT"] = _feature_major(_positions())
    arrays["gpar"] = np.concatenate([i["b_gate"][0].T, i["state_mlstm_m"][0, 0].T], 1)
    ldt = np.repeat(i["s5_log_dt"][0], SP_, 0).reshape(P, GN)
    arrays["s5p"] = np.stack([dirp(i["s5_a_re"][0]), dirp(i["s5_a_im"][0]), ldt,
                              dirp(i["state_s5_re"][0, 0]), dirp(i["state_s5_im"][0, 0])], 1)
    arrays["s5bc"] = np.stack(
        [both(i[n][0].transpose(1, 0, 2)) for n in ("s5_b_re", "s5_b_im")]
        + [i[n][0].transpose(0, 3, 1, 2).reshape(P, GN, GC) for n in ("s5_c_re", "s5_c_im")], 1)
    arrays["s5d"] = i["s5_d"][0].reshape(GN, GC).T
    arrays["Cn"] = np.concatenate([i["state_mlstm_C"][0, 0], i["state_mlstm_n"][0, 0][..., None]], -1)
    for n in ("w_ada", "w_in", "w_pA", "w_pB", "w_out", "w_glu", "w_router", "w_e1", "w_e3", "w_e2"):
        arrays[n] = i[n]
    arrays = {k: np.ascontiguousarray(a) for k, a in arrays.items()}

    nc = bacc.Bacc("TRN2", target_bir_lowering=False, num_devices=1)
    ar = {k: nc.dram_tensor(k + "_dram", a.shape, mybir.dt.from_np(a.dtype), kind="ExternalInput").ap()
          for k, a in arrays.items()}
    ar["moe"] = nc.dram_tensor("moe_dram", (TOK, D), F32, kind="Internal").ap()
    ar["h2"] = nc.dram_tensor("h2_dram", (TOK, D), F32, kind="Internal").ap()
    shapes = {"yT": (P, KD, TOK), "Cn": (2, H, DH, DH + 1), "m": (2, H), "s5": (2, P, GN)}
    out = {k: nc.dram_tensor("out_" + k, s, F32, kind="ExternalOutput").ap() for k, s in shapes.items()}
    program(nc, ar, out)
    r = run_bass_kernel_spmd(nc, [{k + "_dram": a for k, a in arrays.items()}], core_ids=[0]).results[0]
    y = np.asarray(r["out_yT"]).transpose(2, 1, 0).reshape(TOK, D)
    Cn = np.asarray(r["out_Cn"])
    s5 = np.asarray(r["out_s5"]).reshape(2, 2, SP_, GN).transpose(0, 1, 3, 2)
    full = lambda a: np.ascontiguousarray(a)[None, None]
    return (np.ascontiguousarray(y[LAT:])[None], np.ascontiguousarray(y[:LAT])[None], full(Cn[..., :DH]),
            full(Cn[..., DH]), full(np.asarray(r["out_m"])), full(s5[0]), full(s5[1]))
```

```python
from contextlib import ExitStack

import numpy as np
import concourse.bass as bass
from concourse import mybir

F32 = mybir.dt.float32
F32R = mybir.dt.float32r
U32 = mybir.dt.uint32
I32 = mybir.dt.int32
ALU = mybir.AluOpType
ACT = mybir.ActivationFunctionType
AX = mybir.AxisListType

P = 128
D = 1024
KD = D // P
LAT, CTX = 512, 128
TOK = LAT + CTX
NT = TOK // P
H, DH = 4, 256
MW = H * DH
SW, GC, GN, SP_ = 512, 16, 32, 64
L = 8
JL, JC = LAT // L, CTX // L
J = JL + JC
NS_ = (JL + 1) + (JC + 1)
QG = 8
NQ = GN // QG
E, FF = 16, 1536
CAPL, CAPC = 2 * LAT // E, 2 * CTX // E
CAP = CAPL + CAPC
FG = 6
FT = FF // P // FG
EPS = 1e-6
IN_COLS = 4 * MW + 4 * H + SW + 2 * D
C_Q, C_K, C_V, C_O, C_G = 0, MW, 2 * MW, 3 * MW, 4 * MW
C_U = C_G + 4 * H
C_GA = C_U + SW
C_GB = C_GA + D
NSLOT = 3

PC_C, PC_BADA, PC_NMIX, PC_NFFN, PC_NFIN, PC_HN, PC_BGLU, PC_BR = 0, 16, 64, 72, 80, 88, 96, 100
PC_N = 116


def bc(ap, shape):
    return ap.to_broadcast(shape)


class Chain:

    def __init__(self, eng, sem):
        self.eng, self.sem, self.n = eng, sem, 0

    def __call__(self, ins):
        self.n += 1
        ins.then_inc(self.sem, 1)
        self.eng.wait_ge(self.sem, self.n)


def program(nc, ar, out):
    with ExitStack() as ctx:
        def sb(name, shape, dt=F32, stack=None):
            return (stack or ctx).enter_context(nc.sbuf_tensor(name, shape, dt))

        sems = {}

        def sem(name):
            if name not in sems:
                sems[name] = ctx.enter_context(nc.semaphore(name))
            return sems[name]

        chains = {}

        def chain(eng, name):
            if name not in chains:
                chains[name] = Chain(eng, sem("order_" + name))
            chains[name].eng = eng
            return chains[name]

        PS = [ctx.enter_context(nc.psum_tensor(f"bank{i}", [P, 512], F32)) for i in range(8)]

        par = sb("par", [P, PC_N])
        consts = sb("consts", [P, 3, P])
        ident, mask_f, mask_b = consts[:, 0, :], consts[:, 1, :], consts[:, 2, :]
        meanw = sb("meanw", [P, P])
        modT = sb("modT", [P, 48, 2])
        gain = sb("gain", [P, 2, KD, 2])
        xT = sb("xT", [P, KD, TOK])
        rsb = sb("rsb", [P, TOK])
        sq = sb("sq", [P, 2, TOK])
        gpar = sb("gpar", [H, 6])
        wr = sb("wr", [P, KD, E])
        hT = sb("hT", [P, KD, TOK])
        acts = ctx.enter_context(ExitStack())
        W = sb("W", [P, NSLOT, 4096], F32, acts)
        hbT = sb("hbT", [P, 4, TOK], F32, acts)
        colT = sb("colT", [P, NT, 6, H], F32, acts)
        negM = sb("negM", [H, 2, TOK], F32, acts)

        w_in = ar["w_in"][0].rearrange("(k p) n -> p k n", p=P)
        w_ada = ar["w_ada"][0].rearrange("(k p) n -> p k n", p=P)
        w_pA = ar["w_pA"][0].rearrange("(k p) n -> p k n", p=P)
        w_pB = ar["w_pB"][0].rearrange("(k p) n -> p k n", p=P)
        w_out = ar["w_out"][0].rearrange("(k p) n -> p k n", p=P)
        w_glu = ar["w_glu"][0].rearrange("(k p) n -> p k n", p=P)
        plan = []

        def ada_piece(c, slot):
            plan.append(([(8, 0, w_ada[:, :, 512 * c:512 * c + 512])], "ada_done", c + 1, slot))

        for c in range(4):
            ada_piece(c, c % NSLOT)
        CH_U = len(plan)
        plan.append(([(8, 0, w_in[:, :, C_U:C_U + SW])], "u_done", 4, 1))
        CH_A = len(plan)
        for c in range(4, 12):
            ada_piece(c, 1)
        CH_H = len(plan)

        def piece(parts, freed_by, value):
            plan.append((parts, freed_by, value, (1 + len(plan) - CH_H) % NSLOT))

        for h in range(H):
            o = h * DH
            piece([(8, 0, w_in[:, :, C_Q + o:C_Q + o + DH]), (8, DH, w_in[:, :, C_K + o:C_K + o + DH])],
                  "qk_done", 5 * (h + 1))
            piece([(8, 0, w_in[:, :, C_V + o:C_V + o + DH]), (8, DH, w_in[:, :, C_O + o:C_O + o + DH])],
                  "vo_done", NT * (h + 1))
        CH_M = len(plan)
        for m in range(4):
            o = 256 * m
            piece([(8, 0, w_in[:, :, C_GA + o:C_GA + o + 256]), (8, 256, w_in[:, :, C_GB + o:C_GB + o + 256])],
                  "merge_done", 4 * (2 * m + 1) + 2)
            piece([(8, 0, w_pA[:, :, o:o + 256]), (4, 256, w_pB[:, :, o:o + 256])],
                  "merge_done", 4 * (2 * m + 1) + 4)
        CH_O = len(plan)
        for m in range(2):
            piece([(8, 0, w_out[:, :, 512 * m:512 * m + 512])], "out_done", 4 * (m + 1))
        landed, before, per_slot, last_in = [], [], [0] * NSLOT, [None] * NSLOT
        for c, (parts, _, _, slot) in enumerate(plan):
            per_slot[slot] += 16 * len(parts)
            landed.append(per_slot[slot])
            before.append(last_in[slot])
            last_in[slot] = c
        issued = [0]

        def wslot(c, kt=8):
            return W[:, plan[c][3], 0:kt * 512].rearrange("p (k n) -> p k n", k=kt)

        def load_weights(eng, upto):
            while issued[0] < min(upto, len(plan)):
                c = issued[0]
                if before[c] is not None:
                    eng.wait_ge(sem(plan[before[c]][1]), plan[before[c]][2])
                for kt, at, src in plan[c][0]:
                    n = src.shape[2]
                    eng.dma_start(wslot(c, kt)[:, :, at:at + n], src).then_inc(sem(f"ring{plan[c][3]}"), 16)
                issued[0] += 1

        def have_weights(eng, c):
            eng.wait_ge(sem(f"ring{plan[c][3]}"), landed[c])

        def ada_at(c):
            return c if c < 4 else CH_A + c - 4

        def pe_ada(pe, c, bank):
            have_weights(pe, ada_at(c))
            for k in range(KD):
                mm = pe.matmul(PS[bank][0:2, :], cs[:, k, :], wslot(ada_at(c))[:, k, :], start=(k == 0), stop=(k == 7))
            mm.then_inc(sem("ada_done"), 1)
            pe.wait_ge(sem("ada_row"), c + 1)
            for n in range(4):
                mm = pe.transpose(PS[bank][:, 2 * n:2 * n + 2], adar[:, c % 2, n * P:(n + 1) * P], ident[0:2, 0:2])
            mm.then_inc(sem("ada_turned"), 1)

        def act_ada(act, c, bank):
            act.wait_ge(sem("ada_done"), c + 1)
            act.activation(adar[:, c % 2, :], PS[bank][0:2, :], ACT.Copy).then_inc(sem("ada_row"), 1)

        def dve_ada(dve, c, bank):
            dve.wait_ge(sem("ada_turned"), c + 1)
            dve.tensor_tensor(modT[:, 4 * c:4 * c + 4, :], PS[bank][:, 0:8].rearrange("p (n s) -> p n s", s=2),
                              bc(par[:, PC_BADA + 4 * c:PC_BADA + 4 * c + 4].unsqueeze(2), [P, 4, 2]),
                              ALU.add).then_inc(sem("mod_in"), 1)

        def dve_gain(dve, n, pc):
            return dve.scalar_tensor_tensor(gain[:, n], modT[:, 24 * n + 8:24 * n + 16, :], 1.0,
                                            bc(par[:, pc:pc + 8].unsqueeze(2), [P, KD, 2]), ALU.add, ALU.mult)

        def pe_mean_square(pe, n):
            for k in range(KD):
                pe.wait_ge(sem("squares"), 8 * n + k + 1)
                pe.matmul(PS[6][:, 0:LAT], meanw[:], sq[:, k % 2, 0:LAT], start=(k == 0), stop=(k == 7))
                pe.matmul(PS[7][:, 0:CTX], meanw[:], sq[:, k % 2, LAT:TOK], start=(k == 0),
                          stop=(k == 7)).then_inc(sem("squares_summed"), 1)

        def act_square(act, n, k):
            if k >= 2:
                act.wait_ge(sem("squares_summed"), 8 * n + k - 1)
            act.activation(sq[:, k % 2, :], xT[:, k, :], ACT.Square).then_inc(sem("squares"), 1)

        def dve_inverse_mean(dve, v, n, tmp):
            dve.wait_ge(sem("squares_summed"), 8 * n + 8)
            v(dve.tensor_scalar(tmp[:, 0:LAT], PS[6][:, 0:LAT], EPS, None, ALU.add))
            v(dve.tensor_scalar(tmp[:, LAT:TOK], PS[7][:, 0:CTX], EPS, None, ALU.add))
            dve.reciprocal(tmp[:], tmp[:]).then_inc(sem("inverse_mean"), 1)

        def act_rms(act, n, tmp):
            act.wait_ge(sem("inverse_mean"), n + 1)
            act.activation(rsb[:], tmp[:], ACT.Sqrt).then_inc(sem("rms"), 1)

        def dve_normalise(dve, n):
            dve.wait_ge(sem("rms"), n + 1)
            for k in range(KD):
                if k >= 2:
                    dve.wait_ge(sem("modulated"), 8 * n + k - 1)
                dve.tensor_tensor(sq[:, k % 2, :], xT[:, k, :], rsb[:], ALU.mult).then_inc(sem("normalised"), 1)

        def act_modulate(act, n, dst):
            for k in range(KD):
                act.wait_ge(sem("normalised"), 8 * n + k + 1)
                if k == 0:
                    act.wait_ge(sem("gain_ready"), n + 1)
                act.activation(dst[:, k, 0:LAT], sq[:, k % 2, 0:LAT], ACT.Identity,
                               scale=gain[:, n, k, 0:1], bias=modT[:, 24 * n + k, 0:1])
                act.activation(dst[:, k, LAT:TOK], sq[:, k % 2, LAT:TOK], ACT.Identity,
                               scale=gain[:, n, k, 1:2],
                               bias=modT[:, 24 * n + k, 1:2]).then_inc(sem("modulated"), 1)

        s5 = ctx.enter_context(ExitStack())
        s5p = sb("s5p", [P, 5, GN], F32, s5)
        s5bc = sb("s5bc", [P, 4, GN, GC], F32, s5)
        s5d = sb("s5d", [GC, GN], F32, s5)
        bb = sb("bb", [P, 2, GN, GC], F32, s5)
        pwc = sb("pwc", [P, 2, L + 1, GN], F32, s5)
        pwd = sb("pwd", [P, 2, L, GN], F32, s5)
        ph = sb("ph", [P, 2, GN], F32, s5)
        rho = sb("rho", [P, GN], F32, s5)
        U = sb("U", [P, GN, J], F32, s5)
        CA = sb("CA", [P, 2, QG, L + 1, GC], F32, s5)
        wg = sb("wg", [P, KD, 16], F32, s5)
        gbias = sb("gbias", [16, 1], F32, s5)
        cs = sb("cs", [P, KD, 2], F32, s5)
        adar = sb("adar", [2, 2, 512], F32, s5)
        zC = sb("zC", [J, L, SW], F32, s5)

        with ExitStack() as st:
            pw = sb("pw", [P, 2, L + 1, GN], F32, st)
            posT = sb("posT", [P, KD, LAT], F32, st)
            t5 = sb("t5", [P, 12, GN], F32, st)
            tmp = sb("tmp", [P, TOK], F32, st)
            tp = sb("tp", [P, 4, 4, GN], F32, st)
            tb = sb("tb", [P, 2, GN, GC], F32, st)
            zero = sb("zero", [P, D], F32, st)
            block = st.enter_context(nc.Block())

            @block.sync
            def _(sp):
                sp.dma_start(par[:], ar["par"]).then_inc(sem("par_in"), 16)
                sp.dma_start(s5p[:], ar["s5p"]).then_inc(sem("s5p_in"), 16)
                load_weights(sp, 1)
                sp.dma_start(consts[:], ar["consts"]).then_inc(sem("consts_in"), 16)
                load_weights(sp, 2)
                sp.dma_start(xT[:], ar["xT"]).then_inc(sem("x_in"), 16)
                sp.dma_start(posT[:], ar["posT"]).then_inc(sem("x_in"), 16)
                load_weights(sp, 3)
                sp.dma_start(s5bc[:], ar["s5bc"]).then_inc(sem("s5bc_in"), 16)
                load_weights(sp, 4)
                sp.dma_start(s5d[:], ar["s5d"]).then_inc(sem("small_in"), 16)
                sp.dma_start(gpar[:], ar["gpar"]).then_inc(sem("small_in"), 16)
                sp.dma_start(gbias[:], ar["gbias"]).then_inc(sem("small_in"), 16)
                sp.dma_start(wg[:], w_in[:, :, C_G:C_G + 16]).then_inc(sem("small_in"), 16)
                load_weights(sp, CH_U + 1)
                sp.wait_ge(sem("small_in"), 64)

            @block.gpsimd
            def _(pool):
                pool.memset(meanw[:], 1.0 / D).then_inc(sem("meanw_set"), 1)
                pool.memset(zero[:], 0.0).then_inc(sem("zero_set"), 1)
                p = chain(pool, "pool")
                pool.wait_ge(sem("s5bc_in"), 16)
                pool.wait_ge(sem("b_factor"), 1)
                wr = bc(t5[:, 7, :].unsqueeze(2), [P, GN, GC])
                wi = bc(t5[:, 8, :].unsqueeze(2), [P, GN, GC])
                pool.tensor_tensor(tb[:, 0], s5bc[:, 0], wr, ALU.mult)
                p(pool.tensor_tensor(tb[:, 1], s5bc[:, 1], wi, ALU.mult))
                p(pool.tensor_tensor(bb[:, 0], tb[:, 0], tb[:, 1], ALU.subtract))
                pool.tensor_tensor(tb[:, 0], s5bc[:, 0], wi, ALU.mult)
                p(pool.tensor_tensor(tb[:, 1], s5bc[:, 1], wr, ALU.mult))
                p(pool.tensor_tensor(bb[:, 1], tb[:, 0], tb[:, 1], ALU.add))
                pool.wait_ge(sem("zero_set"), 1)
                for t in range(NT):
                    pool.dma_start(ar["moe"][t * P:(t + 1) * P, :], zero[:]).then_inc(sem("moe_zero"), 16)
                pool.wait_ge(sem("moe_zero"), 16 * NT)

            @block.scalar
            def _(act):
                a = chain(act, "act")
                act.wait_ge(sem("par_in"), 16)
                act.activation(cs[:].rearrange("p k s -> p (k s)"), par[:, PC_C:PC_C + 16],
                               ACT.Silu).then_inc(sem("c_silu"), 1)
                act.wait_ge(sem("s5p_in"), 16)
                a(act.activation(t5[:, 0, :], s5p[:, 2, :], ACT.Exp))
                act.wait_ge(sem("s5_z"), 1)
                a(act.activation(t5[:, 3, :], t5[:, 1, :], ACT.Exp))
                act.activation(rho[:], t5[:, 1, :], ACT.Exp, scale=float(L)).then_inc(sem("s5_mag"), 1)
                act.wait_ge(sem("s5_angle"), 1)
                a(act.activation(t5[:, 4, :], t5[:, 2, :], ACT.Sin))
                act.activation(t5[:, 5, :], t5[:, 2, :], ACT.Sin, scale=0.5).then_inc(sem("s5_sin"), 1)
                act_ada(act, 0, 0)
                act_ada(act, 1, 1)
                for k in range(KD):
                    act.wait_ge(sem("x_pos"), k + 1)
                    act_square(act, 0, k)
                act_rms(act, 0, tmp)
                act_ada(act, 2, 0)
                act_ada(act, 3, 1)
                act_modulate(act, 0, hT)

            @block.tensor
            def _(pe):
                pe.wait_ge(sem("c_silu"), 1)
                pe.wait_ge(sem("consts_in"), 16)
                pe_ada(pe, 0, 0)
                pe_ada(pe, 1, 1)
                pe.wait_ge(sem("meanw_set"), 1)
                pe_mean_square(pe, 0)
                for c in (2, 3):
                    pe.wait_ge(sem("mod_in"), c - 1)
                    pe_ada(pe, c, c % 2)

            @block.vector
            def _(dve):
                v = chain(dve, "dve")
                dve.wait_ge(sem("s5p_in"), 16)
                dve.wait_ge(sem("order_act"), 1)
                are, aim = s5p[:, 0, :], s5p[:, 1, :]
                v(dve.tensor_tensor(t5[:, 6, :], aim, t5[:, 0, :], ALU.mult))
                dve.tensor_tensor(t5[:, 1, :], are, t5[:, 0, :], ALU.mult).then_inc(sem("s5_z"), 1)
                MAGIC = 1.5 * 2.0 ** 23
                v(dve.tensor_scalar(t5[:, 7, :], t5[:, 6, :], float(1 / (2 * np.pi)), MAGIC, ALU.mult, ALU.add))
                v(dve.tensor_scalar(t5[:, 7, :], t5[:, 7, :], MAGIC, None, ALU.subtract))
                c1 = 6.28125
                c2 = float(np.float32(2 * np.pi - c1))
                c3 = float(np.float32(2 * np.pi - c1 - float(c2)))
                for cc in (c1, c2, c3):
                    v(dve.scalar_tensor_tensor(t5[:, 6, :], t5[:, 7, :], -cc, t5[:, 6, :], ALU.mult, ALU.add))
                dve.tensor_scalar(t5[:, 2, :], t5[:, 6, :], 3.1415925, -3.1415925, ALU.min,
                                  ALU.max).then_inc(sem("s5_angle"), 1)
                dve.wait_ge(sem("s5_mag"), 1)
                dve.wait_ge(sem("s5_sin"), 1)
                v(dve.tensor_tensor(t5[:, 7, :], t5[:, 5, :], t5[:, 5, :], ALU.mult))
                v(dve.tensor_scalar(ph[:, 0, :], t5[:, 7, :], -2.0, 1.0, ALU.mult, ALU.add))
                v(dve.tensor_copy(ph[:, 1, :], t5[:, 4, :]))
                v(dve.tensor_tensor(pw[:, 0, 1, :], t5[:, 3, :], ph[:, 0, :], ALU.mult))
                v(dve.tensor_tensor(pw[:, 1, 1, :], t5[:, 3, :], ph[:, 1, :], ALU.mult))
                v(dve.memset(pw[:, 0, 0, :], 1.0))
                v(dve.memset(pw[:, 1, 0, :], 0.0))

                def cmul(dr, di, ar_, ai_, br_, bi_, t):
                    dve.tensor_tensor(t[0], ar_, br_, ALU.mult)
                    dve.tensor_tensor(t[1], ai_, bi_, ALU.mult)
                    dve.tensor_tensor(t[2], ar_, bi_, ALU.mult)
                    v(dve.tensor_tensor(t[3], ai_, br_, ALU.mult))
                    dve.tensor_tensor(dr, t[0], t[1], ALU.subtract)
                    v(dve.tensor_tensor(di, t[2], t[3], ALU.add))

                def t4(n):
                    return [tp[:, x, 0:n, :] for x in range(4)]

                for _ in range(3):
                    cmul(ph[:, 0, :], ph[:, 1, :], ph[:, 0, :], ph[:, 1, :], ph[:, 0, :], ph[:, 1, :],
                         [tp[:, x, 0, :] for x in range(4)])
                for m in (1, 2, 4):
                    cmul(pw[:, 0, m + 1:2 * m + 1, :], pw[:, 1, m + 1:2 * m + 1, :],
                         pw[:, 0, 1:m + 1, :], pw[:, 1, 1:m + 1, :],
                         bc(pw[:, 0, m:m + 1, :], [P, m, GN]), bc(pw[:, 1, m:m + 1, :], [P, m, GN]), t4(m))
                F, B = slice(0, SP_), slice(SP_, P)
                for r in range(2):
                    v(dve.tensor_copy(pwc[F, r, :, :], pw[F, r, :, :]))
                    v(dve.tensor_copy(pwc[B, r, :, :], pw[B, r, ::-1, :]))
                    v(dve.tensor_copy(pwd[F, r, :, :], pw[F, r, L - 1::-1, :]))
                    v(dve.tensor_copy(pwd[B, r, :, :], pw[B, r, 0:L, :]))
                v(dve.tensor_tensor(t5[:, 8, :], are, are, ALU.mult))
                v(dve.tensor_tensor(t5[:, 9, :], aim, aim, ALU.mult))
                v(dve.tensor_tensor(t5[:, 8, :], t5[:, 8, :], t5[:, 9, :], ALU.add))
                v(dve.reciprocal(t5[:, 8, :], t5[:, 8, :]))
                v(dve.tensor_tensor(t5[:, 9, :], are, t5[:, 8, :], ALU.mult))
                v(dve.scalar_tensor_tensor(t5[:, 10, :], aim, -1.0, t5[:, 8, :], ALU.mult, ALU.mult))
                v(dve.tensor_scalar(t5[:, 11, :], pw[:, 0, 1, :], 1.0, None, ALU.subtract))
                cmul(t5[:, 6, :], t5[:, 2, :], t5[:, 11, :], pw[:, 1, 1, :], t5[:, 9, :], t5[:, 10, :],
                     [tp[:, x, 0, :] for x in range(4)])
                dve.tensor_copy(t5[:, 7, :], t5[:, 6, :])
                dve.tensor_copy(t5[:, 8, :], t5[:, 2, :]).then_inc(sem("b_factor"), 1)
                dve_ada(dve, 0, 0)
                dve_ada(dve, 1, 1)
                dve.wait_ge(sem("x_in"), 32)
                for k in range(KD):
                    dve.tensor_tensor(xT[:, k, 0:LAT], xT[:, k, 0:LAT], posT[:, k], ALU.add).then_inc(sem("x_pos"), 1)
                dve_inverse_mean(dve, v, 0, tmp)
                dve_ada(dve, 2, 0)
                dve_ada(dve, 3, 1)
                dve.wait_ge(sem("mod_in"), 4)
                dve_gain(dve, 0, PC_NMIX).then_inc(sem("gain_ready"), 1)
                dve_normalise(dve, 0)

        CB = W[:, 0, 0:2048].rearrange("p (r g x) -> p r g x", r=2, g=QG)
        CT = W[:, 0, 2048:4096].rearrange("p (r g x) -> p r g x", r=2, g=QG)
        t8 = hbT[:].rearrange("p a b -> p (a b)")[:, 0:2 * QG * (L + 1) * GC].rearrange("p (x g m) -> p x g m", x=2, g=QG)

        def pool_coefficients(pool, q):
            p = chain(pool, "pool")
            g = slice(QG * q, QG * q + QG)
            s = [P, QG, L, GC]
            if q:
                pool.wait_ge(sem("cb_turned"), 4 * q)
            pr, pi = (bc(pwd[:, r, :, g].rearrange("p i g -> p g i").unsqueeze(3), s) for r in range(2))
            br, bi = (bc(bb[:, r, g, :].unsqueeze(2), s) for r in range(2))
            ta, tb_ = (t8[:, x, :, 0:P].rearrange("p g (i c) -> p g i c", c=GC) for x in range(2))
            cr, ci = (CB[:, r].rearrange("p g (i c) -> p g i c", c=GC) for r in range(2))
            pool.tensor_tensor(ta, pr, br, ALU.mult)
            p(pool.tensor_tensor(tb_, pi, bi, ALU.mult))
            p(pool.tensor_tensor(cr, ta, tb_, ALU.subtract))
            pool.tensor_tensor(ta, pr, bi, ALU.mult)
            p(pool.tensor_tensor(tb_, pi, br, ALU.mult))
            pool.tensor_tensor(ci, ta, tb_, ALU.add).then_inc(sem("cb_ready"), 1)
            pool.wait_ge(sem("cb_ready"), q + 1)
            s = [P, QG, L + 1, GC]
            pr, pi = (bc(pwc[:, r, :, g].rearrange("p i g -> p g i").unsqueeze(3), s) for r in range(2))
            br, bi = (bc(s5bc[:, 2 + r, g, :].unsqueeze(2), s) for r in range(2))
            ta, tb_ = (t8[:, x].rearrange("p g (i c) -> p g i c", c=GC) for x in range(2))
            pool.tensor_tensor(ta, pr, br, ALU.mult)
            p(pool.tensor_tensor(tb_, pi, bi, ALU.mult))
            if q:
                pool.wait_ge(sem("s5_lag_done"), 4 * q)
                pool.wait_ge(sem("cao_ready"), q)
            p(pool.tensor_tensor(CA[:, 0], ta, tb_, ALU.subtract))
            pool.tensor_tensor(ta, pr, bi, ALU.mult)
            p(pool.tensor_tensor(tb_, pi, br, ALU.mult))
            p(pool.tensor_tensor(CA[:, 1], ta, tb_, ALU.add))
            pool.tensor_scalar(CA[:, 1], CA[:, 1], -1.0, 1.0, ALU.mult, ALU.mult).then_inc(sem("ca_ready"), 1)
            pool.wait_ge(sem("ca_ready"), q + 1)

        with ExitStack() as st:
            g16 = sb("g16", [16, TOK], F32, st)
            G = W[0:H, 2, 0:4 * TOK].rearrange("h (g t) -> h g t", g=4)
            gt = W[0:H, 2, 4 * TOK:6 * TOK].rearrange("h (g t) -> h g t", g=2)
            lf = sb("lf", [H, 2, TOK], F32, st)
            cum = sb("cum", [H, 2, TOK], F32, st)
            R = zC[:].rearrange("p a b -> p (a b)")[0:H, 0:6 * TOK].rearrange("h (x t) -> h x t", x=6)
            uF = sq
            Mx = sb("Mx", [H, 2, TOK], F32, st)
            ones4 = sb("ones4", [H, TOK], F32, st)
            mrow = sb("mrow", [H, 2], F32, st)
            block = st.enter_context(nc.Block())

            @block.sync
            def _(sp):
                sp.wait_ge(sem("gates_copied"), 2)
                for g in range(4):
                    sp.dma_start(G[:, g, :], g16[H * g:H * g + H, :]).then_inc(sem("gates_turned"), 16)
                ud = ar["u"].rearrange("(m g c) (i j) -> m i c g j", m=4, c=GC, i=L)
                for m in range(4):
                    sp.wait_ge(sem("u_copied"), m + 1)
                    sp.dma_start(ar["u"][m * P:(m + 1) * P, :], uF[:, m % 2, :]).then_inc(sem(f"u_out{m % 2}"), 16)
                    sp.wait_ge(sem(f"u_out{m % 2}"), 16 * (m // 2 + 1))
                    for i in range(L):
                        sp.dma_start(U[GC * i:GC * i + GC, QG * m:QG * m + QG, :], ud[m, i]
                                     ).then_inc(sem(f"u_in{m}"), 16)
                load_weights(sp, CH_A + 1)
                sp.wait_ge(sem("m_ready"), 1)
                with nc.allow_non_contiguous_dma(reason="eight values"):
                    sp.dma_start(out["m"].rearrange("d h -> h d"), mrow[:]).then_inc(sem("m_out"), 16)
                sp.wait_ge(sem("m_out"), 16)

            @block.gpsimd
            def _(pool):
                pool_coefficients(pool, 0)

            @block.tensor
            def _(pe):
                for k in range(KD):
                    pe.matmul(PS[0][0:16, :], wg[:, k, :], hT[:, k, 0:LAT], start=(k == 0), stop=(k == 7))
                    mm = pe.matmul(PS[1][0:16, 0:CTX], wg[:, k, :], hT[:, k, LAT:TOK], start=(k == 0), stop=(k == 7))
                mm.then_inc(sem("gates_done"), 1)
                have_weights(pe, CH_U)
                for m in range(4):
                    if m >= 2:
                        pe.wait_ge(sem("u_copied"), m - 1)
                    for k in range(KD):
                        w = wslot(CH_U)[:, k, m * P:(m + 1) * P]
                        pe.matmul(PS[2 + m % 2][:, :], w, hT[:, k, 0:LAT], start=(k == 0), stop=(k == 7))
                        mm = pe.matmul(PS[4 + m % 2][:, 0:CTX], w, hT[:, k, LAT:TOK], start=(k == 0), stop=(k == 7))
                    mm.then_inc(sem("u_done"), 1)
                pe.wait_ge(sem("rows_ready"), 1)
                for t in range(NT):
                    for x in range(6):
                        if t < 4 or x not in (2, 3):
                            c = (t * 6 + x) * H
                            mm = pe.transpose(PS[6][:, c:c + H], R[:, x, t * P:(t + 1) * P], ident[0:H, 0:H])
                mm.then_inc(sem("rows_turned"), 1)

            @block.scalar
            def _(act):
                a = chain(act, "act")
                act.wait_ge(sem("gate_abs"), 1)
                a(act.activation(gt, gt, ACT.Exp, scale=-1.0))
                act.activation(gt, gt, ACT.Ln, bias=1.0).then_inc(sem("gate_ln"), 1)

                def out_u(m):
                    act.wait_ge(sem("u_done"), m + 1)
                    if m >= 2:
                        act.wait_ge(sem(f"u_out{m % 2}"), 16)
                    dst = uF[:, m % 2, :].rearrange("p (i j) -> p j i", i=L)
                    act.activation(dst[:, 0:JL, :], PS[2 + m % 2][:, :].rearrange("p (j i) -> p j i", i=L), ACT.Copy)
                    act.activation(dst[:, JL:J, :], PS[4 + m % 2][:, 0:CTX].rearrange("p (j i) -> p j i", i=L),
                                   ACT.Copy).then_inc(sem("u_copied"), 1)

                for m in range(3):
                    out_u(m)
                act.wait_ge(sem("m_ready"), 1)
                for d in range(2):
                    act.activation(R[:, 2 + d, 0:LAT], Mx[:, d, 0:LAT], ACT.Exp, scale=-1.0, bias=gpar[:, 4 + d:5 + d])
                    ins = act.activation(R[:, 4 + d, :], cum[:, d, :], ACT.Exp, scale=-1.0)
                ins.then_inc(sem("rows_ready"), 1)
                out_u(3)

            @block.vector
            def _(dve):
                v = chain(dve, "dve")
                dve.wait_ge(sem("gates_done"), 1)
                dve.tensor_scalar(g16[:, 0:LAT], PS[0][0:16, :], gbias[:, 0:1], None, ALU.add
                                  ).then_inc(sem("gates_copied"), 1)
                dve.tensor_scalar(g16[:, LAT:TOK], PS[1][0:16, 0:CTX], gbias[:, 0:1], None, ALU.add
                                  ).then_inc(sem("gates_copied"), 1)
                v(dve.memset(ones4[:], 1.0))
                dve.wait_ge(sem("gates_turned"), 64)
                x = G[:, 1:4:2, :]
                dve.scalar_tensor_tensor(gt, x, -1.0, x, ALU.mult, ALU.max).then_inc(sem("gate_abs"), 1)
                dve.wait_ge(sem("gate_ln"), 1)
                v(dve.scalar_tensor_tensor(lf[:], x, 0.0, gt, ALU.min, ALU.subtract))

                def part(tile, d, s):
                    ap = tile[:, d, 0:LAT] if s == 0 else tile[:, d, LAT:TOK]
                    return ap[:, ::-1] if d else ap

                for d in range(2):
                    for s in range(2):
                        n = LAT if s == 0 else CTX
                        v(dve.tensor_tensor_scan(part(cum, d, s), ones4[:, 0:n], part(lf, d, s), 0.0,
                                                 ALU.mult, ALU.add))
                v(dve.tensor_tensor(R[:, 0:2, :], G[:, 0:4:2, :], cum[:], ALU.subtract))
                for d in range(2):
                    for s in range(2):
                        v(dve.tensor_tensor_scan(part(Mx, d, s), part(R, d, s), part(R, d, s),
                                                 gpar[:, 4 + d:5 + d] if s == 0 else 0.0, ALU.max, ALU.max))
                v(dve.tensor_scalar(negM[:], Mx[:], -1.0, None, ALU.mult))
                v(dve.tensor_tensor(cum[:], cum[:], Mx[:], ALU.add))
                v(dve.tensor_copy(mrow[:, 0:1], cum[:, 0, TOK - 1:TOK]))
                dve.tensor_copy(mrow[:, 1:2], cum[:, 1, LAT:LAT + 1]).then_inc(sem("m_ready"), 1)
                dve.wait_ge(sem("rows_turned"), 1)
                c4 = PS[6][:, 0:NT * 24].rearrange("p (t x h) -> p t x h", t=NT, x=6)
                dve.tensor_copy(colT[:, 0:4], c4[:, 0:4])
                dve.tensor_copy(colT[:, 4, 0:2], c4[:, 4, 0:2])
                dve.tensor_copy(colT[:, 4, 4:6], c4[:, 4, 4:6])

        with ExitStack() as st:
            n3 = 2 * QG * NS_
            Et, V, Z = (W[:, 2, x * n3:(x + 1) * n3].rearrange("p (r g n) -> p r g n", r=2, g=QG) for x in range(3))
            Xp = sq[:].rearrange("p a b -> p (a b)").rearrange("p (r g j) -> p r g j", r=2, g=QG)
            CAo = sb("CAo", [P, 2, QG, P], F32, st)
            bbz = sb("bbz", [P, 2, 2, QG, GC], F32, st)
            Kt = sb("Kt", [GC, QG, (2 * L - 1) * GC], F32, st)
            kd = sb("kd", [GC, QG, GC], F32, st)
            T = sb("T", [P, QG, P], F32, st)
            rt = sb("rt", [P, QG, NS_], F32, st)
            tz = sb("tz", [P, 4, QG, NS_], F32, st)
            xfin = sb("xfin", [P, 2, GN], F32, st)
            F, B = slice(0, SP_), slice(SP_, P)
            block = st.enter_context(nc.Block())

            @block.sync
            def _(sp):
                for q in range(NQ):
                    sp.wait_ge(sem("lags_ready"), q + 1)
                    if q:
                        sp.wait_ge(sem("s5_y_done"), 2 * q)
                    for i in range(L):
                        sp.dma_start(T[GC * i:GC * i + GC, :, :],
                                     Kt[:, :, (L - 1 - i) * GC:(2 * L - 1 - i) * GC]).then_inc(sem("toeplitz_in"), 16)
                    load_weights(sp, CH_A + 2 * q + 3)
                sp.wait_ge(sem("xfin_ready"), NQ)
                for r in range(2):
                    sp.dma_start(out["s5"][r], xfin[:, r, :]).then_inc(sem("s5_out"), 16)
                sp.wait_ge(sem("s5_out"), 32)

            @block.gpsimd
            def _(pool):
                for q in range(1, NQ):
                    pool_coefficients(pool, q)

            @block.tensor
            def _(pe):
                def additions(q):
                    pe.wait_ge(sem("cb_ready"), q + 1)
                    pe.wait_ge(sem(f"u_in{q}"), 16 * L)
                    if q:
                        pe.wait_ge(sem("v_copied"), 4 * q)
                    for r in range(2):
                        for g in range(QG):
                            mm = pe.transpose(PS[2 + 2 * r + g // 4][:, (g % 4) * P:(g % 4 + 1) * P], CB[:, r, g, :],
                                              ident)
                            if g % 4 == 3:
                                mm.then_inc(sem("cb_turned"), 1)
                    for r in range(2):
                        for g in range(QG):
                            if g % 4 == 0:
                                pe.wait_ge(sem("ct_copied"), 4 * q + 2 * r + g // 4 + 1)
                            mm = pe.matmul(PS[2 + 2 * r + g // 4][:, (g % 4) * J:(g % 4 + 1) * J], CT[:, r, g, :],
                                           U[:, QG * q + g, :], start=True, stop=True)
                            if g % 4 == 3:
                                mm.then_inc(sem("s5_v_done"), 1)

                def lags(q):
                    pe.wait_ge(sem("ca_ready"), q + 1)
                    pe.wait_ge(sem("bbz_ready"), q + 1)
                    if q:
                        pe.wait_ge(sem("mod_in"), 4 + 2 * q)
                    FW, BW = (L - 1) * GC, 0
                    for g in range(QG):
                        n = 4 * q + g // 2
                        bank = 6 + n % 2
                        if g % 2 == 0 and n >= 2:
                            pe.wait_ge(sem("lags_copied"), n - 1)
                        o = (g % 2) * (2 * L - 1) * GC
                        k = 0
                        for d, (at, m0) in enumerate(((FW, 0), (BW, 1))):
                            for r in range(2):
                                mm = pe.matmul(PS[bank][0:GC, o + at:o + at + P], bbz[:, d, r, g, :],
                                               CA[:, r, g, m0:m0 + L, :], start=(k == 0 and g % 2 == 0), stop=(k == 3),
                                               skip_group_check=True)
                                k += 1
                        if g % 2 == 1:
                            mm.then_inc(sem("s5_lag_done"), 1)

                def outputs(q):
                    pe.wait_ge(sem("xp_copied"), q + 1)
                    pe.wait_ge(sem("cao_ready"), q + 1)
                    pe.wait_ge(sem("toeplitz_in"), 128 * (q + 1))
                    if q:
                        pe.wait_ge(sem("z_copied"), 2 * q)
                    for g in range(QG):
                        dst = PS[g // 4][0:J, (g % 4) * P:(g % 4 + 1) * P]
                        pe.matmul(dst, U[:, QG * q + g, :], T[:, g, :], start=True, stop=False)
                        for r in range(2):
                            mm = pe.matmul(dst, Xp[:, r, g, :], CAo[:, r, g, :], start=False, stop=(r == 1))
                        if g % 4 == 3:
                            mm.then_inc(sem("s5_y_done"), 1)

                additions(0)
                for q in range(NQ):
                    lags(q)
                    if q + 1 < NQ:
                        additions(q + 1)
                    pe.wait_ge(sem("lags_copied"), 4 * q + 4)
                    pe_ada(pe, 4 + 2 * q, 7)
                    outputs(q)
                    pe.wait_ge(sem("mod_in"), 5 + 2 * q)
                    pe_ada(pe, 5 + 2 * q, 7)

            @block.scalar
            def _(act):
                def turned_coefficients(q):
                    for b in range(4):
                        act.wait_ge(sem("cb_turned"), 4 * q + b + 1)
                        act.activation(CT[:, b // 2, 4 * (b % 2):4 * (b % 2) + 4, :].rearrange("p g j -> p (g j)"),
                                       PS[2 + b][:], ACT.Copy).then_inc(sem("ct_copied"), 1)

                def additions(q):
                    if q:
                        act.wait_ge(sem("xp_copied"), q)
                    for r in range(2):
                        for b in range(2):
                            act.wait_ge(sem("s5_v_done"), 4 * q + 2 * r + b + 1)
                            src = PS[2 + 2 * r + b][:, 0:4 * J].rearrange("p (g j) -> p g j", g=4)
                            gg = slice(4 * b, 4 * b + 4)
                            act.activation(V[F, r, gg, 1:JL + 1], src[F, :, 0:JL], ACT.Copy)
                            act.activation(V[F, r, gg, JL + 2:NS_], src[F, :, JL:J], ACT.Copy)
                            act.activation(V[B, r, gg, 1:JL + 1], src[B, :, 0:JL][:, :, ::-1], ACT.Copy)
                            act.activation(V[B, r, gg, JL + 2:NS_], src[B, :, JL:J][:, :, ::-1],
                                           ACT.Copy).then_inc(sem("v_copied"), 1)

                turned_coefficients(0)
                additions(0)
                for q in range(NQ):
                    for b in range(4):
                        act.wait_ge(sem("s5_lag_done"), 4 * q + b + 1)
                        if q and b == 0:
                            act.wait_ge(sem("toeplitz_in"), 128 * q)
                        act.activation(Kt[:, 2 * b:2 * b + 2, :].rearrange("p g x -> p (g x)"),
                                       PS[6 + b % 2][0:GC, 0:2 * (2 * L - 1) * GC],
                                       ACT.Copy).then_inc(sem("lags_copied"), 1)
                    act.wait_ge(sem("ca_ready"), q + 1)
                    if q:
                        act.wait_ge(sem("s5_y_done"), 2 * q)
                    for r in range(2):
                        dst = CAo[:, r].rearrange("p g (i c) -> p g i c", c=GC)
                        act.activation(dst[F], CA[F, r, :, 1:L + 1, :], ACT.Copy)
                        ins = act.activation(dst[B], CA[B, r, :, 0:L, :], ACT.Copy)
                    ins.then_inc(sem("cao_ready"), 1)
                    if q + 1 < NQ:
                        turned_coefficients(q + 1)
                    act_ada(act, 4 + 2 * q, 7)
                    if q + 1 < NQ:
                        additions(q + 1)
                    for b in range(2):
                        act.wait_ge(sem("s5_y_done"), 2 * q + b + 1)
                        c0 = (QG * q + 4 * b) * GC
                        act.activation(zC[:, :, c0:c0 + 4 * GC].rearrange("p i (g c) -> p g i c", c=GC),
                                       PS[b][0:J, :].rearrange("p (g i c) -> p g i c", g=4, i=L),
                                       ACT.Copy).then_inc(sem("z_copied"), 1)
                    act_ada(act, 5 + 2 * q, 7)

            @block.vector
            def _(dve):
                v = chain(dve, "dve")
                cx = slice(JL + 1, NS_)
                v(dve.memset(bbz[:], 0.0))
                for q in range(NQ):
                    g = slice(QG * q, QG * q + QG)
                    if q:
                        dve.wait_ge(sem("s5_lag_done"), 4 * q)
                    for d, own in enumerate((F, B)):
                        for r in range(2):
                            ins = dve.tensor_copy(bbz[own, d, r], bb[own, r, g, :])
                    ins.then_inc(sem("bbz_ready"), 1)
                    v(dve.memset(Et[:, 0, :, 0:1], 1.0))
                    v(dve.memset(Et[:, 1, :, 0:1], 0.0))
                    for r in range(2):
                        v(dve.tensor_copy(Et[:, r, :, 1:2], ph[:, r, g].unsqueeze(2)))
                    m = 1
                    while m < JL:
                        x, y = slice(1, m + 1), slice(m + 1, 2 * m + 1)
                        er, ei = (bc(Et[:, r, :, m:m + 1], [P, QG, m]) for r in range(2))
                        dve.tensor_tensor(tz[:, 0, :, 0:m], Et[:, 0, :, x], er, ALU.mult)
                        dve.tensor_tensor(tz[:, 1, :, 0:m], Et[:, 1, :, x], ei, ALU.mult)
                        dve.tensor_tensor(tz[:, 2, :, 0:m], Et[:, 0, :, x], ei, ALU.mult)
                        v(dve.tensor_tensor(tz[:, 3, :, 0:m], Et[:, 1, :, x], er, ALU.mult))
                        dve.tensor_tensor(Et[:, 0, :, y], tz[:, 0, :, 0:m], tz[:, 1, :, 0:m], ALU.subtract)
                        v(dve.tensor_tensor(Et[:, 1, :, y], tz[:, 2, :, 0:m], tz[:, 3, :, 0:m], ALU.add))
                        m *= 2
                    v(dve.tensor_copy(Et[:, :, :, cx], Et[:, :, :, 0:JC + 1]))
                    v(dve.tensor_copy(rt[:], bc(rho[:, g].unsqueeze(2), [P, QG, NS_])))
                    v(dve.memset(rt[:, :, 0:1], 0.0))
                    v(dve.memset(rt[:, :, JL + 1:JL + 2], 0.0))
                    for r in range(2):
                        v(dve.tensor_copy(V[:, r, :, 0:1], s5p[:, 3 + r, g].unsqueeze(2)))
                        v(dve.memset(V[:, r, :, JL + 1:JL + 2], 0.0))
                    v(dve.tensor_tensor(kd[:], bc(s5d[:, g].unsqueeze(2), [GC, QG, GC]),
                                        bc(ident[0:GC, 0:GC].unsqueeze(1), [GC, QG, GC]), ALU.mult))
                    if q:
                        dve_ada(dve, 3 + 2 * q, 7)
                    dve.wait_ge(sem("lags_copied"), 4 * q + 4)
                    k0 = Kt[:, :, (L - 1) * GC:L * GC]
                    dve.tensor_tensor(k0, k0, kd[:], ALU.add).then_inc(sem("lags_ready"), 1)
                    dve.wait_ge(sem("v_copied"), 4 * q + 4)
                    dve.tensor_tensor(tz[:, 0], V[:, 0], Et[:, 0], ALU.mult)
                    dve.tensor_tensor(tz[:, 1], V[:, 1], Et[:, 1], ALU.mult)
                    dve.tensor_tensor(tz[:, 2], V[:, 1], Et[:, 0], ALU.mult)
                    v(dve.tensor_tensor(tz[:, 3], V[:, 0], Et[:, 1], ALU.mult))
                    dve.tensor_tensor(V[:, 0], tz[:, 0], tz[:, 1], ALU.add)
                    v(dve.tensor_tensor(V[:, 1], tz[:, 2], tz[:, 3], ALU.subtract))
                    for r in range(2):
                        v(dve.tensor_tensor_scan(Z[:, r].rearrange("p g n -> p (g n)"),
                                                 rt[:].rearrange("p g n -> p (g n)"),
                                                 V[:, r].rearrange("p g n -> p (g n)"), 0.0, ALU.mult, ALU.add))
                    dve.tensor_tensor(tz[:, 0], Z[:, 0], Et[:, 0], ALU.mult)
                    dve.tensor_tensor(tz[:, 1], Z[:, 1], Et[:, 1], ALU.mult)
                    dve.tensor_tensor(tz[:, 2], Z[:, 1], Et[:, 0], ALU.mult)
                    v(dve.tensor_tensor(tz[:, 3], Z[:, 0], Et[:, 1], ALU.mult))
                    dve.tensor_tensor(V[:, 0], tz[:, 0], tz[:, 1], ALU.subtract)
                    v(dve.tensor_tensor(V[:, 1], tz[:, 2], tz[:, 3], ALU.add))
                    dve.tensor_copy(xfin[:, :, g], V[:, :, :, NS_ - 1]).then_inc(sem("xfin_ready"), 1)
                    if q:
                        dve.wait_ge(sem("s5_y_done"), 2 * q)
                    for r in range(2):
                        dve.tensor_copy(Xp[F, r, :, 0:JL], V[F, r, :, 0:JL])
                        dve.tensor_copy(Xp[F, r, :, JL:J], V[F, r, :, JL + 1:NS_ - 1])
                        dve.tensor_copy(Xp[B, r, :, 0:JL], V[B, r, :, 0:JL][:, :, ::-1])
                        ins = dve.tensor_copy(Xp[B, r, :, JL:J], V[B, r, :, JL + 1:NS_ - 1][:, :, ::-1])
                    ins.then_inc(sem("xp_copied"), 1)
                    dve_ada(dve, 4 + 2 * q, 7)
                dve_ada(dve, 11, 7)

        with ExitStack() as st:
            zT = sb("zT", [P, 4, TOK], F32, st)
            gz = sb("gz", [P, 4, TOK], F32, st)
            sg = sb("sg", [P, 2, TOK], F32, st)
            wgl = sb("wgl", [P, 4, SW], F32, st)
            block = st.enter_context(nc.Block())

            @block.sync
            def _(sp):
                sp.dma_start(wgl[:], w_glu).then_inc(sem("wglu_in"), 16)
                load_weights(sp, CH_H + NSLOT)

            @block.tensor
            def _(pe):
                for b in range(8):
                    if b >= 4:
                        pe.wait_ge(sem("z_in"), b - 3)
                    for i in range(4):
                        mm = pe.transpose(PS[b % 4][:, i * J:(i + 1) * J],
                                          zC[:, 4 * (b % 2) + i, (b // 2) * P:(b // 2 + 1) * P], ident[0:J, 0:J])
                    mm.then_inc(sem("z_turned"), 1)
                pe.wait_ge(sem("wglu_in"), 16)
                pe.wait_ge(sem("z_in"), 8)
                for m in range(4):
                    if m >= 2:
                        pe.wait_ge(sem("glu_sig"), m - 1)
                    for k in range(4):
                        w = wgl[:, k, m * P:(m + 1) * P]
                        pe.matmul(PS[4 + m % 2][:, :], w, zT[:, k, 0:LAT], start=(k == 0), stop=(k == 3))
                        mm = pe.matmul(PS[6 + m % 2][:, 0:CTX], w, zT[:, k, LAT:TOK], start=(k == 0), stop=(k == 3))
                    mm.then_inc(sem("glu_done"), 1)

            @block.scalar
            def _(act):
                act.wait_ge(sem("z_in"), 8)
                for m in range(4):
                    act.activation(gz[:, m, :], zT[:, m, :], ACT.Gelu_apprx_tanh).then_inc(sem("gelu"), 1)
                for m in range(4):
                    act.wait_ge(sem("glu_done"), m + 1)
                    if m >= 2:
                        act.wait_ge(sem("hb_ready"), m - 1)
                    b = par[:, PC_BGLU + m:PC_BGLU + m + 1]
                    act.activation(sg[:, m % 2, 0:LAT], PS[4 + m % 2][:, :], ACT.Sigmoid, bias=b)
                    act.activation(sg[:, m % 2, LAT:TOK], PS[6 + m % 2][:, 0:CTX], ACT.Sigmoid,
                                   bias=b).then_inc(sem("glu_sig"), 1)

            @block.vector
            def _(dve):
                for b in range(8):
                    dve.wait_ge(sem("z_turned"), b + 1)
                    dst = zT[:, b // 2, :].rearrange("p (j i) -> p i j", i=L)[:, 4 * (b % 2):4 * (b % 2) + 4, :]
                    dve.tensor_copy(dst, PS[b % 4][:, 0:4 * J].rearrange("p (i j) -> p i j", i=4)
                                    ).then_inc(sem("z_in"), 1)
                dve.wait_ge(sem("gelu"), 4)
                for m in range(4):
                    dve.wait_ge(sem("glu_sig"), m + 1)
                    dve.tensor_tensor(hbT[:, m, :], gz[:, m, :], sg[:, m % 2, :], ALU.mult).then_inc(sem("hb_ready"), 1)

        s5.close()

        haT = sb("haT", [P, KD, TOK], F32, acts)
        with ExitStack() as st:
            qk = sb("qk", [P, 2, 4, TOK], F32, st)
            vt = sb("vt", [P, 2, NT, DH + 1], F32, st)
            og = sb("og", [P, 2, NT, DH], F32, st)
            PW = LAT * 5 // 2 + CTX
            Pm = sb("Pm", [P, 2, PW], F32, st)
            negMd = sq
            Qs = rsb[:, 0:2 * (DH + 1)].rearrange("p (b n) -> p b n", b=2)
            nd = sb("nd", [P, 2, DH + 1], F32, st)
            rr = sb("rr", [P, 2], F32, st)
            hacc = sb("hacc", [P, NT, DH], F32, st)
            junk = sb("junk", [P, DH], F32, st)
            ssq = sb("ssq", [P, NT], F32, st)
            rs5 = sb("rs5", [P, NT], F32, st)
            C0 = sb("C0", [P, 4, DH + 1], F32, st)
            wk = sb("wk", [P, 2], F32, st)
            kw = sb("kw", [P, 2, DH], F32, st)
            Co = sb("Co", [P, 4, DH + 1], F32, st)
            selH = sb("selH", [H, H, P], F32, st)
            block = st.enter_context(nc.Block())
            Cn = ar["Cn"].rearrange("d h (k p) n -> h d p k n", p=P)
            Cout = out["Cn"].rearrange("d h (k p) n -> h d p k n", p=P)
            OFF = {0: [0, 512, 896, 1152], 1: [0, 128, 384, 768]}

            @block.sync
            def _(sp):
                for h in range(H):
                    if h:
                        sp.wait_ge(sem("pv_done"), 10 * h)
                    for d in range(2):
                        sp.dma_start(C0[:, 2 * d:2 * d + 2, :], Cn[h, d]).then_inc(sem("c0_in"), 16)
                    load_weights(sp, CH_H + 2 * h + 4)
                load_weights(sp, CH_M + NSLOT)

            @block.gpsimd
            def _(pool):
                for h in range(H):
                    pool.wait_ge(sem("co_ready"), 4 * (h + 1))
                    for d in range(2):
                        pool.dma_start(Cout[h, d], Co[:, 2 * d:2 * d + 2, :]).then_inc(sem("c_out"), 16)
                pool.wait_ge(sem("c_out"), 32 * H)

            @block.tensor
            def _(pe):
                def proj_wait(u):
                    if u >= 2:
                        pe.wait_ge(sem("proj_copied"), u - 1 + (u - 2 + 5) // 9)

                def proj_qk(h):
                    c = CH_H + 2 * h
                    have_weights(pe, c)
                    for m in range(4):
                        u = 9 * h + m
                        proj_wait(u)
                        for k in range(KD):
                            w = wslot(c)[:, k, m * P:(m + 1) * P]
                            mm = pe.matmul(PS[u % 2][:, :], w, hT[:, k, 0:LAT], start=(k == 0), stop=(k == 7))
                        mm.then_inc(sem("qk_done"), 1)
                    for m in range(4):
                        for k in range(KD):
                            mm = pe.matmul(PS[2][:, m * P:(m + 1) * P], wslot(c)[:, k, m * P:(m + 1) * P],
                                           hT[:, k, LAT:TOK], start=(k == 0), stop=(k == 7))
                    mm.then_inc(sem("qk_done"), 1)

                def proj_vo(h):
                    c = CH_H + 2 * h + 1
                    have_weights(pe, c)
                    for t in range(NT):
                        u = 9 * h + 4 + t
                        proj_wait(u)
                        for k in range(KD):
                            mm = pe.matmul(PS[u % 2][:, :], hT[:, k, t * P:(t + 1) * P], wslot(c)[:, k, :],
                                           start=(k == 0), stop=(k == 7))
                        mm.then_inc(sem("vo_done"), 1)

                def scores(h):
                    b = h % 2
                    if h:
                        pe.wait_ge(sem("co_ready"), 4 * h)
                        pe.wait_ge(sem("ha_ready"), 3 * h)
                    else:
                        pe.wait_ge(sem("sel_ready"), 1)
                    for d in range(2):
                        pe.matmul(PS[3 + d][:, :], selH[:, h, :], negM[:, d, 0:LAT], start=True, stop=True)
                        mm = pe.matmul(PS[5][:, d * P:(d + 1) * P], selH[:, h, :], negM[:, d, LAT:TOK], start=True,
                                       stop=True)
                    mm.then_inc(sem("m_spread"), 1)
                    pe.wait_ge(sem("proj_copied"), 10 * h + 5)
                    for s in range(NT):
                        if s == 4:
                            pe.wait_ge(sem("negmd_ready"), h + 1)
                        if 2 <= s < 4:
                            pe.wait_ge(sem("p_ready"), NT * h + s - 1)
                        for k in range(2):
                            if s < 4:
                                mm = pe.matmul(PS[6 + s % 2][:, :], qk[:, b, 2 + k, s * P:(s + 1) * P],
                                               qk[:, b, k, 0:LAT], start=(k == 0), stop=(k == 1))
                            else:
                                mm = pe.matmul(PS[5][:, 2 * P:3 * P], qk[:, b, 2 + k, LAT:TOK],
                                               qk[:, b, k, LAT:TOK], start=(k == 0), stop=(k == 1))
                        mm.then_inc(sem("scores_done"), 1)

                def values(h):
                    b = h % 2
                    pe.wait_ge(sem("p_ready"), NT * (h + 1))
                    pe.wait_ge(sem("proj_copied"), 10 * h + 10)
                    if h == 0:
                        pe.wait_ge(sem("ones_set"), 1)
                    pe.wait_ge(sem("c0_in"), 32 * (h + 1))
                    for n in range(10):
                        t, d = n // 2, n % 2
                        if n >= 2:
                            pe.wait_ge(sem("nd_ready"), 10 * h + n - 1)
                        if t < 4:
                            for k in range(2):
                                pe.matmul(PS[6 + d][:, 0:DH + 1], qk[:, b, k, t * P:(t + 1) * P],
                                          C0[:, 2 * d + k, :], start=(k == 0), stop=(k == 1))
                            ss = range(t + 1) if d == 0 else range(t, 4)
                        else:
                            ss = (4,)
                        for s in ss:
                            if t == 4:
                                o = PW - CTX
                            else:
                                o = OFF[d][s] + (t - s if d == 0 else t) * P
                            mm = pe.matmul(PS[3 + d][:, 0:DH + 1], Pm[:, d, o:o + P], vt[:, b, s, :],
                                           start=(s == ss[0]), stop=(s == ss[-1]))
                        mm.then_inc(sem("pv_done"), 1)

                def turn(h):
                    b = h % 2
                    pe.wait_ge(sem("hn_ready"), h + 1)
                    for r, bank in enumerate((5, 3, 4)):
                        n = 2 if r < 2 else 1
                        for f in range(2):
                            for t in range(n):
                                o = (f * n + t) * P
                                mm = pe.transpose(PS[bank][:, o:o + P], hacc[:, 2 * r + t, f * P:(f + 1) * P], ident)
                        if r == 2:
                            for k in range(2):
                                o = (2 + k) * P
                                mm = pe.transpose(PS[bank][:, o:o + P], qk[:, b, 2 + k, LAT:TOK], ident)
                        mm.then_inc(sem("h_turned"), 1)
                    pe.wait_ge(sem("kw_ready"), h + 1)
                    for n in range(4):
                        d, k = n // 2, n % 2
                        if n >= 2:
                            pe.wait_ge(sem("co_ready"), 4 * h + n - 1)
                        pe.matmul(PS[6 + k][:, 0:DH + 1], kw[:, d, k * P:(k + 1) * P], vt[:, b, 4, :], start=True,
                                  stop=True).then_inc(sem("c_done"), 1)

                proj_qk(0)
                proj_vo(0)
                for h in range(H):
                    scores(h)
                    if h + 1 < H:
                        proj_qk(h + 1)
                    values(h)
                    if h + 1 < H:
                        proj_vo(h + 1)
                    turn(h)

            @block.scalar
            def _(act):
                a = chain(act, "act")

                def out_qk(h):
                    for m in range(4):
                        u = 9 * h + m
                        act.wait_ge(sem("qk_done"), 5 * h + m + 1)
                        act.activation(qk[:, h % 2, m, 0:LAT], PS[u % 2][:, :], ACT.Copy,
                                       scale=DH ** -0.5 if m < 2 else 1.0).then_inc(sem("proj_copied"), 1)
                    act.wait_ge(sem("qk_done"), 5 * h + 5)
                    for x in range(2):
                        ins = act.activation(qk[:, h % 2, 2 * x:2 * x + 2, LAT:TOK],
                                             PS[2][:, 256 * x:256 * x + 256].rearrange("p (m t) -> p m t", m=2),
                                             ACT.Copy, scale=1.0 if x else DH ** -0.5)
                    ins.then_inc(sem("proj_copied"), 1)

                def out_vo(h):
                    for t in range(NT):
                        u = 9 * h + 4 + t
                        act.wait_ge(sem("vo_done"), NT * h + t + 1)
                        act.activation(vt[:, h % 2, t, 0:DH], PS[u % 2][:, 0:DH], ACT.Copy)
                        act.activation(og[:, h % 2, t, :], PS[u % 2][:, DH:2 * DH],
                                       ACT.Sigmoid).then_inc(sem("proj_copied"), 1)

                def decays(h):
                    act.wait_ge(sem("negmd_ready"), h + 1)
                    for s in range(NT):
                        for d in range(2):
                            col = colT[:, s, d, h:h + 1]
                            if s == 4:
                                act.activation(Pm[:, d, PW - CTX:PW], negMd[:, d, LAT:TOK], ACT.Exp, bias=col)
                                at = TOK - 1 if d == 0 else LAT
                                ins = act.activation(wk[:, d:d + 1], negMd[:, d, at:at + 1], ACT.Exp, bias=col)
                                continue
                            o = OFF[d][s]
                            dg = o if d == 0 else o + s * P
                            ins = act.activation(Pm[:, d, dg:dg + P], negMd[:, d, s * P:(s + 1) * P], ACT.Exp, bias=col)
                            if d == 0 and s < 3:
                                ins = act.activation(Pm[:, d, o + P:o + (4 - s) * P], PS[3][:, (s + 1) * P:LAT],
                                                     ACT.Exp, bias=col)
                            if d == 1 and s > 0:
                                ins = act.activation(Pm[:, d, o:o + s * P], PS[4][:, 0:s * P], ACT.Exp, bias=col)
                        ins.then_inc(sem("decay_ready"), 1)

                def inter(h):
                    for n in range(8):
                        t, d = n // 2, n % 2
                        act.wait_ge(sem("pv_done"), 10 * h + n + 1)
                        if n >= 2:
                            act.wait_ge(sem("nd_ready"), 10 * h + n - 1)
                        act.activation(Qs[:, d, :], PS[6 + d][:, 0:DH + 1], ACT.Copy,
                                       scale=colT[:, t, 2 + d, h:h + 1]).then_inc(sem("inter_ready"), 1)

                def finish(h):
                    act.wait_ge(sem("ms_inv"), h + 1)
                    act.activation(rs5[:], ssq[:], ACT.Sqrt).then_inc(sem("rs_ready"), 1)
                    for r, bank in enumerate((5, 3, 4)):
                        act.wait_ge(sem("h_turned"), 3 * h + r + 1)
                        w = 256 if r < 2 else P
                        for f in range(2):
                            ins = act.activation(haT[:, 2 * h + f, r * 256:r * 256 + w], PS[bank][:, f * w:(f + 1) * w],
                                                 ACT.Copy, scale=par[:, PC_HN + 2 * h + f:PC_HN + 2 * h + f + 1])
                        ins.then_inc(sem("ha_ready"), 1)
                    if h:
                        act.wait_ge(sem("c_out"), 32 * h)
                    for n in range(4):
                        act.wait_ge(sem("c_done"), 4 * h + n + 1)
                        act.activation(Co[:, n, :], PS[6 + n % 2][:, 0:DH + 1], ACT.Copy).then_inc(sem("co_ready"), 1)

                out_qk(0)
                out_vo(0)
                for h in range(H):
                    decays(h)
                    if h + 1 < H:
                        out_qk(h + 1)
                    inter(h)
                    if h + 1 < H:
                        out_vo(h + 1)
                    finish(h)

            @block.vector
            def _(dve):
                v = chain(dve, "dve")

                def weigh(h):
                    dve.wait_ge(sem("m_spread"), h + 1)
                    for d, mask in enumerate((mask_f, mask_b)):
                        dve.tensor_tensor(negMd[:, d, 0:LAT].rearrange("p (s t) -> p s t", s=4),
                                          PS[3 + d][:, :].rearrange("p (s t) -> p s t", s=4),
                                          bc(mask.unsqueeze(1), [P, 4, P]), ALU.add)
                        ins = dve.tensor_tensor(negMd[:, d, LAT:TOK], PS[5][:, d * P:(d + 1) * P], mask, ALU.add)
                    ins.then_inc(sem("negmd_ready"), 1)
                    for s in range(NT):
                        dve.wait_ge(sem("scores_done"), NT * h + s + 1)
                        dve.wait_ge(sem("decay_ready"), NT * h + s + 1)
                        for d in range(2):
                            if s == 4:
                                x, sc = Pm[:, d, PW - CTX:PW], PS[5][:, 2 * P:3 * P]
                            elif d == 0:
                                x, sc = Pm[:, 0, OFF[0][s]:OFF[0][s] + (4 - s) * P], PS[6 + s % 2][:, s * P:LAT]
                            else:
                                x, sc = Pm[:, 1, OFF[1][s]:OFF[1][s] + (s + 1) * P], PS[6 + s % 2][:, 0:(s + 1) * P]
                            ins = dve.tensor_tensor(x, x, sc, ALU.mult)
                        ins.then_inc(sem("p_ready"), 1)

                def combine(h):
                    for n in range(10):
                        t, d = n // 2, n % 2
                        dve.wait_ge(sem("pv_done"), 10 * h + n + 1)
                        if t < 4:
                            dve.wait_ge(sem("inter_ready"), 8 * h + n + 1)
                            dve.tensor_tensor(nd[:, d, :], PS[3 + d][:, 0:DH + 1], Qs[:, d, :],
                                              ALU.add).then_inc(sem("nd_ready"), 1)
                        else:
                            dve.tensor_copy(nd[:, d, :], PS[3 + d][:, 0:DH + 1]).then_inc(sem("nd_ready"), 1)
                        if d == 0:
                            continue
                        dve.wait_ge(sem("nd_ready"), 10 * h + n + 1)
                        v(dve.scalar_tensor_tensor(rr[:], nd[:, :, DH], -1.0, nd[:, :, DH], ALU.mult, ALU.max))
                        v(dve.tensor_tensor(rr[:], rr[:], colT[:, t, 4:6, h], ALU.max))
                        v(dve.reciprocal(rr[:], rr[:]))
                        x = hacc[:, t, :]
                        v(dve.tensor_scalar(x, nd[:, 0, 0:DH], rr[:, 0:1], None, ALU.mult))
                        v(dve.scalar_tensor_tensor(x, nd[:, 1, 0:DH], rr[:, 1:2], x, ALU.mult, ALU.add))
                        dve.wait_ge(sem("proj_copied"), 10 * h + 5 + t + 1)
                        v(dve.tensor_tensor(x, x, og[:, h % 2, t, :], ALU.mult))
                        v(dve.scalar_tensor_tensor(junk[:], x, 1.0, x, ALU.mult, ALU.mult, accum_out=ssq[:, t:t + 1]))

                def finish(h):
                    v(dve.tensor_scalar(ssq[:], ssq[:], 1.0 / DH, EPS, ALU.mult, ALU.add))
                    dve.reciprocal(ssq[:], ssq[:]).then_inc(sem("ms_inv"), 1)
                    dve.wait_ge(sem("rs_ready"), h + 1)
                    for t in range(NT):
                        ins = dve.tensor_scalar(hacc[:, t, :], hacc[:, t, :], rs5[:, t:t + 1], None, ALU.mult)
                    ins.then_inc(sem("hn_ready"), 1)
                    dve.wait_ge(sem("ha_ready"), 3 * h + 3)
                    for d in range(2):
                        ins = dve.tensor_scalar(kw[:, d, :], PS[4][:, 2 * P:4 * P], wk[:, d:d + 1], None, ALU.mult)
                    ins.then_inc(sem("kw_ready"), 1)

                dve.tensor_copy(selH[:], bc(ident[0:H, 0:H].unsqueeze(2), [H, H, P])).then_inc(sem("sel_ready"), 1)
                dve.memset(vt[:, :, :, DH:DH + 1], 1.0).then_inc(sem("ones_set"), 1)
                for h in range(H):
                    weigh(h)
                    combine(h)
                    finish(h)

        with ExitStack() as st:
            mg = sb("mg", [P, KD, TOK], F32, st)
            sg = sb("sg2", [P, 2, TOK], F32, st)
            tm = sb("tm", [P, 2, TOK], F32, st)
            tmp = sb("tmp6", [P, TOK], F32, st)
            block = st.enter_context(nc.Block())

            @block.sync
            def _(sp):
                with nc.allow_non_contiguous_dma(reason="small"):
                    sp.dma_start(wr[:], ar["w_router"][0].rearrange("(k p) e -> p k e", p=P)).then_inc(sem("wr_in"), 16)
                load_weights(sp, len(plan))

            @block.tensor
            def _(pe):
                for m in range(KD):
                    cg, cp = CH_M + 2 * (m // 2), CH_M + 2 * (m // 2) + 1
                    for x in range(4):
                        if m >= 1:
                            pe.wait_ge(sem("gate_sig" if x < 2 else "branch_used"), 2 * (m - 1) + x % 2 + 1)
                        c = cg if x < 2 else cp
                        have_weights(pe, c)
                        src = (hT, hT, haT, hbT)[x]
                        kt = 4 if x == 3 else 8
                        o = 256 * (x % 2) + (m % 2) * P
                        for k in range(kt):
                            w = wslot(c)[:, k, o:o + P]
                            pe.matmul(PS[x][:, :], w, src[:, k, 0:LAT], start=(k == 0), stop=(k == kt - 1))
                            mm = pe.matmul(PS[4 + x][:, 0:CTX], w, src[:, k, LAT:TOK],
                                           start=(k == 0), stop=(k == kt - 1))
                        mm.then_inc(sem("merge_done"), 1)
                pe.wait_ge(sem("mg_ready"), KD)
                for m in range(KD):
                    c = CH_O + m // 4
                    have_weights(pe, c)
                    if m >= 2:
                        pe.wait_ge(sem("x2_ready"), m - 1)
                    for k in range(KD):
                        w = wslot(c)[:, k, (m % 4) * P:(m % 4 + 1) * P]
                        pe.matmul(PS[m % 2][:, :], w, mg[:, k, 0:LAT], start=(k == 0), stop=(k == 7))
                        mm = pe.matmul(PS[2 + m % 2][:, 0:CTX], w, mg[:, k, LAT:TOK], start=(k == 0), stop=(k == 7))
                    mm.then_inc(sem("out_done"), 1)
                pe_mean_square(pe, 1)
                pe.wait_ge(sem("wr_in"), 16)
                for k in range(KD):
                    pe.wait_ge(sem("modulated"), 8 + k + 1)
                    pe.matmul(PS[0][0:E, :], wr[:, k, :], hT[:, k, 0:LAT], start=(k == 0), stop=(k == 7))
                    mm = pe.matmul(PS[1][0:E, 0:CTX], wr[:, k, :], hT[:, k, LAT:TOK], start=(k == 0), stop=(k == 7))
                mm.then_inc(sem("logits_done"), 1)

            @block.scalar
            def _(act):
                for m in range(KD):
                    for x in range(2):
                        act.wait_ge(sem("merge_done"), 4 * m + x + 1)
                        if m:
                            act.wait_ge(sem("branch_used"), 2 * (m - 1) + x + 1)
                        act.activation(sg[:, x, 0:LAT], PS[x][:, :], ACT.Sigmoid)
                        act.activation(sg[:, x, LAT:TOK], PS[4 + x][:, 0:CTX],
                                       ACT.Sigmoid).then_inc(sem("gate_sig"), 1)
                for k in range(KD):
                    act.wait_ge(sem("x2_ready"), k + 1)
                    act_square(act, 1, k)
                act_rms(act, 1, tmp)
                act_modulate(act, 1, hT)

            @block.vector
            def _(dve):
                v = chain(dve, "dve")
                for m in range(KD):
                    if m:
                        dve.wait_ge(sem("mg_ready"), m)
                    for x in range(2):
                        dve.wait_ge(sem("gate_sig"), 2 * m + x + 1)
                        dve.wait_ge(sem("merge_done"), 4 * m + 2 + x + 1)
                        dve.tensor_tensor(tm[:, x, 0:LAT], sg[:, x, 0:LAT], PS[2 + x][:, :], ALU.mult)
                        dve.tensor_tensor(tm[:, x, LAT:TOK], sg[:, x, LAT:TOK], PS[6 + x][:, 0:CTX],
                                          ALU.mult).then_inc(sem("branch_used"), 1)
                    dve.wait_ge(sem("branch_used"), 2 * m + 2)
                    dve.tensor_tensor(mg[:, m, :], tm[:, 0, :], tm[:, 1, :], ALU.add).then_inc(sem("mg_ready"), 1)
                for m in range(KD):
                    dve.wait_ge(sem("out_done"), m + 1)
                    dve.scalar_tensor_tensor(xT[:, m, 0:LAT], PS[m % 2][:, :], modT[:, 16 + m, 0:1], xT[:, m, 0:LAT],
                                             ALU.mult, ALU.add)
                    dve.scalar_tensor_tensor(xT[:, m, LAT:TOK], PS[2 + m % 2][:, 0:CTX], modT[:, 16 + m, 1:2],
                                             xT[:, m, LAT:TOK], ALU.mult, ALU.add).then_inc(sem("x2_ready"), 1)
                dve_gain(dve, 1, PC_NFFN).then_inc(sem("gain_ready"), 1)
                dve_inverse_mean(dve, v, 1, tmp)
                dve_normalise(dve, 1)
        acts.close()

        moe = ctx.enter_context(ExitStack())
        w13 = sb("w13", [P, FG, 2, KD, FT * P], F32, moe)
        w2 = sb("w2", [P, 2, FT, D], F32, moe)
        gval = sb("gval", [CAP, E], F32, moe)
        gidx = sb("gidx", [CAP, E], I32, moe)
        we1 = ar["w_e1"][0].rearrange("e (k p) f -> p e k f", p=P)
        we3 = ar["w_e3"][0].rearrange("e (k p) f -> p e k f", p=P)
        we2 = ar["w_e2"][0].rearrange("e (t p) d -> p e t d", p=P)

        def load_w13(sp, e, q):
            c = q * FT * P
            for x, src in enumerate((we1, we3)):
                sp.dma_start(w13[:, q, x], src[:, bass.ds(e, 1), :, c:c + FT * P].rearrange("p e k f -> p (e k) f")
                             ).then_inc(sem(f"w13_in{q}"), 16)

        def load_w2(sp, e, q):
            sp.dma_start(w2[:, q % 2], we2[:, bass.ds(e, 1), q * FT:(q + 1) * FT, :].rearrange("p e t d -> p (e t) d")
                         ).then_inc(sem(f"w2_in{q % 2}"), 16)

        with ExitStack() as st:
            lgT = rsb[0:E, :]
            lg = sb("lg", [P, NT, E], F32, st)
            mx = sb("mx", [P, NT], F32, st)
            af = sb("af", [E, TOK], F32, st)
            topv = sb("topv", [E, CAP], F32, st)
            topi = sb("topi", [E, CAP], U32, st)
            topf = sb("topf", [E, CAP], F32, st)
            block = st.enter_context(nc.Block())

            htok = w13[:, FG - 2:FG].rearrange("p q x k f -> p (q x k f)")[:, 0:NT * D].rearrange("p (t d) -> p t d", t=NT)

            def token_rows(t):
                return htok[:, t, :]

            @block.sync
            def _(sp):
                load_w13(sp, 0, 0)
                load_w13(sp, 0, 1)
                load_w2(sp, 0, 0)
                for t in range(NT):
                    sp.wait_ge(sem(f"h2_out{t}"), 16)
                load_w13(sp, 0, 2)
                load_w2(sp, 0, 1)

            @block.gpsimd
            def _(pool):
                for t in range(NT):
                    pool.wait_ge(sem("htok_ready"), t + 1)
                    pool.dma_start(ar["h2"][t * P:(t + 1) * P, :], token_rows(t)).then_inc(sem(f"h2_out{t}"), 16)
                for t in range(NT):
                    pool.wait_ge(sem(f"h2_out{t}"), 16)

            @block.tensor
            def _(pe):
                pe.wait_ge(sem("lgT_ready"), 1)
                for t in range(NT):
                    mm = pe.transpose(PS[7][:, E * t:E * t + E], lgT[:, t * P:(t + 1) * P], ident[0:E, 0:E])
                mm.then_inc(sem("logits_turned"), 1)
                for t in range(NT):
                    if t >= 2:
                        pe.wait_ge(sem("htok_ready"), t - 1)
                    for k in range(KD):
                        mm = pe.transpose(PS[1 + 2 * (t % 2) + k // 4][:, (k % 4) * P:(k % 4 + 1) * P],
                                          hT[:, k, t * P:(t + 1) * P], ident)
                    mm.then_inc(sem("h2_turned"), 1)
                pe.wait_ge(sem("aff_ready"), 1)
                for t in range(NT):
                    mm = pe.transpose(PS[5 + t // 4][0:E, (t % 4) * P:(t % 4 + 1) * P], lg[:, t, :], ident)
                mm.then_inc(sem("aff_turned"), 1)
                pe.wait_ge(sem("top_ready"), 1)
                pe.transpose(PS[7][0:CAP, 0:E], topv[:], ident[0:E, 0:E])
                pe.transpose(PS[7][0:CAP, E:2 * E], topf[:], ident[0:E, 0:E]).then_inc(sem("top_turned"), 1)

            @block.scalar
            def _(act):
                act.wait_ge(sem("lg_shifted"), 1)
                act.activation(lg[:], lg[:], ACT.Exp).then_inc(sem("lg_exp"), 1)
                for t in range(NT):
                    act.wait_ge(sem("h2_turned"), t + 1)
                    for x in range(2):
                        ins = act.activation(token_rows(t)[:, x * 512:(x + 1) * 512], PS[1 + 2 * (t % 2) + x][:, :],
                                             ACT.Copy)
                    ins.then_inc(sem("htok_ready"), 1)

            @block.vector
            def _(dve):
                v = chain(dve, "dve")
                dve.wait_ge(sem("logits_done"), 1)
                dve.tensor_copy(lgT[:, 0:LAT], PS[0][0:E, :])
                dve.tensor_copy(lgT[:, LAT:TOK], PS[1][0:E, 0:CTX]).then_inc(sem("lgT_ready"), 1)
                dve.wait_ge(sem("logits_turned"), 1)
                v(dve.tensor_tensor(lg[:], PS[7][:, 0:NT * E].rearrange("p (t e) -> p t e", t=NT),
                                    bc(par[:, PC_BR:PC_BR + E].unsqueeze(1), [P, NT, E]), ALU.add))
                v(dve.tensor_reduce(mx[:], lg[:], AX.X, ALU.max))
                dve.tensor_tensor(lg[:], lg[:], bc(mx[:].unsqueeze(2), [P, NT, E]),
                                  ALU.subtract).then_inc(sem("lg_shifted"), 1)
                dve.wait_ge(sem("lg_exp"), 1)
                v(dve.tensor_reduce(mx[:], lg[:], AX.X, ALU.add))
                v(dve.reciprocal(mx[:], mx[:]))
                dve.tensor_tensor(lg[:], lg[:], bc(mx[:].unsqueeze(2), [P, NT, E]),
                                  ALU.mult).then_inc(sem("aff_ready"), 1)
                dve.wait_ge(sem("aff_turned"), 1)
                dve.tensor_copy(af[:, 0:LAT], PS[5][0:E, :])
                v(dve.tensor_copy(af[:, LAT:TOK], PS[6][0:E, 0:CTX]))
                for lo, hi, at, cap in ((0, LAT, 0, CAPL), (LAT, TOK, CAPL, CAPC)):
                    for o in range(at, at + cap, 8):
                        v(dve.max(topv[:, o:o + 8], af[:, lo:hi]))
                        v(dve.max_index(topi[:, o:o + 8], topv[:, o:o + 8], af[:, lo:hi]))
                        if o + 8 < at + cap:
                            v(dve.match_replace(af[:, lo:hi], topv[:, o:o + 8], af[:, lo:hi], -1.0))
                v(dve.tensor_copy(topf[:], topi[:]))
                dve.tensor_scalar(topf[:, CAPL:CAP], topf[:, CAPL:CAP], float(LAT), None,
                                  ALU.add).then_inc(sem("top_ready"), 1)
                dve.wait_ge(sem("top_turned"), 1)
                dve.tensor_copy(gval[:], PS[7][0:CAP, 0:E])
                dve.tensor_copy(gidx[:], PS[7][0:CAP, E:2 * E])

        with ExitStack() as st:
            rows = hT[:].rearrange("p k t -> p (k t)")
            xe = rows[0:CAP, 0:2 * D].rearrange("p (b d) -> p b d", b=2)
            ys = rows[0:CAP, 2 * D:4 * D].rearrange("p (b d) -> p b d", b=2)
            xeT = sb("xeT", [P, 2, KD, CAP], F32, st)
            HC = FT * CAP
            sl, hid = (sq[:, x, 0:2 * HC].rearrange("p (b n) -> p b n", b=2) for x in range(2))
            hid_h = sb("hid_h", [P, 2, HC], F32R, st)
            hid_l = sb("hid_l", [P, 2, HC], F32R, st)
            w2_h = sb("w2_h", [P, 2, FT, D], F32R, st)
            w2_l = sb("w2_l", [P, 2, FT, D], F32R, st)
            block = st.enter_context(nc.Block())

            @block.sync
            def _(sp):
                def next_w13(e, q):
                    sp.wait_ge(sem("hidden_done"), FG * e + (q - FG + 1))
                    load_w13(sp, e, q)

                def next_w2(e, q):
                    sp.wait_ge(sem("w2_split"), FG * e + (q - 1))
                    load_w2(sp, e, q)

                sp.wait_ge(sem("xe_in0"), 16)
                for q in range(3, FG):
                    load_w13(sp, 0, q)
                with sp.Fori(1, E) as e:
                    for q in range(FG):
                        next_w13(e, q)
                        if q < 4:
                            next_w2(e - 1, q + 2)
                        else:
                            next_w2(e, q - 4)
                for q in range(2, FG):
                    next_w2(E - 1, q)

            @block.gpsimd
            def _(pool):
                def gather(e):
                    if e >= 2:
                        pool.wait_ge(sem("x_turned"), e - 1)
                    pool.indirect_dma_start(out=xe[:, e % 2, :], out_offset=None, in_=ar["h2"][:, :],
                                            in_offset=bass.IndirectOffsetOnAxis(ap=gidx[:, e:e + 1], axis=0)
                                            ).then_inc(sem(f"xe_in{e % 2}"), 16)

                def scatter(e):
                    pool.wait_ge(sem("y_ready"), e + 1)
                    if e:
                        pool.wait_ge(sem(f"y_out{(e - 1) % 2}"), 16 * ((e - 1) // 2 + 1))
                    pool.indirect_dma_start(out=ar["moe"][:, :],
                                            out_offset=bass.IndirectOffsetOnAxis(ap=gidx[:, e:e + 1], axis=0),
                                            in_=ys[:, e % 2, :], in_offset=None, compute_op=ALU.add
                                            ).then_inc(sem(f"y_out{e % 2}"), 16)

                gather(0)
                for e in range(E):
                    if e + 1 < E:
                        gather(e + 1)
                    scatter(e)
                pool.wait_ge(sem("y_out0"), 16 * E // 2)
                pool.wait_ge(sem("y_out1"), 16 * E // 2)

            def pairs(eng, body):
                body(0, 0)
                body(0, 1)
                with eng.Fori(1, E // 2) as i:
                    body(i, 0)
                    body(i, 1)

            def is_first(i, u):
                return isinstance(i, int) and i == 0 and u == 0

            @block.tensor
            def _(pe):
                def down(i, u, q):
                    n = 2 * FG * i + FG * u + q
                    pe.wait_ge(sem("hid_split"), n + 1)
                    pe.wait_ge(sem("w2_split"), n + 1)
                    for t in range(FT):
                        cols = slice(t * CAP, (t + 1) * CAP)
                        for x in range(2):
                            for j, (hp, wp) in enumerate(((hid_h, w2_h), (hid_h, w2_l), (hid_l, w2_h))):
                                mm = pe.matmul(PS[2 + x][0:CAP, :], hp[:, q % 2, cols],
                                               wp[:, q % 2, t, x * 512:(x + 1) * 512],
                                               start=(q == 0 and t == 0 and j == 0),
                                               stop=(q == FG - 1 and t == FT - 1 and j == 2))
                    mm.then_inc(sem("down_done"), 1)

                def body(i, u):
                    first = is_first(i, u)
                    pe.wait_ge(sem(f"xe_in{u}"), 16 * i + 16)
                    for k in range(KD):
                        mm = pe.transpose(PS[4 + k // 4][:, (k % 4) * CAP:(k % 4 + 1) * CAP],
                                          xe[:, u, k * P:(k + 1) * P], ident[0:CAP, 0:CAP])
                    mm.then_inc(sem("x_turned"), 1)
                    if not first:
                        down(i if u else i - 1, 1 - u, FG - 1)
                    pe.wait_ge(sem("xt_ready"), 2 * i + u + 1)
                    for q in range(FG):
                        if not (first and q < 2):
                            pe.wait_ge(sem("hid_ready"), 2 * FG * i + (FG * u + q - 1))
                        pe.wait_ge(sem(f"w13_in{q}"), 64 * i + 32 * u + 32)
                        for x in range(2):
                            for t in range(FT):
                                o = x * HC + t * CAP
                                for k in range(KD):
                                    mm = pe.matmul(PS[q % 2][:, o:o + CAP], w13[:, q, x, k, t * P:(t + 1) * P],
                                                   xeT[:, u, k, :], start=(k == 0), stop=(k == 7))
                        mm.then_inc(sem("hidden_done"), 1)
                        if q == 1 and not first:
                            pe.wait_ge(sem("y_ready"), 2 * i + u)
                        if q >= 1:
                            down(i, u, q - 1)

                pairs(pe, body)
                down(E // 2 - 1, 1, FG - 1)

            @block.scalar
            def _(act):
                def body(i, u):
                    act.wait_ge(sem("x_turned"), 2 * i + u + 1)
                    for x in range(2):
                        ins = act.activation(xeT[:, u, 4 * x:4 * x + 4, :].rearrange("p k c -> p (k c)"),
                                             PS[4 + x][:, 0:4 * CAP], ACT.Copy)
                    ins.then_inc(sem("xt_ready"), 1)
                    for q in range(FG):
                        n = 2 * FG * i + (FG * u + q)
                        early = is_first(i, u) and q < 2
                        act.wait_ge(sem("hidden_done"), n + 1)
                        if not early:
                            act.wait_ge(sem("hid_ready"), n - 1)
                        act.activation(sl[:, q % 2, :], PS[q % 2][:, 0:HC], ACT.Silu).then_inc(sem("silu_ready"), 1)
                        if not early:
                            act.wait_ge(sem("down_done"), n - 1)
                        act.wait_ge(sem(f"w2_in{q % 2}"), 96 * i + (48 * u + 16 * (q // 2) + 16))
                        act.activation(w2_h[:, q % 2], w2[:, q % 2], ACT.Copy).then_inc(sem("w2_high"), 1)
                        act.wait_ge(sem("hid_ready"), n + 1)
                        act.activation(hid_h[:, q % 2, :], hid[:, q % 2, :], ACT.Copy).then_inc(sem("hid_high"), 1)

                pairs(act, body)

            @block.vector
            def _(dve):
                def take_y(i, u):
                    dve.wait_ge(sem("down_done"), 2 * FG * i + (FG * u + FG))
                    if not (isinstance(i, int) and i == 0):
                        dve.wait_ge(sem(f"y_out{u}"), 16 * i)
                    g = gval[:, bass.ds(2 * i + u, 1)]
                    dve.tensor_scalar(ys[:, u, 0:512], PS[2][0:CAP, :], g, None, ALU.mult)
                    dve.tensor_scalar(ys[:, u, 512:D], PS[3][0:CAP, :], g, None, ALU.mult).then_inc(sem("y_ready"), 1)

                def body(i, u):
                    first = is_first(i, u)
                    if not first:
                        take_y(i if u else i - 1, 1 - u)
                    for q in range(FG):
                        n = 2 * FG * i + (FG * u + q)
                        dve.wait_ge(sem("silu_ready"), n + 1)
                        if not (first and q < 2):
                            dve.wait_ge(sem("hid_split"), n - 1)
                        dve.tensor_tensor(hid[:, q % 2, :], sl[:, q % 2, :], PS[q % 2][:, HC:2 * HC],
                                          ALU.mult).then_inc(sem("hid_ready"), 1)
                        dve.wait_ge(sem("w2_high"), n + 1)
                        if not (first and q < 2):
                            dve.wait_ge(sem("down_done"), n - 1)
                        dve.tensor_tensor(w2_l[:, q % 2], w2[:, q % 2], w2_h[:, q % 2].bitcast(F32),
                                          ALU.subtract).then_inc(sem("w2_split"), 1)
                        dve.wait_ge(sem("hid_high"), n + 1)
                        dve.tensor_tensor(hid_l[:, q % 2, :], hid[:, q % 2, :], hid_h[:, q % 2, :].bitcast(F32),
                                          ALU.subtract).then_inc(sem("hid_split"), 1)

                pairs(dve, body)
                take_y(E // 2 - 1, 1)
        moe.close()

        with ExitStack() as st:
            mt = sb("mt", [P, NT, D], F32, st)
            yT = sb("yT", [P, KD, TOK], F32, st)
            tmp = sb("tmp9", [P, TOK], F32, st)
            block = st.enter_context(nc.Block())

            @block.sync
            def _(sp):
                for t in range(NT):
                    sp.dma_start(mt[:, t, :], ar["moe"][t * P:(t + 1) * P, :]).then_inc(sem(f"mt_in{t}"), 16)
                for k in range(KD):
                    sp.wait_ge(sem("y_done"), k + 1)
                    sp.dma_start(out["yT"][:, k, :], yT[:, k, :]).then_inc(sem("yT_out"), 16)
                sp.wait_ge(sem("yT_out"), 16 * KD)

            @block.tensor
            def _(pe):
                for k in range(KD):
                    if k >= 2:
                        pe.wait_ge(sem("x3_ready"), k - 1)
                    for t in range(NT):
                        if k == 0:
                            pe.wait_ge(sem(f"mt_in{t}"), 16)
                        dst = PS[k % 2][:, t * P:(t + 1) * P] if t < 4 else PS[2 + k % 2][:, 0:CTX]
                        mm = pe.transpose(dst, mt[:, t, k * P:(k + 1) * P], ident)
                    mm.then_inc(sem("moe_turned"), 1)
                pe_mean_square(pe, 2)

            @block.scalar
            def _(act):
                for k in range(KD):
                    act.wait_ge(sem("x3_ready"), k + 1)
                    act_square(act, 2, k)
                act_rms(act, 2, tmp)
                for k in range(KD):
                    act.wait_ge(sem("normalised"), 16 + k + 1)
                    act.activation(yT[:, k, :], sq[:, k % 2, :], ACT.Copy,
                                   scale=par[:, PC_NFIN + k:PC_NFIN + k + 1]).then_inc(sem("y_done"), 1)

            @block.vector
            def _(dve):
                v = chain(dve, "dve")
                for k in range(KD):
                    dve.wait_ge(sem("moe_turned"), k + 1)
                    dve.scalar_tensor_tensor(xT[:, k, 0:LAT], PS[k % 2][:, :], modT[:, 40 + k, 0:1], xT[:, k, 0:LAT],
                                             ALU.mult, ALU.add)
                    dve.scalar_tensor_tensor(xT[:, k, LAT:TOK], PS[2 + k % 2][:, 0:CTX], modT[:, 40 + k, 1:2],
                                             xT[:, k, LAT:TOK], ALU.mult, ALU.add).then_inc(sem("x3_ready"), 1)
                dve_inverse_mean(dve, v, 2, tmp)
                dve.wait_ge(sem("rms"), 3)
                for k in range(KD):
                    if k >= 2:
                        dve.wait_ge(sem("y_done"), k - 1)
                    dve.tensor_tensor(sq[:, k % 2, :], xT[:, k, :], rsb[:], ALU.mult).then_inc(sem("normalised"), 1)


def _positions():
    q = D // 4
    n = np.arange(LAT)
    r, c = (n // 64).astype(np.float32), (n % 64).astype(np.float32)
    fr = (1.0 / (np.float32(10000.0) ** (np.arange(q, dtype=np.float32) / np.float32(q)))).astype(np.float32)
    er, ec = r[:, None] * fr, c[:, None] * fr
    return np.concatenate([np.sin(er), np.cos(er), np.sin(ec), np.cos(ec)], -1).astype(np.float32)


def _feature_major(a):
    return np.ascontiguousarray(np.asarray(a).reshape(a.shape[0], -1, P).transpose(2, 1, 0))


def kernel(**inputs):
    import concourse.bacc as bacc
    from concourse.bass_utils import run_bass_kernel_spmd

    i = {k: np.asarray(v) for k, v in inputs.items()}
    col = lambda a, n: np.asarray(a).reshape(n, P).T
    both = lambda a: np.concatenate([a, a], 0)
    dirp = lambda a: np.asarray(a).reshape(2, GN, SP_).transpose(0, 2, 1).reshape(P, GN)
    c2 = np.stack([i["c"][0], i["c_ctx"]])
    arrays = {}
    arrays["par"] = np.concatenate([
        _feature_major(c2).reshape(P, 16), col(i["b_ada"][0], 48), col(i["norm_mix"][0], 8), col(i["norm_ffn"][0], 8),
        col(i["norm_final"], 8), col(i["head_norm"][0].reshape(-1), 8), col(i["b_glu"][0], 4),
        np.broadcast_to(i["b_router"][0][None], (P, E))], 1)
    arrays["consts"] = np.stack([np.eye(P), np.where(np.arange(P)[None] >= np.arange(P)[:, None], 0, -1e30),
                                 np.where(np.arange(P)[None] <= np.arange(P)[:, None], 0, -1e30)],
                                1).astype(np.float32)
    arrays["xT"] = _feature_major(np.concatenate([i["x_sample"][0], i["x_prompt"][0]], 0))
    arrays["posT"] = _feature_major(_positions())
    arrays["gbias"] = i["b_gate"][0].reshape(4 * H, 1)
    arrays["gpar"] = np.concatenate([i["b_gate"][0].T, i["state_mlstm_m"][0, 0].T], 1)
    ldt = np.repeat(i["s5_log_dt"][0], SP_, 0).reshape(P, GN)
    arrays["s5p"] = np.stack([dirp(i["s5_a_re"][0]), dirp(i["s5_a_im"][0]), ldt,
                              dirp(i["state_s5_re"][0, 0]), dirp(i["state_s5_im"][0, 0])], 1)
    arrays["s5bc"] = np.stack(
        [both(i[n][0].transpose(1, 0, 2)) for n in ("s5_b_re", "s5_b_im")]
        + [i[n][0].transpose(0, 3, 1, 2).reshape(P, GN, GC) for n in ("s5_c_re", "s5_c_im")], 1)
    arrays["s5d"] = i["s5_d"][0].reshape(GN, GC).T
    arrays["Cn"] = np.concatenate([i["state_mlstm_C"][0, 0], i["state_mlstm_n"][0, 0][..., None]], -1)
    for n in ("w_ada", "w_in", "w_pA", "w_pB", "w_out", "w_glu", "w_router", "w_e1", "w_e3", "w_e2"):
        arrays[n] = i[n]
    arrays = {k: np.ascontiguousarray(a) for k, a in arrays.items()}

    nc = bacc.Bacc("TRN2", target_bir_lowering=False, num_devices=1)
    ar = {k: nc.dram_tensor(k + "_dram", a.shape, mybir.dt.from_np(a.dtype), kind="ExternalInput").ap()
          for k, a in arrays.items()}
    ar["moe"] = nc.dram_tensor("moe_dram", (TOK, D), F32, kind="Internal").ap()
    ar["u"] = nc.dram_tensor("u_dram", (SW, TOK), F32, kind="Internal").ap()
    ar["h2"] = nc.dram_tensor("h2_dram", (TOK, D), F32, kind="Internal").ap()
    shapes = {"yT": (P, KD, TOK), "Cn": (2, H, DH, DH + 1), "m": (2, H), "s5": (2, P, GN)}
    out = {k: nc.dram_tensor("out_" + k, s, F32, kind="ExternalOutput").ap() for k, s in shapes.items()}
    program(nc, ar, out)
    r = run_bass_kernel_spmd(nc, [{k + "_dram": a for k, a in arrays.items()}], core_ids=[0]).results[0]
    y = np.asarray(r["out_yT"]).transpose(2, 1, 0).reshape(TOK, D)
    Cn = np.asarray(r["out_Cn"])
    s5 = np.asarray(r["out_s5"]).reshape(2, 2, SP_, GN).transpose(0, 1, 3, 2)
    full = lambda a: np.ascontiguousarray(a)[None, None]
    return (np.ascontiguousarray(y[LAT:])[None], np.ascontiguousarray(y[:LAT])[None], full(Cn[..., :DH]),
            full(Cn[..., DH]), full(np.asarray(r["out_m"])), full(s5[0]), full(s5[1]))
```

```python
from contextlib import ExitStack

import numpy as np
import concourse.bass as bass
from concourse import mybir

F32 = mybir.dt.float32
F32R = mybir.dt.float32r
U32 = mybir.dt.uint32
I32 = mybir.dt.int32
ALU = mybir.AluOpType
ACT = mybir.ActivationFunctionType
AX = mybir.AxisListType

P = 128
D = 1024
KD = D // P
LAT, CTX = 512, 128
TOK = LAT + CTX
TH = TOK // 2
NT = TOK // P
H, DH = 4, 256
MW = H * DH
SW, GC, GN, SP_ = 512, 16, 32, 64
L = 8
JL, JC = LAT // L, CTX // L
J = JL + JC
NS_ = (JL + 1) + (JC + 1)
QG = 8
NQ = GN // QG
E, FF = 16, 1536
CAPL, CAPC = 2 * LAT // E, 2 * CTX // E
CAP = CAPL + CAPC
FG = 6
NRAW = 3
FT = FF // P // FG
EPS = 1e-6
IN_COLS = 4 * MW + 4 * H + SW + 2 * D
C_Q, C_K, C_V, C_O, C_G = 0, MW, 2 * MW, 3 * MW, 4 * MW
C_U = C_G + 4 * H
C_GA = C_U + SW
C_GB = C_GA + D
NSLOT = 3

PC_C, PC_BADA, PC_NMIX, PC_NFFN, PC_NFIN, PC_HN, PC_BGLU, PC_BR = 0, 16, 64, 72, 80, 88, 96, 100
PC_N = 116


def bc(ap, shape):
    return ap.to_broadcast(shape)


class Chain:

    def __init__(self, eng, sem):
        self.eng, self.sem, self.n = eng, sem, 0

    def __call__(self, ins):
        self.n += 1
        ins.then_inc(self.sem, 1)
        self.eng.wait_ge(self.sem, self.n)


def program(nc, ar, out):
    with ExitStack() as ctx:
        def sb(name, shape, dt=F32, stack=None):
            return (stack or ctx).enter_context(nc.sbuf_tensor(name, shape, dt))

        sems = {}

        def sem(name):
            if name not in sems:
                sems[name] = ctx.enter_context(nc.semaphore(name))
            return sems[name]

        chains = {}

        def chain(eng, name):
            if name not in chains:
                chains[name] = Chain(eng, sem("order_" + name))
            chains[name].eng = eng
            return chains[name]

        PS = [ctx.enter_context(nc.psum_tensor(f"bank{i}", [P, 512], F32)) for i in range(8)]

        par = sb("par", [P, PC_N])
        consts = sb("consts", [P, 3, P])
        ident, mask_f, mask_b = consts[:, 0, :], consts[:, 1, :], consts[:, 2, :]
        meanw = sb("meanw", [P, P])
        modT = sb("modT", [P, 48, 2])
        gain = sb("gain", [P, 2, KD, 2])
        xT = sb("xT", [P, KD, TOK])
        rsb = sb("rsb", [P, TOK])
        sq = sb("sq", [P, 2, TOK])
        gpar = sb("gpar", [H, 6])
        wr = sb("wr", [P, KD, E])
        hT = sb("hT", [P, KD, TOK])
        acts = ctx.enter_context(ExitStack())
        place = sb("place", [P, 3 * NRAW, 2048])
        W = place[:, 0:2 * NSLOT].rearrange("p (s x) n -> p s (x n)", x=2)
        spare = place[:, 2 * NSLOT:3 * NRAW].rearrange("p x n -> p (x n)")
        hbT = sb("hbT", [P, 4, TOK], F32, acts)
        colT = sb("colT", [P, NT, 6, H], F32, acts)
        negM = sb("negM", [H, 2, TOK], F32, acts)

        w_in = ar["w_in"][0].rearrange("(k p) n -> p k n", p=P)
        w_ada = ar["w_ada"][0].rearrange("(k p) n -> p k n", p=P)
        w_pA = ar["w_pA"][0].rearrange("(k p) n -> p k n", p=P)
        w_pB = ar["w_pB"][0].rearrange("(k p) n -> p k n", p=P)
        w_out = ar["w_out"][0].rearrange("(k p) n -> p k n", p=P)
        w_glu = ar["w_glu"][0].rearrange("(k p) n -> p k n", p=P)
        plan = []

        def ada_piece(c, slot):
            plan.append(([(8, 0, w_ada[:, :, 512 * c:512 * c + 512])], "ada_done", c + 1, slot))

        for c in range(4):
            ada_piece(c, c % NSLOT)
        CH_U = len(plan)
        plan.append(([(8, 0, w_in[:, :, C_U:C_U + SW])], "u_done", 4, 1))
        CH_A = len(plan)
        for c in range(4, 12):
            ada_piece(c, 1)
        CH_H = len(plan)

        def piece(parts, freed_by, value):
            plan.append((parts, freed_by, value, (1 + len(plan) - CH_H) % NSLOT))

        for h in range(H):
            o = h * DH
            piece([(8, 0, w_in[:, :, C_Q + o:C_Q + o + DH]), (8, DH, w_in[:, :, C_K + o:C_K + o + DH])],
                  "qk_done", 5 * (h + 1))
            piece([(8, 0, w_in[:, :, C_V + o:C_V + o + DH]), (8, DH, w_in[:, :, C_O + o:C_O + o + DH])],
                  "vo_done", NT * (h + 1))
        steps = []
        for m in range(4):
            steps += [("G", m, k) for k in range(8)] + [("A", m, k) for k in range(8)] + [("B", m, k) for k in range(4)]
        for m in range(2):
            steps += [("O", m, k) for k in range(8)]
        ends = {kind + str(m): n + 1 for n, (kind, m, k) in enumerate(steps)}
        CH_M = len(plan)
        for m in range(4):
            o = 256 * m
            piece([(8, 0, w_in[:, :, C_GA + o:C_GA + o + 256]), (8, 256, w_in[:, :, C_GB + o:C_GB + o + 256])],
                  "parts_ready", ends[f"G{m}"])
            piece([(8, 0, w_pA[:, :, o:o + 256]), (4, 256, w_pB[:, :, o:o + 256])],
                  "parts_ready", ends[f"B{m}"])
        CH_O = len(plan)
        for m in range(2):
            piece([(8, 0, w_out[:, :, 512 * m:512 * m + 512])], "parts_ready", ends[f"O{m}"])
        landed, before, per_slot, last_in = [], [], [0] * NSLOT, [None] * NSLOT
        for c, (parts, _, _, slot) in enumerate(plan):
            per_slot[slot] += 16 * len(parts)
            landed.append(per_slot[slot])
            before.append(last_in[slot])
            last_in[slot] = c
        issued = [0]

        def wslot(c, kt=8):
            return W[:, plan[c][3], 0:kt * 512].rearrange("p (k n) -> p k n", k=kt)

        def load_weights(eng, upto):
            while issued[0] < min(upto, len(plan)):
                c = issued[0]
                if before[c] is not None:
                    eng.wait_ge(sem(plan[before[c]][1]), plan[before[c]][2])
                for kt, at, src in plan[c][0]:
                    n = src.shape[2]
                    eng.dma_start(wslot(c, kt)[:, :, at:at + n], src).then_inc(sem(f"ring{plan[c][3]}"), 16)
                issued[0] += 1

        def have_weights(eng, c):
            eng.wait_ge(sem(f"ring{plan[c][3]}"), landed[c])

        def ada_at(c):
            return c if c < 4 else CH_A + c - 4

        def pe_ada(pe, c, bank):
            have_weights(pe, ada_at(c))
            for k in range(KD):
                mm = pe.matmul(PS[bank][0:2, :], cs[:, k, :], wslot(ada_at(c))[:, k, :], start=(k == 0), stop=(k == 7))
            mm.then_inc(sem("ada_done"), 1)
            pe.wait_ge(sem("ada_row"), c + 1)
            for n in range(4):
                mm = pe.transpose(PS[bank][:, 2 * n:2 * n + 2], adar[:, c % 2, n * P:(n + 1) * P], ident[0:2, 0:2])
            mm.then_inc(sem("ada_turned"), 1)

        def act_ada(act, c, bank):
            act.wait_ge(sem("ada_done"), c + 1)
            act.activation(adar[:, c % 2, :], PS[bank][0:2, :], ACT.Copy).then_inc(sem("ada_row"), 1)

        def dve_ada(dve, c, bank):
            dve.wait_ge(sem("ada_turned"), c + 1)
            dve.tensor_tensor(modT[:, 4 * c:4 * c + 4, :], PS[bank][:, 0:8].rearrange("p (n s) -> p n s", s=2),
                              bc(par[:, PC_BADA + 4 * c:PC_BADA + 4 * c + 4].unsqueeze(2), [P, 4, 2]),
                              ALU.add).then_inc(sem("mod_in"), 1)

        def dve_gain(dve, n, pc):
            return dve.scalar_tensor_tensor(gain[:, n], modT[:, 24 * n + 8:24 * n + 16, :], 1.0,
                                            bc(par[:, pc:pc + 8].unsqueeze(2), [P, KD, 2]), ALU.add, ALU.mult)

        MS = {0: (6, 7), 1: (0, 1), 2: (6, 7)}

        def pe_mean_square(pe, n):
            for k in range(KD):
                pe.wait_ge(sem("squares"), 8 * n + k + 1)
                pe.matmul(PS[MS[n][0]][:, 0:LAT], meanw[:], sq[:, k % 2, 0:LAT], start=(k == 0), stop=(k == 7))
                pe.matmul(PS[MS[n][1]][:, 0:CTX], meanw[:], sq[:, k % 2, LAT:TOK], start=(k == 0),
                          stop=(k == 7)).then_inc(sem("squares_summed"), 1)

        def act_square(act, n, k):
            if k >= 2:
                act.wait_ge(sem("squares_summed"), 8 * n + k - 1)
            act.activation(sq[:, k % 2, :], xT[:, k, :], ACT.Square).then_inc(sem("squares"), 1)

        def dve_inverse_mean(dve, v, n, tmp):
            dve.wait_ge(sem("squares_summed"), 8 * n + 8)
            v(dve.tensor_scalar(tmp[:, 0:LAT], PS[MS[n][0]][:, 0:LAT], EPS, None, ALU.add))
            v(dve.tensor_scalar(tmp[:, LAT:TOK], PS[MS[n][1]][:, 0:CTX], EPS, None, ALU.add))
            dve.reciprocal(tmp[:], tmp[:]).then_inc(sem("inverse_mean"), 1)

        def act_rms(act, n, tmp):
            act.wait_ge(sem("inverse_mean"), n + 1)
            act.activation(rsb[:], tmp[:], ACT.Sqrt).then_inc(sem("rms"), 1)

        def dve_normalise(dve, n):
            dve.wait_ge(sem("rms"), n + 1)
            for k in range(KD):
                if k >= 2:
                    dve.wait_ge(sem("modulated"), 8 * n + k - 1)
                dve.tensor_tensor(sq[:, k % 2, :], xT[:, k, :], rsb[:], ALU.mult).then_inc(sem("normalised"), 1)

        def act_modulate(act, n, dst):
            for k in range(KD):
                act.wait_ge(sem("normalised"), 8 * n + k + 1)
                if k == 0:
                    act.wait_ge(sem("gain_ready"), n + 1)
                act.activation(dst[:, k, 0:LAT], sq[:, k % 2, 0:LAT], ACT.Identity,
                               scale=gain[:, n, k, 0:1], bias=modT[:, 24 * n + k, 0:1])
                act.activation(dst[:, k, LAT:TOK], sq[:, k % 2, LAT:TOK], ACT.Identity,
                               scale=gain[:, n, k, 1:2],
                               bias=modT[:, 24 * n + k, 1:2]).then_inc(sem("modulated"), 1)

        s5 = ctx.enter_context(ExitStack())
        s5p = sb("s5p", [P, 5, GN], F32, s5)
        s5bc = sb("s5bc", [P, 4, GN, GC], F32, s5)
        s5d = sb("s5d", [GC, GN], F32, s5)
        bb = sb("bb", [P, 2, GN, GC], F32, s5)
        pwc = sb("pwc", [P, 2, L + 1, GN], F32, s5)
        pwd = sb("pwd", [P, 2, L, GN], F32, s5)
        ph = sb("ph", [P, 2, GN], F32, s5)
        rho = sb("rho", [P, GN], F32, s5)
        U = sb("U", [P, GN, J], F32, s5)
        CA = sb("CA", [P, 2, QG, L + 1, GC], F32, s5)
        wg = sb("wg", [P, KD, 16], F32, s5)
        gbias = sb("gbias", [16, 1], F32, s5)
        cs = sb("cs", [P, KD, 2], F32, s5)
        mrow = sb("mrow", [H, 2], F32, s5)
        adar = sb("adar", [2, 2, 512], F32, s5)
        zC = spare[0:J, 0:L * SW].rearrange("p (i c) -> p i c", i=L)

        with ExitStack() as st:
            pw = sb("pw", [P, 2, L + 1, GN], F32, st)
            posT = spare[:, 0:KD * LAT].rearrange("p (k t) -> p k t", k=KD)
            t5 = sb("t5", [P, 12, GN], F32, st)
            tmp = sb("tmp", [P, TOK], F32, st)
            tp = sb("tp", [P, 4, 4, GN], F32, st)
            tb = sb("tb", [P, 2, GN, GC], F32, st)
            zero = sb("zero", [P, D], F32, st)
            block = st.enter_context(nc.Block())

            @block.sync
            def _(sp):
                sp.dma_start(par[:], ar["par"]).then_inc(sem("par_in"), 16)
                sp.dma_start(s5p[:], ar["s5p"]).then_inc(sem("s5p_in"), 16)
                load_weights(sp, 1)
                sp.dma_start(consts[:], ar["consts"]).then_inc(sem("consts_in"), 16)
                load_weights(sp, 2)
                sp.dma_start(xT[:], ar["xT"]).then_inc(sem("x_in"), 16)
                sp.dma_start(posT[:], ar["posT"]).then_inc(sem("x_in"), 16)
                load_weights(sp, 3)
                sp.dma_start(s5bc[:], ar["s5bc"]).then_inc(sem("s5bc_in"), 16)
                load_weights(sp, 4)
                sp.dma_start(s5d[:], ar["s5d"]).then_inc(sem("small_in"), 16)
                sp.dma_start(gpar[:], ar["gpar"]).then_inc(sem("small_in"), 16)
                sp.dma_start(gbias[:], ar["gbias"]).then_inc(sem("small_in"), 16)
                sp.dma_start(wg[:], w_in[:, :, C_G:C_G + 16]).then_inc(sem("small_in"), 16)
                load_weights(sp, CH_U + 1)
                sp.wait_ge(sem("small_in"), 64)

            @block.gpsimd
            def _(pool):
                pool.memset(meanw[:], 1.0 / D).then_inc(sem("meanw_set"), 1)
                pool.memset(zero[:], 0.0).then_inc(sem("zero_set"), 1)
                p = chain(pool, "pool")
                pool.wait_ge(sem("s5bc_in"), 16)
                pool.wait_ge(sem("b_factor"), 1)
                wr = bc(t5[:, 7, :].unsqueeze(2), [P, GN, GC])
                wi = bc(t5[:, 8, :].unsqueeze(2), [P, GN, GC])
                pool.tensor_tensor(tb[:, 0], s5bc[:, 0], wr, ALU.mult)
                p(pool.tensor_tensor(tb[:, 1], s5bc[:, 1], wi, ALU.mult))
                p(pool.tensor_tensor(bb[:, 0], tb[:, 0], tb[:, 1], ALU.subtract))
                pool.tensor_tensor(tb[:, 0], s5bc[:, 0], wi, ALU.mult)
                p(pool.tensor_tensor(tb[:, 1], s5bc[:, 1], wr, ALU.mult))
                p(pool.tensor_tensor(bb[:, 1], tb[:, 0], tb[:, 1], ALU.add))
                pool.wait_ge(sem("zero_set"), 1)
                for t in range(NT):
                    pool.dma_start(ar["moe"][t * P:(t + 1) * P, :], zero[:]).then_inc(sem("moe_zero"), 16)
                pool.wait_ge(sem("moe_zero"), 16 * NT)

            @block.scalar
            def _(act):
                a = chain(act, "act")
                act.wait_ge(sem("par_in"), 16)
                act.activation(cs[:].rearrange("p k s -> p (k s)"), par[:, PC_C:PC_C + 16],
                               ACT.Silu).then_inc(sem("c_silu"), 1)
                act.wait_ge(sem("s5p_in"), 16)
                a(act.activation(t5[:, 0, :], s5p[:, 2, :], ACT.Exp))
                act.wait_ge(sem("s5_z"), 1)
                a(act.activation(t5[:, 3, :], t5[:, 1, :], ACT.Exp))
                act.activation(rho[:], t5[:, 1, :], ACT.Exp, scale=float(L)).then_inc(sem("s5_mag"), 1)
                act.wait_ge(sem("s5_angle"), 1)
                a(act.activation(t5[:, 4, :], t5[:, 2, :], ACT.Sin))
                act.activation(t5[:, 5, :], t5[:, 2, :], ACT.Sin, scale=0.5).then_inc(sem("s5_sin"), 1)
                act_ada(act, 0, 0)
                act_ada(act, 1, 1)
                for k in range(KD):
                    act.wait_ge(sem("x_pos"), k + 1)
                    act_square(act, 0, k)
                act_rms(act, 0, tmp)
                act_ada(act, 2, 0)
                act_ada(act, 3, 1)
                act_modulate(act, 0, hT)

            @block.tensor
            def _(pe):
                pe.wait_ge(sem("c_silu"), 1)
                pe.wait_ge(sem("consts_in"), 16)
                pe_ada(pe, 0, 0)
                pe_ada(pe, 1, 1)
                pe.wait_ge(sem("meanw_set"), 1)
                pe_mean_square(pe, 0)
                for c in (2, 3):
                    pe.wait_ge(sem("mod_in"), c - 1)
                    pe_ada(pe, c, c % 2)

            @block.vector
            def _(dve):
                v = chain(dve, "dve")
                dve.wait_ge(sem("s5p_in"), 16)
                dve.wait_ge(sem("order_act"), 1)
                are, aim = s5p[:, 0, :], s5p[:, 1, :]
                v(dve.tensor_tensor(t5[:, 6, :], aim, t5[:, 0, :], ALU.mult))
                dve.tensor_tensor(t5[:, 1, :], are, t5[:, 0, :], ALU.mult).then_inc(sem("s5_z"), 1)
                MAGIC = 1.5 * 2.0 ** 23
                v(dve.tensor_scalar(t5[:, 7, :], t5[:, 6, :], float(1 / (2 * np.pi)), MAGIC, ALU.mult, ALU.add))
                v(dve.tensor_scalar(t5[:, 7, :], t5[:, 7, :], MAGIC, None, ALU.subtract))
                c1 = 6.28125
                c2 = float(np.float32(2 * np.pi - c1))
                c3 = float(np.float32(2 * np.pi - c1 - float(c2)))
                for cc in (c1, c2, c3):
                    v(dve.scalar_tensor_tensor(t5[:, 6, :], t5[:, 7, :], -cc, t5[:, 6, :], ALU.mult, ALU.add))
                dve.tensor_scalar(t5[:, 2, :], t5[:, 6, :], 3.1415925, -3.1415925, ALU.min,
                                  ALU.max).then_inc(sem("s5_angle"), 1)
                dve.wait_ge(sem("s5_mag"), 1)
                dve.wait_ge(sem("s5_sin"), 1)
                v(dve.tensor_tensor(t5[:, 7, :], t5[:, 5, :], t5[:, 5, :], ALU.mult))
                v(dve.tensor_scalar(ph[:, 0, :], t5[:, 7, :], -2.0, 1.0, ALU.mult, ALU.add))
                v(dve.tensor_copy(ph[:, 1, :], t5[:, 4, :]))
                v(dve.tensor_tensor(pw[:, 0, 1, :], t5[:, 3, :], ph[:, 0, :], ALU.mult))
                v(dve.tensor_tensor(pw[:, 1, 1, :], t5[:, 3, :], ph[:, 1, :], ALU.mult))
                v(dve.memset(pw[:, 0, 0, :], 1.0))
                v(dve.memset(pw[:, 1, 0, :], 0.0))

                def cmul(dr, di, ar_, ai_, br_, bi_, t):
                    dve.tensor_tensor(t[0], ar_, br_, ALU.mult)
                    dve.tensor_tensor(t[1], ai_, bi_, ALU.mult)
                    dve.tensor_tensor(t[2], ar_, bi_, ALU.mult)
                    v(dve.tensor_tensor(t[3], ai_, br_, ALU.mult))
                    dve.tensor_tensor(dr, t[0], t[1], ALU.subtract)
                    v(dve.tensor_tensor(di, t[2], t[3], ALU.add))

                def t4(n):
                    return [tp[:, x, 0:n, :] for x in range(4)]

                for _ in range(3):
                    cmul(ph[:, 0, :], ph[:, 1, :], ph[:, 0, :], ph[:, 1, :], ph[:, 0, :], ph[:, 1, :],
                         [tp[:, x, 0, :] for x in range(4)])
                for m in (1, 2, 4):
                    cmul(pw[:, 0, m + 1:2 * m + 1, :], pw[:, 1, m + 1:2 * m + 1, :],
                         pw[:, 0, 1:m + 1, :], pw[:, 1, 1:m + 1, :],
                         bc(pw[:, 0, m:m + 1, :], [P, m, GN]), bc(pw[:, 1, m:m + 1, :], [P, m, GN]), t4(m))
                F, B = slice(0, SP_), slice(SP_, P)
                for r in range(2):
                    v(dve.tensor_copy(pwc[F, r, :, :], pw[F, r, :, :]))
                    v(dve.tensor_copy(pwc[B, r, :, :], pw[B, r, ::-1, :]))
                    v(dve.tensor_copy(pwd[F, r, :, :], pw[F, r, L - 1::-1, :]))
                    v(dve.tensor_copy(pwd[B, r, :, :], pw[B, r, 0:L, :]))
                v(dve.tensor_tensor(t5[:, 8, :], are, are, ALU.mult))
                v(dve.tensor_tensor(t5[:, 9, :], aim, aim, ALU.mult))
                v(dve.tensor_tensor(t5[:, 8, :], t5[:, 8, :], t5[:, 9, :], ALU.add))
                v(dve.reciprocal(t5[:, 8, :], t5[:, 8, :]))
                v(dve.tensor_tensor(t5[:, 9, :], are, t5[:, 8, :], ALU.mult))
                v(dve.scalar_tensor_tensor(t5[:, 10, :], aim, -1.0, t5[:, 8, :], ALU.mult, ALU.mult))
                v(dve.tensor_scalar(t5[:, 11, :], pw[:, 0, 1, :], 1.0, None, ALU.subtract))
                cmul(t5[:, 6, :], t5[:, 2, :], t5[:, 11, :], pw[:, 1, 1, :], t5[:, 9, :], t5[:, 10, :],
                     [tp[:, x, 0, :] for x in range(4)])
                dve.tensor_copy(t5[:, 7, :], t5[:, 6, :])
                dve.tensor_copy(t5[:, 8, :], t5[:, 2, :]).then_inc(sem("b_factor"), 1)
                dve_ada(dve, 0, 0)
                dve_ada(dve, 1, 1)
                dve.wait_ge(sem("x_in"), 32)
                for k in range(KD):
                    dve.tensor_tensor(xT[:, k, 0:LAT], xT[:, k, 0:LAT], posT[:, k], ALU.add).then_inc(sem("x_pos"), 1)
                dve_inverse_mean(dve, v, 0, tmp)
                dve_ada(dve, 2, 0)
                dve_ada(dve, 3, 1)
                dve.wait_ge(sem("mod_in"), 4)
                dve_gain(dve, 0, PC_NMIX).then_inc(sem("gain_ready"), 1)
                dve_normalise(dve, 0)

        CB = W[:, 0, 0:2048].rearrange("p (r g x) -> p r g x", r=2, g=QG)
        CT = W[:, 0, 2048:4096].rearrange("p (r g x) -> p r g x", r=2, g=QG)
        t8 = hbT[:].rearrange("p a b -> p (a b)")[:, 0:2 * QG * (L + 1) * GC].rearrange("p (x g m) -> p x g m", x=2, g=QG)

        ud = ar["u"].rearrange("(m g c) (i j) -> m i c g j", m=4, c=GC, i=L)

        def turn_u(sp, m):
            sp.wait_ge(sem("u_copied"), m + 1)
            sp.dma_start(ar["u"][m * P:(m + 1) * P, :], sq[:, m % 2, :]).then_inc(sem(f"u_out{m % 2}"), 16)
            sp.wait_ge(sem(f"u_out{m % 2}"), 16 * (m // 2 + 1))
            for i in range(L):
                sp.dma_start(U[GC * i:GC * i + GC, QG * m:QG * m + QG, :], ud[m, i]).then_inc(sem(f"u_in{m}"), 16)

        def pool_coefficients(pool, q):
            p = chain(pool, "pool")
            g = slice(QG * q, QG * q + QG)
            s = [P, QG, L, GC]
            if q:
                pool.wait_ge(sem("cb_turned"), 4 * q)
            pr, pi = (bc(pwd[:, r, :, g].rearrange("p i g -> p g i").unsqueeze(3), s) for r in range(2))
            br, bi = (bc(bb[:, r, g, :].unsqueeze(2), s) for r in range(2))
            ta, tb_ = (t8[:, x, :, 0:P].rearrange("p g (i c) -> p g i c", c=GC) for x in range(2))
            cr, ci = (CB[:, r].rearrange("p g (i c) -> p g i c", c=GC) for r in range(2))
            pool.tensor_tensor(ta, pr, br, ALU.mult)
            p(pool.tensor_tensor(tb_, pi, bi, ALU.mult))
            p(pool.tensor_tensor(cr, ta, tb_, ALU.subtract))
            pool.tensor_tensor(ta, pr, bi, ALU.mult)
            p(pool.tensor_tensor(tb_, pi, br, ALU.mult))
            pool.tensor_tensor(ci, ta, tb_, ALU.add).then_inc(sem("cb_ready"), 1)
            pool.wait_ge(sem("cb_ready"), q + 1)
            s = [P, QG, L + 1, GC]
            pr, pi = (bc(pwc[:, r, :, g].rearrange("p i g -> p g i").unsqueeze(3), s) for r in range(2))
            br, bi = (bc(s5bc[:, 2 + r, g, :].unsqueeze(2), s) for r in range(2))
            ta, tb_ = (t8[:, x].rearrange("p g (i c) -> p g i c", c=GC) for x in range(2))
            pool.tensor_tensor(ta, pr, br, ALU.mult)
            p(pool.tensor_tensor(tb_, pi, bi, ALU.mult))
            if q:
                pool.wait_ge(sem("s5_lag_done"), 4 * q)
                pool.wait_ge(sem("cao_ready"), q)
            p(pool.tensor_tensor(CA[:, 0], ta, tb_, ALU.subtract))
            pool.tensor_tensor(ta, pr, bi, ALU.mult)
            p(pool.tensor_tensor(tb_, pi, br, ALU.mult))
            p(pool.tensor_tensor(CA[:, 1], ta, tb_, ALU.add))
            pool.tensor_scalar(CA[:, 1], CA[:, 1], -1.0, 1.0, ALU.mult, ALU.mult).then_inc(sem("ca_ready"), 1)
            pool.wait_ge(sem("ca_ready"), q + 1)

        with ExitStack() as st:
            g16 = sb("g16", [16, TOK], F32, st)
            G = W[0:H, 2, 0:4 * TOK].rearrange("h (g t) -> h g t", g=4)
            gt = W[0:H, 2, 4 * TOK:6 * TOK].rearrange("h (g t) -> h g t", g=2)
            lf = sb("lf", [H, 2, TOK], F32, st)
            cum = sb("cum", [H, 2, TOK], F32, st)
            R = zC[:].rearrange("p a b -> p (a b)")[0:H, 0:6 * TOK].rearrange("h (x t) -> h x t", x=6)
            uF = sq
            Mx = sb("Mx", [H, 2, TOK], F32, st)
            ones4 = sb("ones4", [H, TOK], F32, st)
            block = st.enter_context(nc.Block())

            @block.sync
            def _(sp):
                sp.wait_ge(sem("gates_copied"), 2)
                for g in range(4):
                    sp.dma_start(G[:, g, :], g16[H * g:H * g + H, :]).then_inc(sem("gates_turned"), 16)
                for m in range(3):
                    turn_u(sp, m)
                load_weights(sp, CH_A + 1)

            @block.gpsimd
            def _(pool):
                pool_coefficients(pool, 0)

            @block.tensor
            def _(pe):
                for k in range(KD):
                    pe.matmul(PS[0][0:16, :], wg[:, k, :], hT[:, k, 0:LAT], start=(k == 0), stop=(k == 7))
                    mm = pe.matmul(PS[1][0:16, 0:CTX], wg[:, k, :], hT[:, k, LAT:TOK], start=(k == 0), stop=(k == 7))
                mm.then_inc(sem("gates_done"), 1)
                have_weights(pe, CH_U)
                for m in range(4):
                    if m >= 2:
                        pe.wait_ge(sem("u_copied"), m - 1)
                    for k in range(KD):
                        w = wslot(CH_U)[:, k, m * P:(m + 1) * P]
                        pe.matmul(PS[2 + m % 2][:, :], w, hT[:, k, 0:LAT], start=(k == 0), stop=(k == 7))
                        mm = pe.matmul(PS[4 + m % 2][:, 0:CTX], w, hT[:, k, LAT:TOK], start=(k == 0), stop=(k == 7))
                    mm.then_inc(sem("u_done"), 1)
                pe.wait_ge(sem("rows_ready"), 1)
                for t in range(NT):
                    for x in range(6):
                        if t < 4 or x not in (2, 3):
                            c = (t * 6 + x) * H
                            mm = pe.transpose(PS[6][:, c:c + H], R[:, x, t * P:(t + 1) * P], ident[0:H, 0:H])
                mm.then_inc(sem("rows_turned"), 1)

            @block.scalar
            def _(act):
                a = chain(act, "act")
                act.wait_ge(sem("gate_abs"), 1)
                a(act.activation(gt, gt, ACT.Exp, scale=-1.0))
                act.activation(gt, gt, ACT.Ln, bias=1.0).then_inc(sem("gate_ln"), 1)

                def out_u(m):
                    act.wait_ge(sem("u_done"), m + 1)
                    if m >= 2:
                        act.wait_ge(sem(f"u_out{m % 2}"), 16)
                    dst = uF[:, m % 2, :].rearrange("p (i j) -> p j i", i=L)
                    act.activation(dst[:, 0:JL, :], PS[2 + m % 2][:, :].rearrange("p (j i) -> p j i", i=L), ACT.Copy)
                    act.activation(dst[:, JL:J, :], PS[4 + m % 2][:, 0:CTX].rearrange("p (j i) -> p j i", i=L),
                                   ACT.Copy).then_inc(sem("u_copied"), 1)

                for m in range(3):
                    out_u(m)
                act.wait_ge(sem("m_ready"), 1)
                for d in range(2):
                    act.activation(R[:, 2 + d, 0:LAT], Mx[:, d, 0:LAT], ACT.Exp, scale=-1.0, bias=gpar[:, 4 + d:5 + d])
                    ins = act.activation(R[:, 4 + d, :], cum[:, d, :], ACT.Exp, scale=-1.0)
                ins.then_inc(sem("rows_ready"), 1)
                out_u(3)

            @block.vector
            def _(dve):
                v = chain(dve, "dve")
                dve.wait_ge(sem("gates_done"), 1)
                dve.tensor_scalar(g16[:, 0:LAT], PS[0][0:16, :], gbias[:, 0:1], None, ALU.add
                                  ).then_inc(sem("gates_copied"), 1)
                dve.tensor_scalar(g16[:, LAT:TOK], PS[1][0:16, 0:CTX], gbias[:, 0:1], None, ALU.add
                                  ).then_inc(sem("gates_copied"), 1)
                v(dve.memset(ones4[:], 1.0))
                dve.wait_ge(sem("gates_turned"), 64)
                x = G[:, 1:4:2, :]
                dve.scalar_tensor_tensor(gt, x, -1.0, x, ALU.mult, ALU.max).then_inc(sem("gate_abs"), 1)
                dve.wait_ge(sem("gate_ln"), 1)
                v(dve.scalar_tensor_tensor(lf[:], x, 0.0, gt, ALU.min, ALU.subtract))

                def part(tile, d, s):
                    ap = tile[:, d, 0:LAT] if s == 0 else tile[:, d, LAT:TOK]
                    return ap[:, ::-1] if d else ap

                for d in range(2):
                    for s in range(2):
                        n = LAT if s == 0 else CTX
                        v(dve.tensor_tensor_scan(part(cum, d, s), ones4[:, 0:n], part(lf, d, s), 0.0,
                                                 ALU.mult, ALU.add))
                v(dve.tensor_tensor(R[:, 0:2, :], G[:, 0:4:2, :], cum[:], ALU.subtract))
                for d in range(2):
                    for s in range(2):
                        v(dve.tensor_tensor_scan(part(Mx, d, s), part(R, d, s), part(R, d, s),
                                                 gpar[:, 4 + d:5 + d] if s == 0 else 0.0, ALU.max, ALU.max))
                v(dve.tensor_scalar(negM[:], Mx[:], -1.0, None, ALU.mult))
                v(dve.tensor_tensor(cum[:], cum[:], Mx[:], ALU.add))
                v(dve.tensor_copy(mrow[:, 0:1], cum[:, 0, TOK - 1:TOK]))
                dve.tensor_copy(mrow[:, 1:2], cum[:, 1, LAT:LAT + 1]).then_inc(sem("m_ready"), 1)
                dve.wait_ge(sem("rows_turned"), 1)
                c4 = PS[6][:, 0:NT * 24].rearrange("p (t x h) -> p t x h", t=NT, x=6)
                dve.tensor_copy(colT[:, 0:4], c4[:, 0:4])
                dve.tensor_copy(colT[:, 4, 0:2], c4[:, 4, 0:2])
                dve.tensor_copy(colT[:, 4, 4:6], c4[:, 4, 4:6])

        with ExitStack() as st:
            n3 = 2 * QG * NS_
            Et, V, Z = (W[:, 2, x * n3:(x + 1) * n3].rearrange("p (r g n) -> p r g n", r=2, g=QG) for x in range(3))
            Xp = sq[:].rearrange("p a b -> p (a b)").rearrange("p (r g j) -> p r g j", r=2, g=QG)
            CAo = spare[:, 4096:6144].rearrange("p (r g x) -> p r g x", r=2, g=QG)
            bbz = sb("bbz", [P, 2, 2, QG, GC], F32, st)
            Kt = sb("Kt", [GC, QG, (2 * L - 1) * GC], F32, st)
            kd = sb("kd", [GC, QG, GC], F32, st)
            T = sb("T", [P, QG, P], F32, st)
            rt = sb("rt", [P, QG, NS_], F32, st)
            tz = sb("tz", [P, 4, QG, NS_], F32, st)
            xfin = sb("xfin", [P, 2, GN], F32, st)
            F, B = slice(0, SP_), slice(SP_, P)
            block = st.enter_context(nc.Block())

            @block.sync
            def _(sp):
                turn_u(sp, 3)
                sp.wait_ge(sem("m_ready"), 1)
                with nc.allow_non_contiguous_dma(reason="eight values"):
                    sp.dma_start(out["m"].rearrange("d h -> h d"), mrow[:]).then_inc(sem("m_out"), 16)
                sp.wait_ge(sem("m_out"), 16)
                for q in range(NQ):
                    sp.wait_ge(sem("lags_ready"), q + 1)
                    if q:
                        sp.wait_ge(sem("s5_y_done"), 2 * q)
                    for i in range(L):
                        sp.dma_start(T[GC * i:GC * i + GC, :, :],
                                     Kt[:, :, (L - 1 - i) * GC:(2 * L - 1 - i) * GC]).then_inc(sem("toeplitz_in"), 16)
                    load_weights(sp, CH_A + 2 * q + 3)
                sp.wait_ge(sem("xfin_ready"), NQ)
                for r in range(2):
                    sp.dma_start(out["s5"][r], xfin[:, r, :]).then_inc(sem("s5_out"), 16)
                sp.wait_ge(sem("s5_out"), 32)

            @block.gpsimd
            def _(pool):
                for q in range(1, NQ):
                    pool_coefficients(pool, q)

            @block.tensor
            def _(pe):
                def additions(q):
                    pe.wait_ge(sem("cb_ready"), q + 1)
                    pe.wait_ge(sem(f"u_in{q}"), 16 * L)
                    if q:
                        pe.wait_ge(sem("v_copied"), 4 * q)
                    for r in range(2):
                        for g in range(QG):
                            mm = pe.transpose(PS[2 + 2 * r + g // 4][:, (g % 4) * P:(g % 4 + 1) * P], CB[:, r, g, :],
                                              ident)
                            if g % 4 == 3:
                                mm.then_inc(sem("cb_turned"), 1)
                    for r in range(2):
                        for g in range(QG):
                            if g % 4 == 0:
                                pe.wait_ge(sem("ct_copied"), 4 * q + 2 * r + g // 4 + 1)
                            mm = pe.matmul(PS[2 + 2 * r + g // 4][:, (g % 4) * J:(g % 4 + 1) * J], CT[:, r, g, :],
                                           U[:, QG * q + g, :], start=True, stop=True)
                            if g % 4 == 3:
                                mm.then_inc(sem("s5_v_done"), 1)

                def lags(q):
                    pe.wait_ge(sem("ca_ready"), q + 1)
                    pe.wait_ge(sem("bbz_ready"), q + 1)
                    if q:
                        pe.wait_ge(sem("mod_in"), 4 + 2 * q)
                    FW, BW = (L - 1) * GC, 0
                    for g in range(QG):
                        n = 4 * q + g // 2
                        bank = 6 + n % 2
                        if g % 2 == 0 and n >= 2:
                            pe.wait_ge(sem("lags_copied"), n - 1)
                        o = (g % 2) * (2 * L - 1) * GC
                        k = 0
                        for d, (at, m0) in enumerate(((FW, 0), (BW, 1))):
                            for r in range(2):
                                mm = pe.matmul(PS[bank][0:GC, o + at:o + at + P], bbz[:, d, r, g, :],
                                               CA[:, r, g, m0:m0 + L, :], start=(k == 0 and g % 2 == 0), stop=(k == 3),
                                               skip_group_check=True)
                                k += 1
                        if g % 2 == 1:
                            mm.then_inc(sem("s5_lag_done"), 1)

                def outputs(q):
                    pe.wait_ge(sem("xp_copied"), q + 1)
                    pe.wait_ge(sem("cao_ready"), q + 1)
                    pe.wait_ge(sem("toeplitz_in"), 128 * (q + 1))
                    if q:
                        pe.wait_ge(sem("z_copied"), 2 * q)
                    for g in range(QG):
                        dst = PS[g // 4][0:J, (g % 4) * P:(g % 4 + 1) * P]
                        pe.matmul(dst, U[:, QG * q + g, :], T[:, g, :], start=True, stop=False)
                        for r in range(2):
                            mm = pe.matmul(dst, Xp[:, r, g, :], CAo[:, r, g, :], start=False, stop=(r == 1))
                        if g % 4 == 3:
                            mm.then_inc(sem("s5_y_done"), 1)

                additions(0)
                for q in range(NQ):
                    lags(q)
                    if q + 1 < NQ:
                        additions(q + 1)
                    pe.wait_ge(sem("lags_copied"), 4 * q + 4)
                    pe_ada(pe, 4 + 2 * q, 7)
                    outputs(q)
                    pe.wait_ge(sem("mod_in"), 5 + 2 * q)
                    pe_ada(pe, 5 + 2 * q, 7)

            @block.scalar
            def _(act):
                def turned_coefficients(q):
                    for b in range(4):
                        act.wait_ge(sem("cb_turned"), 4 * q + b + 1)
                        act.activation(CT[:, b // 2, 4 * (b % 2):4 * (b % 2) + 4, :].rearrange("p g j -> p (g j)"),
                                       PS[2 + b][:], ACT.Copy).then_inc(sem("ct_copied"), 1)

                def additions(q):
                    if q:
                        act.wait_ge(sem("xp_copied"), q)
                    for r in range(2):
                        for b in range(2):
                            act.wait_ge(sem("s5_v_done"), 4 * q + 2 * r + b + 1)
                            src = PS[2 + 2 * r + b][:, 0:4 * J].rearrange("p (g j) -> p g j", g=4)
                            gg = slice(4 * b, 4 * b + 4)
                            act.activation(V[F, r, gg, 1:JL + 1], src[F, :, 0:JL], ACT.Copy)
                            act.activation(V[F, r, gg, JL + 2:NS_], src[F, :, JL:J], ACT.Copy)
                            act.activation(V[B, r, gg, 1:JL + 1], src[B, :, 0:JL][:, :, ::-1], ACT.Copy)
                            act.activation(V[B, r, gg, JL + 2:NS_], src[B, :, JL:J][:, :, ::-1],
                                           ACT.Copy).then_inc(sem("v_copied"), 1)

                turned_coefficients(0)
                additions(0)
                for q in range(NQ):
                    for b in range(4):
                        act.wait_ge(sem("s5_lag_done"), 4 * q + b + 1)
                        if q and b == 0:
                            act.wait_ge(sem("toeplitz_in"), 128 * q)
                        act.activation(Kt[:, 2 * b:2 * b + 2, :].rearrange("p g x -> p (g x)"),
                                       PS[6 + b % 2][0:GC, 0:2 * (2 * L - 1) * GC],
                                       ACT.Copy).then_inc(sem("lags_copied"), 1)
                    act.wait_ge(sem("ca_ready"), q + 1)
                    if q:
                        act.wait_ge(sem("s5_y_done"), 2 * q)
                    for r in range(2):
                        dst = CAo[:, r].rearrange("p g (i c) -> p g i c", c=GC)
                        act.activation(dst[F], CA[F, r, :, 1:L + 1, :], ACT.Copy)
                        ins = act.activation(dst[B], CA[B, r, :, 0:L, :], ACT.Copy)
                    ins.then_inc(sem("cao_ready"), 1)
                    if q + 1 < NQ:
                        turned_coefficients(q + 1)
                    act_ada(act, 4 + 2 * q, 7)
                    if q + 1 < NQ:
                        additions(q + 1)
                    for b in range(2):
                        act.wait_ge(sem("s5_y_done"), 2 * q + b + 1)
                        c0 = (QG * q + 4 * b) * GC
                        act.activation(zC[:, :, c0:c0 + 4 * GC].rearrange("p i (g c) -> p g i c", c=GC),
                                       PS[b][0:J, :].rearrange("p (g i c) -> p g i c", g=4, i=L),
                                       ACT.Copy).then_inc(sem("z_copied"), 1)
                    act_ada(act, 5 + 2 * q, 7)

            @block.vector
            def _(dve):
                v = chain(dve, "dve")
                cx = slice(JL + 1, NS_)
                v(dve.memset(bbz[:], 0.0))
                for q in range(NQ):
                    g = slice(QG * q, QG * q + QG)
                    if q:
                        dve.wait_ge(sem("s5_lag_done"), 4 * q)
                    for d, own in enumerate((F, B)):
                        for r in range(2):
                            ins = dve.tensor_copy(bbz[own, d, r], bb[own, r, g, :])
                    ins.then_inc(sem("bbz_ready"), 1)
                    v(dve.memset(Et[:, 0, :, 0:1], 1.0))
                    v(dve.memset(Et[:, 1, :, 0:1], 0.0))
                    for r in range(2):
                        v(dve.tensor_copy(Et[:, r, :, 1:2], ph[:, r, g].unsqueeze(2)))
                    m = 1
                    while m < JL:
                        x, y = slice(1, m + 1), slice(m + 1, 2 * m + 1)
                        er, ei = (bc(Et[:, r, :, m:m + 1], [P, QG, m]) for r in range(2))
                        dve.tensor_tensor(tz[:, 0, :, 0:m], Et[:, 0, :, x], er, ALU.mult)
                        dve.tensor_tensor(tz[:, 1, :, 0:m], Et[:, 1, :, x], ei, ALU.mult)
                        dve.tensor_tensor(tz[:, 2, :, 0:m], Et[:, 0, :, x], ei, ALU.mult)
                        v(dve.tensor_tensor(tz[:, 3, :, 0:m], Et[:, 1, :, x], er, ALU.mult))
                        dve.tensor_tensor(Et[:, 0, :, y], tz[:, 0, :, 0:m], tz[:, 1, :, 0:m], ALU.subtract)
                        v(dve.tensor_tensor(Et[:, 1, :, y], tz[:, 2, :, 0:m], tz[:, 3, :, 0:m], ALU.add))
                        m *= 2
                    v(dve.tensor_copy(Et[:, :, :, cx], Et[:, :, :, 0:JC + 1]))
                    v(dve.tensor_copy(rt[:], bc(rho[:, g].unsqueeze(2), [P, QG, NS_])))
                    v(dve.memset(rt[:, :, 0:1], 0.0))
                    v(dve.memset(rt[:, :, JL + 1:JL + 2], 0.0))
                    for r in range(2):
                        v(dve.tensor_copy(V[:, r, :, 0:1], s5p[:, 3 + r, g].unsqueeze(2)))
                        v(dve.memset(V[:, r, :, JL + 1:JL + 2], 0.0))
                    v(dve.tensor_tensor(kd[:], bc(s5d[:, g].unsqueeze(2), [GC, QG, GC]),
                                        bc(ident[0:GC, 0:GC].unsqueeze(1), [GC, QG, GC]), ALU.mult))
                    if q:
                        dve_ada(dve, 3 + 2 * q, 7)
                    dve.wait_ge(sem("lags_copied"), 4 * q + 4)
                    k0 = Kt[:, :, (L - 1) * GC:L * GC]
                    dve.tensor_tensor(k0, k0, kd[:], ALU.add).then_inc(sem("lags_ready"), 1)
                    dve.wait_ge(sem("v_copied"), 4 * q + 4)
                    dve.tensor_tensor(tz[:, 0], V[:, 0], Et[:, 0], ALU.mult)
                    dve.tensor_tensor(tz[:, 1], V[:, 1], Et[:, 1], ALU.mult)
                    dve.tensor_tensor(tz[:, 2], V[:, 1], Et[:, 0], ALU.mult)
                    v(dve.tensor_tensor(tz[:, 3], V[:, 0], Et[:, 1], ALU.mult))
                    dve.tensor_tensor(V[:, 0], tz[:, 0], tz[:, 1], ALU.add)
                    v(dve.tensor_tensor(V[:, 1], tz[:, 2], tz[:, 3], ALU.subtract))
                    for r in range(2):
                        v(dve.tensor_tensor_scan(Z[:, r].rearrange("p g n -> p (g n)"),
                                                 rt[:].rearrange("p g n -> p (g n)"),
                                                 V[:, r].rearrange("p g n -> p (g n)"), 0.0, ALU.mult, ALU.add))
                    dve.tensor_tensor(tz[:, 0], Z[:, 0], Et[:, 0], ALU.mult)
                    dve.tensor_tensor(tz[:, 1], Z[:, 1], Et[:, 1], ALU.mult)
                    dve.tensor_tensor(tz[:, 2], Z[:, 1], Et[:, 0], ALU.mult)
                    v(dve.tensor_tensor(tz[:, 3], Z[:, 0], Et[:, 1], ALU.mult))
                    dve.tensor_tensor(V[:, 0], tz[:, 0], tz[:, 1], ALU.subtract)
                    v(dve.tensor_tensor(V[:, 1], tz[:, 2], tz[:, 3], ALU.add))
                    dve.tensor_copy(xfin[:, :, g], V[:, :, :, NS_ - 1]).then_inc(sem("xfin_ready"), 1)
                    if q:
                        dve.wait_ge(sem("s5_y_done"), 2 * q)
                    else:
                        dve.wait_ge(sem("u_out1"), 32)
                    for r in range(2):
                        dve.tensor_copy(Xp[F, r, :, 0:JL], V[F, r, :, 0:JL])
                        dve.tensor_copy(Xp[F, r, :, JL:J], V[F, r, :, JL + 1:NS_ - 1])
                        dve.tensor_copy(Xp[B, r, :, 0:JL], V[B, r, :, 0:JL][:, :, ::-1])
                        ins = dve.tensor_copy(Xp[B, r, :, JL:J], V[B, r, :, JL + 1:NS_ - 1][:, :, ::-1])
                    ins.then_inc(sem("xp_copied"), 1)
                    dve_ada(dve, 4 + 2 * q, 7)
                dve_ada(dve, 11, 7)

        with ExitStack() as st:
            zT = sb("zT", [P, 4, TOK], F32, st)
            gz = sb("gz", [P, 4, TOK], F32, st)
            sg = sb("sg", [P, 2, TOK], F32, st)
            wgl = spare[:, 4096:6144].rearrange("p (k n) -> p k n", k=4)
            block = st.enter_context(nc.Block())

            @block.sync
            def _(sp):
                sp.dma_start(wgl[:], w_glu).then_inc(sem("wglu_in"), 16)
                load_weights(sp, CH_H + NSLOT)

            @block.tensor
            def _(pe):
                for b in range(8):
                    if b >= 4:
                        pe.wait_ge(sem("z_in"), b - 3)
                    for i in range(4):
                        mm = pe.transpose(PS[b % 4][:, i * J:(i + 1) * J],
                                          zC[:, 4 * (b % 2) + i, (b // 2) * P:(b // 2 + 1) * P], ident[0:J, 0:J])
                    mm.then_inc(sem("z_turned"), 1)
                pe.wait_ge(sem("wglu_in"), 16)
                pe.wait_ge(sem("z_in"), 8)
                for m in range(4):
                    if m >= 2:
                        pe.wait_ge(sem("glu_sig"), m - 1)
                    for k in range(4):
                        w = wgl[:, k, m * P:(m + 1) * P]
                        pe.matmul(PS[4 + m % 2][:, :], w, zT[:, k, 0:LAT], start=(k == 0), stop=(k == 3))
                        mm = pe.matmul(PS[6 + m % 2][:, 0:CTX], w, zT[:, k, LAT:TOK], start=(k == 0), stop=(k == 3))
                    mm.then_inc(sem("glu_done"), 1)

            @block.scalar
            def _(act):
                act.wait_ge(sem("z_in"), 8)
                for m in range(4):
                    act.activation(gz[:, m, :], zT[:, m, :], ACT.Gelu_apprx_tanh).then_inc(sem("gelu"), 1)
                for m in range(4):
                    act.wait_ge(sem("glu_done"), m + 1)
                    if m >= 2:
                        act.wait_ge(sem("hb_ready"), m - 1)
                    b = par[:, PC_BGLU + m:PC_BGLU + m + 1]
                    act.activation(sg[:, m % 2, 0:LAT], PS[4 + m % 2][:, :], ACT.Sigmoid, bias=b)
                    act.activation(sg[:, m % 2, LAT:TOK], PS[6 + m % 2][:, 0:CTX], ACT.Sigmoid,
                                   bias=b).then_inc(sem("glu_sig"), 1)

            @block.vector
            def _(dve):
                for b in range(8):
                    dve.wait_ge(sem("z_turned"), b + 1)
                    dst = zT[:, b // 2, :].rearrange("p (j i) -> p i j", i=L)[:, 4 * (b % 2):4 * (b % 2) + 4, :]
                    dve.tensor_copy(dst, PS[b % 4][:, 0:4 * J].rearrange("p (i j) -> p i j", i=4)
                                    ).then_inc(sem("z_in"), 1)
                dve.wait_ge(sem("gelu"), 4)
                for m in range(4):
                    dve.wait_ge(sem("glu_sig"), m + 1)
                    dve.tensor_tensor(hbT[:, m, :], gz[:, m, :], sg[:, m % 2, :], ALU.mult).then_inc(sem("hb_ready"), 1)

        s5.close()

        haT = spare[:, 0:KD * TOK].rearrange("p (k t) -> p k t", k=KD)
        with ExitStack() as st:
            qk = sb("qk", [P, 2, 4, TOK], F32, st)
            vt = sb("vt", [P, 2, NT, DH + 1], F32, st)
            og = sb("og", [P, 2, NT, DH], F32, st)
            PW = LAT * 5 // 2 + CTX
            Pm = sb("Pm", [P, 2, PW], F32, st)
            negMd = sq
            Qs = rsb[:, 0:2 * (DH + 1)].rearrange("p (b n) -> p b n", b=2)
            nd = sb("nd", [P, 2, DH + 1], F32, st)
            rr = sb("rr", [P, 2], F32, st)
            hacc = sb("hacc", [P, NT, DH], F32, st)
            junk = sb("junk", [P, DH], F32, st)
            ssq = sb("ssq", [P, NT], F32, st)
            rs5 = sb("rs5", [P, NT], F32, st)
            C0 = sb("C0", [P, 4, DH + 1], F32, st)
            wk = sb("wk", [P, 2], F32, st)
            kw = spare[:, KD * TOK:KD * TOK + 2 * DH].rearrange("p (d n) -> p d n", d=2)
            Co = sb("Co", [P, 4, DH + 1], F32, st)
            selH = spare[0:H, KD * TOK + 2 * DH:KD * TOK + 2 * DH + H * P].rearrange("p (h n) -> p h n", h=H)
            block = st.enter_context(nc.Block())
            Cn = ar["Cn"].rearrange("d h (k p) n -> h d p k n", p=P)
            Cout = out["Cn"].rearrange("d h (k p) n -> h d p k n", p=P)
            OFF = {0: [0, 512, 896, 1152], 1: [0, 128, 384, 768]}

            @block.sync
            def _(sp):
                for h in range(H):
                    if h:
                        sp.wait_ge(sem("pv_done"), 10 * h)
                    for d in range(2):
                        sp.dma_start(C0[:, 2 * d:2 * d + 2, :], Cn[h, d]).then_inc(sem("c0_in"), 16)
                    load_weights(sp, CH_H + 2 * h + 4)
                load_weights(sp, CH_M + NSLOT)

            @block.gpsimd
            def _(pool):
                for h in range(H):
                    pool.wait_ge(sem("co_ready"), 4 * (h + 1))
                    for d in range(2):
                        pool.dma_start(Cout[h, d], Co[:, 2 * d:2 * d + 2, :]).then_inc(sem("c_out"), 16)
                pool.wait_ge(sem("c_out"), 32 * H)

            @block.tensor
            def _(pe):
                def proj_wait(u):
                    if u >= 2:
                        pe.wait_ge(sem("proj_copied"), u - 1 + (u - 2 + 5) // 9)

                def proj_qk(h):
                    c = CH_H + 2 * h
                    have_weights(pe, c)
                    for m in range(4):
                        u = 9 * h + m
                        proj_wait(u)
                        for k in range(KD):
                            w = wslot(c)[:, k, m * P:(m + 1) * P]
                            mm = pe.matmul(PS[u % 2][:, :], w, hT[:, k, 0:LAT], start=(k == 0), stop=(k == 7))
                        mm.then_inc(sem("qk_done"), 1)
                    for m in range(4):
                        for k in range(KD):
                            mm = pe.matmul(PS[2][:, m * P:(m + 1) * P], wslot(c)[:, k, m * P:(m + 1) * P],
                                           hT[:, k, LAT:TOK], start=(k == 0), stop=(k == 7))
                    mm.then_inc(sem("qk_done"), 1)

                def proj_vo(h):
                    c = CH_H + 2 * h + 1
                    have_weights(pe, c)
                    for t in range(NT):
                        u = 9 * h + 4 + t
                        proj_wait(u)
                        for k in range(KD):
                            mm = pe.matmul(PS[u % 2][:, :], hT[:, k, t * P:(t + 1) * P], wslot(c)[:, k, :],
                                           start=(k == 0), stop=(k == 7))
                        mm.then_inc(sem("vo_done"), 1)

                def scores(h):
                    b = h % 2
                    if h:
                        pe.wait_ge(sem("co_ready"), 4 * h)
                        pe.wait_ge(sem("ha_ready"), 3 * h)
                    else:
                        pe.wait_ge(sem("sel_ready"), 1)
                    for d in range(2):
                        pe.matmul(PS[3 + d][:, :], selH[:, h, :], negM[:, d, 0:LAT], start=True, stop=True)
                        mm = pe.matmul(PS[5][:, d * P:(d + 1) * P], selH[:, h, :], negM[:, d, LAT:TOK], start=True,
                                       stop=True)
                    mm.then_inc(sem("m_spread"), 1)
                    pe.wait_ge(sem("proj_copied"), 10 * h + 5)
                    for s in range(NT):
                        if s == 4:
                            pe.wait_ge(sem("negmd_ready"), h + 1)
                        if 2 <= s < 4:
                            pe.wait_ge(sem("p_ready"), NT * h + s - 1)
                        for k in range(2):
                            if s < 4:
                                mm = pe.matmul(PS[6 + s % 2][:, :], qk[:, b, 2 + k, s * P:(s + 1) * P],
                                               qk[:, b, k, 0:LAT], start=(k == 0), stop=(k == 1))
                            else:
                                mm = pe.matmul(PS[5][:, 2 * P:3 * P], qk[:, b, 2 + k, LAT:TOK],
                                               qk[:, b, k, LAT:TOK], start=(k == 0), stop=(k == 1))
                        mm.then_inc(sem("scores_done"), 1)

                def values(h):
                    b = h % 2
                    pe.wait_ge(sem("p_ready"), NT * (h + 1))
                    pe.wait_ge(sem("proj_copied"), 10 * h + 10)
                    if h == 0:
                        pe.wait_ge(sem("ones_set"), 1)
                    pe.wait_ge(sem("c0_in"), 32 * (h + 1))
                    for n in range(10):
                        t, d = n // 2, n % 2
                        if n >= 2:
                            pe.wait_ge(sem("nd_ready"), 10 * h + n - 1)
                        if t < 4:
                            for k in range(2):
                                pe.matmul(PS[6 + d][:, 0:DH + 1], qk[:, b, k, t * P:(t + 1) * P],
                                          C0[:, 2 * d + k, :], start=(k == 0), stop=(k == 1))
                            ss = range(t + 1) if d == 0 else range(t, 4)
                        else:
                            ss = (4,)
                        for s in ss:
                            if t == 4:
                                o = PW - CTX
                            else:
                                o = OFF[d][s] + (t - s if d == 0 else t) * P
                            mm = pe.matmul(PS[3 + d][:, 0:DH + 1], Pm[:, d, o:o + P], vt[:, b, s, :],
                                           start=(s == ss[0]), stop=(s == ss[-1]))
                        mm.then_inc(sem("pv_done"), 1)

                def turn(h):
                    b = h % 2
                    pe.wait_ge(sem("hn_ready"), h + 1)
                    for r, bank in enumerate((5, 3, 4)):
                        n = 2 if r < 2 else 1
                        for f in range(2):
                            for t in range(n):
                                o = (f * n + t) * P
                                mm = pe.transpose(PS[bank][:, o:o + P], hacc[:, 2 * r + t, f * P:(f + 1) * P], ident)
                        if r == 2:
                            for k in range(2):
                                o = (2 + k) * P
                                mm = pe.transpose(PS[bank][:, o:o + P], qk[:, b, 2 + k, LAT:TOK], ident)
                        mm.then_inc(sem("h_turned"), 1)
                    pe.wait_ge(sem("kw_ready"), h + 1)
                    for n in range(4):
                        d, k = n // 2, n % 2
                        if n >= 2:
                            pe.wait_ge(sem("co_ready"), 4 * h + n - 1)
                        pe.matmul(PS[6 + k][:, 0:DH + 1], kw[:, d, k * P:(k + 1) * P], vt[:, b, 4, :], start=True,
                                  stop=True).then_inc(sem("c_done"), 1)

                proj_qk(0)
                proj_vo(0)
                for h in range(H):
                    scores(h)
                    if h + 1 < H:
                        proj_qk(h + 1)
                    values(h)
                    if h + 1 < H:
                        proj_vo(h + 1)
                    turn(h)

            @block.scalar
            def _(act):
                a = chain(act, "act")

                def out_qk(h):
                    for m in range(4):
                        u = 9 * h + m
                        act.wait_ge(sem("qk_done"), 5 * h + m + 1)
                        act.activation(qk[:, h % 2, m, 0:LAT], PS[u % 2][:, :], ACT.Copy,
                                       scale=DH ** -0.5 if m < 2 else 1.0).then_inc(sem("proj_copied"), 1)
                    act.wait_ge(sem("qk_done"), 5 * h + 5)
                    for x in range(2):
                        ins = act.activation(qk[:, h % 2, 2 * x:2 * x + 2, LAT:TOK],
                                             PS[2][:, 256 * x:256 * x + 256].rearrange("p (m t) -> p m t", m=2),
                                             ACT.Copy, scale=1.0 if x else DH ** -0.5)
                    ins.then_inc(sem("proj_copied"), 1)

                def out_vo(h):
                    for t in range(NT):
                        u = 9 * h + 4 + t
                        act.wait_ge(sem("vo_done"), NT * h + t + 1)
                        act.activation(vt[:, h % 2, t, 0:DH], PS[u % 2][:, 0:DH], ACT.Copy)
                        act.activation(og[:, h % 2, t, :], PS[u % 2][:, DH:2 * DH],
                                       ACT.Sigmoid).then_inc(sem("proj_copied"), 1)

                def decays(h):
                    act.wait_ge(sem("negmd_ready"), h + 1)
                    for s in range(NT):
                        for d in range(2):
                            col = colT[:, s, d, h:h + 1]
                            if s == 4:
                                act.activation(Pm[:, d, PW - CTX:PW], negMd[:, d, LAT:TOK], ACT.Exp, bias=col)
                                at = TOK - 1 if d == 0 else LAT
                                ins = act.activation(wk[:, d:d + 1], negMd[:, d, at:at + 1], ACT.Exp, bias=col)
                                continue
                            o = OFF[d][s]
                            dg = o if d == 0 else o + s * P
                            ins = act.activation(Pm[:, d, dg:dg + P], negMd[:, d, s * P:(s + 1) * P], ACT.Exp, bias=col)
                            if d == 0 and s < 3:
                                ins = act.activation(Pm[:, d, o + P:o + (4 - s) * P], PS[3][:, (s + 1) * P:LAT],
                                                     ACT.Exp, bias=col)
                            if d == 1 and s > 0:
                                ins = act.activation(Pm[:, d, o:o + s * P], PS[4][:, 0:s * P], ACT.Exp, bias=col)
                        ins.then_inc(sem("decay_ready"), 1)

                def inter(h):
                    for n in range(8):
                        t, d = n // 2, n % 2
                        act.wait_ge(sem("pv_done"), 10 * h + n + 1)
                        if n >= 2:
                            act.wait_ge(sem("nd_ready"), 10 * h + n - 1)
                        act.activation(Qs[:, d, :], PS[6 + d][:, 0:DH + 1], ACT.Copy,
                                       scale=colT[:, t, 2 + d, h:h + 1]).then_inc(sem("inter_ready"), 1)

                def finish(h):
                    act.wait_ge(sem("ms_inv"), h + 1)
                    act.activation(rs5[:], ssq[:], ACT.Sqrt).then_inc(sem("rs_ready"), 1)
                    for r, bank in enumerate((5, 3, 4)):
                        act.wait_ge(sem("h_turned"), 3 * h + r + 1)
                        w = 256 if r < 2 else P
                        for f in range(2):
                            ins = act.activation(haT[:, 2 * h + f, r * 256:r * 256 + w], PS[bank][:, f * w:(f + 1) * w],
                                                 ACT.Copy, scale=par[:, PC_HN + 2 * h + f:PC_HN + 2 * h + f + 1])
                        ins.then_inc(sem("ha_ready"), 1)
                    if h:
                        act.wait_ge(sem("c_out"), 32 * h)
                    for n in range(4):
                        act.wait_ge(sem("c_done"), 4 * h + n + 1)
                        act.activation(Co[:, n, :], PS[6 + n % 2][:, 0:DH + 1], ACT.Copy).then_inc(sem("co_ready"), 1)

                out_qk(0)
                out_vo(0)
                for h in range(H):
                    decays(h)
                    if h + 1 < H:
                        out_qk(h + 1)
                    inter(h)
                    if h + 1 < H:
                        out_vo(h + 1)
                    finish(h)

            @block.vector
            def _(dve):
                v = chain(dve, "dve")

                def weigh(h):
                    dve.wait_ge(sem("m_spread"), h + 1)
                    for d, mask in enumerate((mask_f, mask_b)):
                        dve.tensor_tensor(negMd[:, d, 0:LAT].rearrange("p (s t) -> p s t", s=4),
                                          PS[3 + d][:, :].rearrange("p (s t) -> p s t", s=4),
                                          bc(mask.unsqueeze(1), [P, 4, P]), ALU.add)
                        ins = dve.tensor_tensor(negMd[:, d, LAT:TOK], PS[5][:, d * P:(d + 1) * P], mask, ALU.add)
                    ins.then_inc(sem("negmd_ready"), 1)
                    for s in range(NT):
                        dve.wait_ge(sem("scores_done"), NT * h + s + 1)
                        dve.wait_ge(sem("decay_ready"), NT * h + s + 1)
                        for d in range(2):
                            if s == 4:
                                x, sc = Pm[:, d, PW - CTX:PW], PS[5][:, 2 * P:3 * P]
                            elif d == 0:
                                x, sc = Pm[:, 0, OFF[0][s]:OFF[0][s] + (4 - s) * P], PS[6 + s % 2][:, s * P:LAT]
                            else:
                                x, sc = Pm[:, 1, OFF[1][s]:OFF[1][s] + (s + 1) * P], PS[6 + s % 2][:, 0:(s + 1) * P]
                            ins = dve.tensor_tensor(x, x, sc, ALU.mult)
                        ins.then_inc(sem("p_ready"), 1)

                def combine(h):
                    for n in range(10):
                        t, d = n // 2, n % 2
                        dve.wait_ge(sem("pv_done"), 10 * h + n + 1)
                        if t < 4:
                            dve.wait_ge(sem("inter_ready"), 8 * h + n + 1)
                            dve.tensor_tensor(nd[:, d, :], PS[3 + d][:, 0:DH + 1], Qs[:, d, :],
                                              ALU.add).then_inc(sem("nd_ready"), 1)
                        else:
                            dve.tensor_copy(nd[:, d, :], PS[3 + d][:, 0:DH + 1]).then_inc(sem("nd_ready"), 1)
                        if d == 0:
                            continue
                        dve.wait_ge(sem("nd_ready"), 10 * h + n + 1)
                        v(dve.scalar_tensor_tensor(rr[:], nd[:, :, DH], -1.0, nd[:, :, DH], ALU.mult, ALU.max))
                        v(dve.tensor_tensor(rr[:], rr[:], colT[:, t, 4:6, h], ALU.max))
                        v(dve.reciprocal(rr[:], rr[:]))
                        x = hacc[:, t, :]
                        v(dve.tensor_scalar(x, nd[:, 0, 0:DH], rr[:, 0:1], None, ALU.mult))
                        v(dve.scalar_tensor_tensor(x, nd[:, 1, 0:DH], rr[:, 1:2], x, ALU.mult, ALU.add))
                        dve.wait_ge(sem("proj_copied"), 10 * h + 5 + t + 1)
                        v(dve.tensor_tensor(x, x, og[:, h % 2, t, :], ALU.mult))
                        v(dve.scalar_tensor_tensor(junk[:], x, 1.0, x, ALU.mult, ALU.mult, accum_out=ssq[:, t:t + 1]))

                def finish(h):
                    v(dve.tensor_scalar(ssq[:], ssq[:], 1.0 / DH, EPS, ALU.mult, ALU.add))
                    dve.reciprocal(ssq[:], ssq[:]).then_inc(sem("ms_inv"), 1)
                    dve.wait_ge(sem("rs_ready"), h + 1)
                    for t in range(NT):
                        ins = dve.tensor_scalar(hacc[:, t, :], hacc[:, t, :], rs5[:, t:t + 1], None, ALU.mult)
                    ins.then_inc(sem("hn_ready"), 1)
                    dve.wait_ge(sem("ha_ready"), 3 * h + 3)
                    for d in range(2):
                        ins = dve.tensor_scalar(kw[:, d, :], PS[4][:, 2 * P:4 * P], wk[:, d:d + 1], None, ALU.mult)
                    ins.then_inc(sem("kw_ready"), 1)

                dve.tensor_copy(selH[:], bc(ident[0:H, 0:H].unsqueeze(2), [H, H, P])).then_inc(sem("sel_ready"), 1)
                dve.memset(vt[:, :, :, DH:DH + 1], 1.0).then_inc(sem("ones_set"), 1)
                for h in range(H):
                    weigh(h)
                    combine(h)
                    finish(h)

        PLACE = {"w1": (2, 7, 4), "w3": (3, 8, 0), "w2": (6, 5, 1)}
        we1 = ar["w_e1"][0].rearrange("e (k p) f -> p e k f", p=P)
        we3 = ar["w_e3"][0].rearrange("e (k p) f -> p e k f", p=P)
        we2 = ar["w_e2"][0].rearrange("e (t p) d -> p e t d", p=P)

        def load_up(sp, name, e, q):
            src = we1 if name == "w1" else we3
            c = q * FT * P
            dst = place[:, PLACE[name][q % NRAW]].rearrange("p (k f) -> p k f", k=KD)
            sp.dma_start(dst, src[:, bass.ds(e, 1), :, c:c + FT * P].rearrange("p e k f -> p (e k) f")
                         ).then_inc(sem(f"{name}_in{q % NRAW}"), 16)

        def load_w2(sp, e, q):
            dst = place[:, PLACE["w2"][q % NRAW]].rearrange("p (t d) -> p t d", t=FT)
            sp.dma_start(dst, we2[:, bass.ds(e, 1), q * FT:(q + 1) * FT, :].rearrange("p e t d -> p (e t) d")
                         ).then_inc(sem(f"w2_in{q % NRAW}"), 16)

        with ExitStack() as st:
            mg = sb("mg", [P, KD, TOK], F32, st)
            sg = sb("sg2", [P, 4, TOK], F32, st)
            tm = sb("tm", [P, 2, TH], F32, st)
            tmp = sb("tmp6", [P, TOK], F32, st)
            AHEAD, RING = 2, 3
            a_h = sb("a_h", [P, RING, TOK], F32R, st)
            a_l = sb("a_l", [P, RING, TOK], F32R, st)
            w_h = sb("w_h", [P, RING, 512], F32R, st)
            w_l = sb("w_l", [P, RING, 512], F32R, st)

            def operands(n):
                kind, m, k = steps[n]
                act_of = {"G": hT, "A": haT, "B": hbT, "O": mg}[kind]
                c = CH_O + m if kind == "O" else CH_M + 2 * m + (0 if kind == "G" else 1)
                lo, hi = {"G": (0, 512), "A": (0, 256), "B": (256, 512), "O": (0, 512)}[kind]
                return act_of[:, k, :], c, wslot(c)[:, k, lo:hi], (hi - lo), lo // P

            def after_step(n, kinds, leave):
                if n >= AHEAD:
                    kind, m, k = steps[n - AHEAD]
                    if kind in kinds and ends[kind + str(m)] == n - AHEAD + 1:
                        leave(kind, m)

            block = st.enter_context(nc.Block())

            @block.sync
            def _(sp):
                with nc.allow_non_contiguous_dma(reason="small"):
                    sp.dma_start(wr[:], ar["w_router"][0].rearrange("(k p) e -> p k e", p=P)).then_inc(sem("wr_in"), 16)
                load_weights(sp, len(plan))
                sp.wait_ge(sem("parts_ready"), ends["B3"])
                load_up(sp, "w1", 0, 0)
                load_up(sp, "w3", 0, 0)
                load_w2(sp, 0, 0)
                load_up(sp, "w1", 0, 1)
                load_up(sp, "w3", 0, 1)
                sp.wait_ge(sem("parts_ready"), ends["O0"])
                load_w2(sp, 0, 1)

            @block.tensor
            def _(pe):
                for n, (kind, m, k) in enumerate(steps):
                    _, _, _, width, j0 = operands(n)
                    pe.wait_ge(sem("parts_ready"), n + 1)
                    for j in range(width // P):
                        for x in range(2):
                            bank = 2 * (j0 + j) + x
                            if k == 0:
                                if kind in "AB":
                                    pe.wait_ge(sem("gate_sig"), 8 * m + bank + 1)
                                elif kind == "O" and m:
                                    pe.wait_ge(sem("x2_ready"), j + 1)
                                elif m or kind == "O":
                                    pe.wait_ge(sem("branch_used"), 8 * (m - 1 if kind == "G" else 3) + bank + 1)
                            for i, (wp, ap) in enumerate(((w_h, a_h), (w_h, a_l), (w_l, a_h))):
                                mm = pe.matmul(PS[bank][:, 0:TH], wp[:, n % RING, j * P:(j + 1) * P],
                                               ap[:, n % RING, x * TH:(x + 1) * TH], start=(k == 0 and i == 0),
                                               stop=(i == 2 and n + 1 == ends[kind + str(m)]))
                    mm.then_inc(sem("step_done"), 1)
                pe.wait_ge(sem("x2_ready"), 5)
                pe_mean_square(pe, 1)
                pe.wait_ge(sem("wr_in"), 16)
                for k in range(KD):
                    pe.wait_ge(sem("modulated"), 8 + k + 1)
                    pe.matmul(PS[2][0:E, :], wr[:, k, :], hT[:, k, 0:LAT], start=(k == 0), stop=(k == 7))
                    mm = pe.matmul(PS[3][0:E, 0:CTX], wr[:, k, :], hT[:, k, LAT:TOK], start=(k == 0), stop=(k == 7))
                mm.then_inc(sem("logits_done"), 1)

            @block.scalar
            def _(act):
                def sigmoids(kind, m):
                    act.wait_ge(sem("step_done"), ends[kind + str(m)])
                    if m:
                        act.wait_ge(sem("branch_used"), 8 * m)
                    for b in range(8):
                        act.activation(sg[:, b // 2, (b % 2) * TH:(b % 2 + 1) * TH], PS[b][:, 0:TH],
                                       ACT.Sigmoid).then_inc(sem("gate_sig"), 1)

                for n, (kind, m, k) in enumerate(steps):
                    a_raw, c, w_raw, width, _ = operands(n)
                    have_weights(act, c)
                    if kind == "O":
                        act.wait_ge(sem("mg_ready"), k // 2 + 1)
                    if n >= RING:
                        act.wait_ge(sem("step_done"), n - RING + 1)
                    act.activation(a_h[:, n % RING, :], a_raw, ACT.Copy)
                    act.activation(w_h[:, n % RING, 0:width], w_raw, ACT.Copy).then_inc(sem("high_ready"), 1)
                    after_step(n, "G", sigmoids)
                for k in range(KD):
                    act.wait_ge(sem("x2_ready"), k + 1)
                    act_square(act, 1, k)
                act_rms(act, 1, tmp)
                act_modulate(act, 1, hT)

            @block.vector
            def _(dve):
                v = chain(dve, "dve")
                def leave(kind, m):
                    dve.wait_ge(sem("step_done"), ends[kind + str(m)])
                    if kind == "A":
                        dve.wait_ge(sem("gate_sig"), 8 * m + 4)
                        for b in range(4):
                            t = slice((b % 2) * TH, (b % 2 + 1) * TH)
                            dve.tensor_tensor(mg[:, 2 * m + b // 2, t], sg[:, b // 2, t], PS[b][:, 0:TH],
                                              ALU.mult).then_inc(sem("branch_used"), 1)
                    elif kind == "B":
                        dve.wait_ge(sem("gate_sig"), 8 * m + 8)
                        for b in range(4):
                            t = slice((b % 2) * TH, (b % 2 + 1) * TH)
                            dve.wait_ge(sem("order_dve"), v.n)
                            dve.tensor_tensor(tm[:, b % 2, :], sg[:, 2 + b // 2, t], PS[4 + b][:, 0:TH],
                                              ALU.mult).then_inc(sem("branch_used"), 1)
                            dve.wait_ge(sem("branch_used"), 8 * m + 4 + b + 1)
                            x = mg[:, 2 * m + b // 2, t]
                            ins = dve.tensor_tensor(x, x, tm[:, b % 2, :], ALU.add)
                            if b == 3:
                                ins.then_inc(sem("mg_ready"), 1)
                                dve.wait_ge(sem("mg_ready"), m + 1)
                            else:
                                v(ins)
                    else:
                        for j in range(4):
                            x = xT[:, 4 * m + j, :]
                            g = modT[:, 16 + 4 * m + j, :]
                            dve.scalar_tensor_tensor(x[:, 0:TH], PS[2 * j][:, 0:TH], g[:, 0:1], x[:, 0:TH],
                                                     ALU.mult, ALU.add)
                            dve.scalar_tensor_tensor(x[:, TH:LAT], PS[2 * j + 1][:, 0:LAT - TH], g[:, 0:1],
                                                     x[:, TH:LAT], ALU.mult, ALU.add)
                            dve.scalar_tensor_tensor(x[:, LAT:TOK], PS[2 * j + 1][:, LAT - TH:TH], g[:, 1:2],
                                                     x[:, LAT:TOK], ALU.mult, ALU.add).then_inc(sem("x2_ready"), 1)

                for n in range(len(steps)):
                    a_raw, _, w_raw, width, _ = operands(n)
                    dve.wait_ge(sem("high_ready"), n + 1)
                    dve.tensor_tensor(a_l[:, n % RING, :], a_raw, a_h[:, n % RING, :].bitcast(F32), ALU.subtract)
                    dve.tensor_tensor(w_l[:, n % RING, 0:width], w_raw, w_h[:, n % RING, 0:width].bitcast(F32),
                                      ALU.subtract).then_inc(sem("parts_ready"), 1)
                    after_step(n, "ABO", leave)
                leave("O", 1)
                dve_gain(dve, 1, PC_NFFN).then_inc(sem("gain_ready"), 1)
                dve_inverse_mean(dve, v, 1, tmp)
                dve_normalise(dve, 1)
        acts.close()

        moe = ctx.enter_context(ExitStack())
        gval = sb("gval", [CAP, E], F32, moe)
        gidx = sb("gidx", [CAP, E], I32, moe)
        with ExitStack() as st:
            lgT = rsb[0:E, :]
            lg = sb("lg", [P, NT, E], F32, st)
            mx = sb("mx", [P, NT], F32, st)
            af = sb("af", [E, TOK], F32, st)
            topv = sb("topv", [E, CAP], F32, st)
            topi = sb("topi", [E, CAP], U32, st)
            topf = sb("topf", [E, CAP], F32, st)
            block = st.enter_context(nc.Block())

            def token_rows(t):
                return place[:, (0, 0, 1, 1, 4)[t], (t % 2) * D:(t % 2 + 1) * D]

            @block.sync
            def _(sp):
                sp.wait_ge(sem("h2_out"), 16 * NT)
                load_up(sp, "w1", 0, 2)
                load_up(sp, "w3", 0, 2)
                load_w2(sp, 0, 2)

            @block.gpsimd
            def _(pool):
                for t in range(NT):
                    pool.wait_ge(sem("htok_ready"), t + 1)
                    pool.dma_start(ar["h2"][t * P:(t + 1) * P, :], token_rows(t)).then_inc(sem("h2_out"), 16)
                pool.wait_ge(sem("h2_out"), 16 * NT)

            @block.tensor
            def _(pe):
                pe.wait_ge(sem("lgT_ready"), 1)
                for t in range(NT):
                    mm = pe.transpose(PS[7][:, E * t:E * t + E], lgT[:, t * P:(t + 1) * P], ident[0:E, 0:E])
                mm.then_inc(sem("logits_turned"), 1)
                for t in range(NT):
                    if t >= 2:
                        pe.wait_ge(sem("htok_ready"), t - 1)
                    for k in range(KD):
                        mm = pe.transpose(PS[1 + 2 * (t % 2) + k // 4][:, (k % 4) * P:(k % 4 + 1) * P],
                                          hT[:, k, t * P:(t + 1) * P], ident)
                    mm.then_inc(sem("h2_turned"), 1)
                pe.wait_ge(sem("aff_ready"), 1)
                for t in range(NT):
                    mm = pe.transpose(PS[5 + t // 4][0:E, (t % 4) * P:(t % 4 + 1) * P], lg[:, t, :], ident)
                mm.then_inc(sem("aff_turned"), 1)
                pe.wait_ge(sem("top_ready"), 1)
                pe.transpose(PS[7][0:CAP, 0:E], topv[:], ident[0:E, 0:E])
                pe.transpose(PS[7][0:CAP, E:2 * E], topf[:], ident[0:E, 0:E]).then_inc(sem("top_turned"), 1)

            @block.scalar
            def _(act):
                act.wait_ge(sem("lg_shifted"), 1)
                act.activation(lg[:], lg[:], ACT.Exp).then_inc(sem("lg_exp"), 1)
                for t in range(NT):
                    act.wait_ge(sem("h2_turned"), t + 1)
                    for x in range(2):
                        ins = act.activation(token_rows(t)[:, x * 512:(x + 1) * 512], PS[1 + 2 * (t % 2) + x][:, :],
                                             ACT.Copy)
                    ins.then_inc(sem("htok_ready"), 1)

            @block.vector
            def _(dve):
                v = chain(dve, "dve")
                dve.wait_ge(sem("logits_done"), 1)
                dve.tensor_copy(lgT[:, 0:LAT], PS[2][0:E, :])
                dve.tensor_copy(lgT[:, LAT:TOK], PS[3][0:E, 0:CTX]).then_inc(sem("lgT_ready"), 1)
                dve.wait_ge(sem("logits_turned"), 1)
                v(dve.tensor_tensor(lg[:], PS[7][:, 0:NT * E].rearrange("p (t e) -> p t e", t=NT),
                                    bc(par[:, PC_BR:PC_BR + E].unsqueeze(1), [P, NT, E]), ALU.add))
                v(dve.tensor_reduce(mx[:], lg[:], AX.X, ALU.max))
                dve.tensor_tensor(lg[:], lg[:], bc(mx[:].unsqueeze(2), [P, NT, E]),
                                  ALU.subtract).then_inc(sem("lg_shifted"), 1)
                dve.wait_ge(sem("lg_exp"), 1)
                v(dve.tensor_reduce(mx[:], lg[:], AX.X, ALU.add))
                v(dve.reciprocal(mx[:], mx[:]))
                dve.tensor_tensor(lg[:], lg[:], bc(mx[:].unsqueeze(2), [P, NT, E]),
                                  ALU.mult).then_inc(sem("aff_ready"), 1)
                dve.wait_ge(sem("aff_turned"), 1)
                dve.tensor_copy(af[:, 0:LAT], PS[5][0:E, :])
                v(dve.tensor_copy(af[:, LAT:TOK], PS[6][0:E, 0:CTX]))
                for lo, hi, at, cap in ((0, LAT, 0, CAPL), (LAT, TOK, CAPL, CAPC)):
                    for o in range(at, at + cap, 8):
                        v(dve.max(topv[:, o:o + 8], af[:, lo:hi]))
                        v(dve.max_index(topi[:, o:o + 8], topv[:, o:o + 8], af[:, lo:hi]))
                        if o + 8 < at + cap:
                            v(dve.match_replace(af[:, lo:hi], topv[:, o:o + 8], af[:, lo:hi], -1.0))
                v(dve.tensor_copy(topf[:], topi[:]))
                dve.tensor_scalar(topf[:, CAPL:CAP], topf[:, CAPL:CAP], float(LAT), None,
                                  ALU.add).then_inc(sem("top_ready"), 1)
                dve.wait_ge(sem("top_turned"), 1)
                dve.tensor_copy(gval[:], PS[7][0:CAP, 0:E])
                dve.tensor_copy(gidx[:], PS[7][0:CAP, E:2 * E])

        with ExitStack() as st:
            rows = hT[:].rearrange("p k t -> p (k t)")
            xe = rows[0:CAP, 0:2 * D].rearrange("p (b d) -> p b d", b=2)
            ys = rows[0:CAP, 2 * D:4 * D].rearrange("p (b d) -> p b d", b=2)
            HC, HF = FT * CAP, FT * P
            sl, hid = (rows[0:CAP, (4 + x) * D - x * D // 2:(4 + x) * D - x * D // 2 + D // 2].rearrange("p (b n) -> p b n", b=2)
                       for x in range(2))
            flag = sb("flag", [1, 1], F32, st)
            x_h = sb("x_h", [P, 2, KD, CAP], F32R, st)
            x_l = sb("x_l", [P, 2, KD, CAP], F32R, st)
            hid_h = sb("hid_h", [P, 2, HC], F32R, st)
            hid_l = sb("hid_l", [P, 2, HC], F32R, st)
            PR = 4
            p_h = sb("p_h", [P, PR, KD * HF], F32R, st)
            p_l = sb("p_l", [P, PR, KD * HF], F32R, st)

            def parts(o, q, name):
                r = (3 * (o + q) + {"w1": 0, "w3": 1, "w2": 5}[name]) % PR
                return p_h[:, r, :], p_l[:, r, :]

            def up_tiles(ap):
                return ap.rearrange("p (k f) -> p k f", k=KD)

            def down_tiles(ap):
                return ap.rearrange("p (t d) -> p t d", t=FT)

            def raw(q, name):
                return place[:, PLACE[name][q % NRAW], :]

            block = st.enter_context(nc.Block())

            def known(i, o, q, least):
                return not isinstance(i, int) or 2 * FG * i + o + q >= least

            def landed_at(i, o, q):
                return 16 * (2 * FG // NRAW) * i + 16 * ((o + q) // NRAW + 1)

            def experts(eng, begin, step, after=0):
                def half(i, o, h, coming=None):
                    for x, q in enumerate(range(h * FG // 2, (h + 1) * FG // 2)):
                        if coming and x == after:
                            begin(*coming)
                        step(i, o, q)

                if after:
                    step(0, 0, 0)
                begin(0, 0)
                for q in range(1 if after else 0, FG // 2):
                    step(0, 0, q)
                half(0, 0, 1, (0, 1))
                half(0, FG, 0)
                with eng.Fori(1, E // 2) as i:
                    half(i, -FG, 1, (i, 0))
                    half(i, 0, 0)
                    half(i, 0, 1, (i, 1))
                    half(i, FG, 0)
                half(E // 2 - 1, FG, 1)

            @block.sync
            def _(sp):
                def pieces(e, q):
                    sp.wait_ge(sem("w1_split"), FG * e + (q - NRAW + 1))
                    load_up(sp, "w1", e, q)
                    sp.wait_ge(sem("w3_split"), FG * e + (q - NRAW + 1))
                    load_up(sp, "w3", e, q)
                    sp.wait_ge(sem("w2_split"), FG * e + (q - NRAW))
                    if q:
                        load_w2(sp, e, q - 1)
                    else:
                        load_w2(sp, e - 1, FG - 1)

                sp.wait_ge(sem("w1_split"), 1)
                load_up(sp, "w1", 0, 3)
                sp.wait_ge(sem("w3_split"), 1)
                load_up(sp, "w3", 0, 3)
                for q in (4, 5):
                    pieces(0, q)
                with sp.Fori(1, E) as e:
                    for q in range(FG):
                        pieces(e, q)
                sp.wait_ge(sem("w2_split"), FG * E - NRAW)
                load_w2(sp, E - 1, FG - 1)

            @block.gpsimd
            def _(pool):
                def gather(e):
                    if e >= 2:
                        pool.wait_ge(sem("x_turned"), e - 1)
                    pool.indirect_dma_start(out=xe[:, e % 2, :], out_offset=None, in_=ar["h2"][:, :],
                                            in_offset=bass.IndirectOffsetOnAxis(ap=gidx[:, e:e + 1], axis=0)
                                            ).then_inc(sem(f"xe_in{e % 2}"), 16)

                def scatter(e):
                    pool.wait_ge(sem("y_ready"), e + 1)
                    if e:
                        pool.wait_ge(sem(f"y_out{(e - 1) % 2}"), 16 * ((e - 1) // 2 + 1))
                    pool.memset(flag[:], 0.0).then_inc(sem("ys_free"), 1)
                    pool.wait_ge(sem("ys_free"), e + 1)
                    pool.indirect_dma_start(out=ar["moe"][:, :],
                                            out_offset=bass.IndirectOffsetOnAxis(ap=gidx[:, e:e + 1], axis=0),
                                            in_=ys[:, e % 2, :], in_offset=None, compute_op=ALU.add
                                            ).then_inc(sem(f"y_out{e % 2}"), 16)

                gather(0)
                gather(1)
                for e in range(E):
                    if e + 2 < E:
                        gather(e + 2)
                    scatter(e)
                pool.wait_ge(sem("y_out0"), 16 * E // 2)
                pool.wait_ge(sem("y_out1"), 16 * E // 2)

            PARTS = ((0, 0), (0, 1), (1, 0))

            @block.tensor
            def _(pe):
                def begin(i, u):
                    pe.wait_ge(sem(f"xe_in{u}"), 16 * i + 16)
                    for k in range(KD):
                        mm = pe.transpose(PS[4 + k // 4][:, (k % 4) * CAP:(k % 4 + 1) * CAP],
                                          xe[:, u, k * P:(k + 1) * P], ident[0:CAP, 0:CAP])
                    mm.then_inc(sem("x_turned"), 1)

                def down(i, o, q):
                    n = 2 * FG * i + (o + q)
                    if q == 0 and known(i, o, q, FG):
                        pe.wait_ge(sem("y_ready"), 2 * i + o // FG)
                    pe.wait_ge(sem("hid_split"), n + 1)
                    pe.wait_ge(sem("w2_split"), n + 1)
                    w2p = [down_tiles(x) for x in parts(o, q, "w2")]
                    for t in range(FT):
                        for x in range(2):
                            for j, (a, b) in enumerate(PARTS):
                                mm = pe.matmul(PS[2 + x][0:CAP, :], (hid_h, hid_l)[a][:, q % 2, t * CAP:(t + 1) * CAP],
                                               w2p[b][:, t, x * 512:(x + 1) * 512],
                                               start=(q == 0 and t == 0 and j == 0),
                                               stop=(q == FG - 1 and t == FT - 1 and j == 2))
                    mm.then_inc(sem("down_done"), 1)

                def turn(i, o, q):
                    pe.wait_ge(sem("hid_ready"), 2 * FG * i + (o + q + 1))
                    for t in range(FT):
                        mm = pe.transpose(PS[6 + q % 2][:, t * CAP:(t + 1) * CAP], hid[:, q % 2, t * P:(t + 1) * P],
                                          ident[0:CAP, 0:CAP])
                    mm.then_inc(sem("hid_turned"), 1)

                def step(i, o, q):
                    n = 2 * FG * i + (o + q)
                    u = (o // FG) % 2
                    if q == 0:
                        pe.wait_ge(sem("x_split"), 2 * i + (o // FG + 1))
                    if known(i, o, q, 2):
                        pe.wait_ge(sem("hid_ready"), n - 1)

                    def up(name, at):
                        pe.wait_ge(sem(f"{name}_split"), n + 1)
                        wp = [up_tiles(x) for x in parts(o, q, name)]
                        for k in range(KD):
                            for j, (a, b) in enumerate(PARTS):
                                mm = pe.matmul(PS[q % 2][0:CAP, at:at + HF], (x_h, x_l)[a][:, u, k, :], wp[b][:, k, :],
                                               start=(k == 0 and j == 0), stop=(k == 7 and j == 2))
                        return mm

                    up("w1", 0).then_inc(sem("w1_done"), 1)
                    if q:
                        turn(i, o, q - 1)
                    elif known(i, o, q, 1):
                        turn(i, o - FG, FG - 1)
                    mm = up("w3", HF)
                    mm.then_inc(sem("hidden_done"), 1)
                    if q:
                        down(i, o, q - 1)
                    elif known(i, o, q, 1):
                        down(i, o - FG, FG - 1)

                experts(pe, begin, step)
                turn(E // 2 - 1, FG, FG - 1)
                down(E // 2 - 1, FG, FG - 1)

            @block.scalar
            def _(act):
                def begin(i, u):
                    act.wait_ge(sem("x_turned"), 2 * i + (u + 1))
                    for x in range(2):
                        ins = act.activation(x_h[:, u, 4 * x:4 * x + 4, :].rearrange("p k c -> p (k c)"),
                                             PS[4 + x][:, 0:4 * CAP], ACT.Copy)
                    ins.then_inc(sem("x_high"), 1)

                def high(i, o, q, name):
                    act.wait_ge(sem(f"{name}_in{q % NRAW}"), landed_at(i, o, q))
                    act.activation(parts(o, q, name)[0], raw(q, name), ACT.Copy).then_inc(sem(f"{name}_high"), 1)

                def finish(i, o, q):
                    n = 2 * FG * i + (o + q)
                    act.wait_ge(sem("hidden_done"), n + 1)
                    if known(i, o, q, 2):
                        act.wait_ge(sem("hid_ready"), n - 1)
                    act.activation(sl[:, q % 2, :], PS[q % 2][0:CAP, 0:HF], ACT.Silu).then_inc(sem("silu_ready"), 1)
                    high(i, o, q, "w2")
                    if known(i, o, q, 2):
                        act.wait_ge(sem("down_done"), n - 1)
                    act.wait_ge(sem("hid_turned"), n + 1)
                    act.activation(hid_h[:, q % 2, :], PS[6 + q % 2][:, 0:HC], ACT.Copy).then_inc(sem("hid_high"), 1)

                def step(i, o, q):
                    n = 2 * FG * i + (o + q)
                    if known(i, o, q, 3):
                        act.wait_ge(sem("down_done"), n - 2)
                    high(i, o, q, "w1")
                    if known(i, o, q, 1):
                        act.wait_ge(sem("w1_done"), n)
                    high(i, o, q, "w3")
                    if q:
                        finish(i, o, q - 1)
                    elif known(i, o, q, 1):
                        finish(i, o - FG, FG - 1)

                experts(act, begin, step, after=1)
                finish(E // 2 - 1, FG, FG - 1)

            @block.vector
            def _(dve):
                def begin(i, u):
                    dve.wait_ge(sem("x_high"), 2 * i + (u + 1))
                    for x in range(2):
                        ks = slice(4 * x, 4 * x + 4)
                        ins = dve.tensor_tensor(x_l[:, u, ks, :], PS[4 + x][:, 0:4 * CAP].rearrange("p (k c) -> p k c", k=4),
                                                x_h[:, u, ks, :].bitcast(F32), ALU.subtract)
                    ins.then_inc(sem("x_split"), 1)

                def low(i, o, q, name):
                    dve.wait_ge(sem(f"{name}_high"), 2 * FG * i + (o + q + 1))
                    h, l = parts(o, q, name)
                    dve.tensor_tensor(l, raw(q, name), h.bitcast(F32), ALU.subtract).then_inc(sem(f"{name}_split"), 1)

                def take_y(i, o):
                    dve.wait_ge(sem("down_done"), 2 * FG * i + (o + FG))
                    s = (o // FG) % 2
                    if known(i, o, 0, 2 * FG):
                        dve.wait_ge(sem("ys_free"), 2 * i + o // FG)
                    g = gval[:, bass.ds(2 * i + o // FG, 1)]
                    dve.tensor_scalar(ys[:, s, 0:512], PS[2][0:CAP, :], g, None, ALU.mult)
                    dve.tensor_scalar(ys[:, s, 512:D], PS[3][0:CAP, :], g, None, ALU.mult).then_inc(sem("y_ready"), 1)

                def finish(i, o, q):
                    n = 2 * FG * i + (o + q)
                    dve.wait_ge(sem("silu_ready"), n + 1)
                    if known(i, o, q, 2):
                        dve.wait_ge(sem("hid_turned"), n - 1)
                    dve.tensor_tensor(hid[:, q % 2, :], sl[:, q % 2, :], PS[q % 2][0:CAP, HF:2 * HF],
                                      ALU.mult).then_inc(sem("hid_ready"), 1)
                    low(i, o, q, "w2")
                    dve.wait_ge(sem("hid_high"), n + 1)
                    dve.tensor_tensor(hid_l[:, q % 2, :], PS[6 + q % 2][:, 0:HC], hid_h[:, q % 2, :].bitcast(F32),
                                      ALU.subtract).then_inc(sem("hid_split"), 1)

                def step(i, o, q):
                    low(i, o, q, "w1")
                    low(i, o, q, "w3")
                    if q == 1 and known(i, o, q, FG):
                        take_y(i, o - FG)
                    if q:
                        finish(i, o, q - 1)
                    elif known(i, o, q, 1):
                        finish(i, o - FG, FG - 1)

                experts(dve, begin, step, after=1)
                finish(E // 2 - 1, FG, FG - 1)
                take_y(E // 2 - 1, FG)
        moe.close()

        with ExitStack() as st:
            mt = sb("mt", [P, NT, D], F32, st)
            yT = sb("yT", [P, KD, TOK], F32, st)
            tmp = sb("tmp9", [P, TOK], F32, st)
            block = st.enter_context(nc.Block())

            @block.sync
            def _(sp):
                for t in range(NT):
                    sp.dma_start(mt[:, t, :], ar["moe"][t * P:(t + 1) * P, :]).then_inc(sem("mt_in"), 16)
                for k in range(KD):
                    sp.wait_ge(sem("y_done"), k + 1)
                    sp.dma_start(out["yT"][:, k, :], yT[:, k, :]).then_inc(sem("yT_out"), 16)
                sp.wait_ge(sem("yT_out"), 16 * KD)

            @block.tensor
            def _(pe):
                pe.wait_ge(sem("mt_in"), 16 * NT)
                for k in range(KD):
                    if k >= 3:
                        pe.wait_ge(sem("x3_ready"), k - 2)
                    for t in range(NT):
                        dst = PS[k % 3][:, t * P:(t + 1) * P] if t < 4 else PS[3 + k % 3][:, 0:CTX]
                        mm = pe.transpose(dst, mt[:, t, k * P:(k + 1) * P], ident)
                    mm.then_inc(sem("moe_turned"), 1)
                pe_mean_square(pe, 2)

            @block.scalar
            def _(act):
                for k in range(KD):
                    act.wait_ge(sem("x3_ready"), k + 1)
                    act_square(act, 2, k)
                act_rms(act, 2, tmp)

            @block.vector
            def _(dve):
                v = chain(dve, "dve")
                for k in range(KD):
                    dve.wait_ge(sem("moe_turned"), k + 1)
                    dve.scalar_tensor_tensor(xT[:, k, 0:LAT], PS[k % 3][:, :], modT[:, 40 + k, 0:1], xT[:, k, 0:LAT],
                                             ALU.mult, ALU.add)
                    dve.scalar_tensor_tensor(xT[:, k, LAT:TOK], PS[3 + k % 3][:, 0:CTX], modT[:, 40 + k, 1:2],
                                             xT[:, k, LAT:TOK], ALU.mult, ALU.add).then_inc(sem("x3_ready"), 1)
                dve_inverse_mean(dve, v, 2, tmp)
                dve.wait_ge(sem("rms"), 3)
                for k in range(KD):
                    dve.scalar_tensor_tensor(yT[:, k, :], xT[:, k, :], par[:, PC_NFIN + k:PC_NFIN + k + 1], rsb[:],
                                             ALU.mult, ALU.mult).then_inc(sem("y_done"), 1)


def _positions():
    q = D // 4
    n = np.arange(LAT)
    r, c = (n // 64).astype(np.float32), (n % 64).astype(np.float32)
    fr = (1.0 / (np.float32(10000.0) ** (np.arange(q, dtype=np.float32) / np.float32(q)))).astype(np.float32)
    er, ec = r[:, None] * fr, c[:, None] * fr
    return np.concatenate([np.sin(er), np.cos(er), np.sin(ec), np.cos(ec)], -1).astype(np.float32)


def _feature_major(a):
    return np.ascontiguousarray(np.asarray(a).reshape(a.shape[0], -1, P).transpose(2, 1, 0))


def kernel(**inputs):
    import concourse.bacc as bacc
    from concourse.bass_utils import run_bass_kernel_spmd

    i = {k: np.asarray(v) for k, v in inputs.items()}
    col = lambda a, n: np.asarray(a).reshape(n, P).T
    both = lambda a: np.concatenate([a, a], 0)
    dirp = lambda a: np.asarray(a).reshape(2, GN, SP_).transpose(0, 2, 1).reshape(P, GN)
    c2 = np.stack([i["c"][0], i["c_ctx"]])
    arrays = {}
    arrays["par"] = np.concatenate([
        _feature_major(c2).reshape(P, 16), col(i["b_ada"][0], 48), col(i["norm_mix"][0], 8), col(i["norm_ffn"][0], 8),
        col(i["norm_final"], 8), col(i["head_norm"][0].reshape(-1), 8), col(i["b_glu"][0], 4),
        np.broadcast_to(i["b_router"][0][None], (P, E))], 1)
    arrays["consts"] = np.stack([np.eye(P), np.where(np.arange(P)[None] >= np.arange(P)[:, None], 0, -1e30),
                                 np.where(np.arange(P)[None] <= np.arange(P)[:, None], 0, -1e30)],
                                1).astype(np.float32)
    arrays["xT"] = _feature_major(np.concatenate([i["x_sample"][0], i["x_prompt"][0]], 0))
    arrays["posT"] = _feature_major(_positions())
    arrays["gbias"] = i["b_gate"][0].reshape(4 * H, 1)
    arrays["gpar"] = np.concatenate([i["b_gate"][0].T, i["state_mlstm_m"][0, 0].T], 1)
    ldt = np.repeat(i["s5_log_dt"][0], SP_, 0).reshape(P, GN)
    arrays["s5p"] = np.stack([dirp(i["s5_a_re"][0]), dirp(i["s5_a_im"][0]), ldt,
                              dirp(i["state_s5_re"][0, 0]), dirp(i["state_s5_im"][0, 0])], 1)
    arrays["s5bc"] = np.stack(
        [both(i[n][0].transpose(1, 0, 2)) for n in ("s5_b_re", "s5_b_im")]
        + [i[n][0].transpose(0, 3, 1, 2).reshape(P, GN, GC) for n in ("s5_c_re", "s5_c_im")], 1)
    arrays["s5d"] = i["s5_d"][0].reshape(GN, GC).T
    arrays["Cn"] = np.concatenate([i["state_mlstm_C"][0, 0], i["state_mlstm_n"][0, 0][..., None]], -1)
    for n in ("w_ada", "w_in", "w_pA", "w_pB", "w_out", "w_glu", "w_router", "w_e1", "w_e3", "w_e2"):
        arrays[n] = i[n]
    arrays = {k: np.ascontiguousarray(a) for k, a in arrays.items()}

    nc = bacc.Bacc("TRN2", target_bir_lowering=False, num_devices=1)
    ar = {k: nc.dram_tensor(k + "_dram", a.shape, mybir.dt.from_np(a.dtype), kind="ExternalInput").ap()
          for k, a in arrays.items()}
    ar["moe"] = nc.dram_tensor("moe_dram", (TOK, D), F32, kind="Internal").ap()
    ar["u"] = nc.dram_tensor("u_dram", (SW, TOK), F32, kind="Internal").ap()
    ar["h2"] = nc.dram_tensor("h2_dram", (TOK, D), F32, kind="Internal").ap()
    shapes = {"yT": (P, KD, TOK), "Cn": (2, H, DH, DH + 1), "m": (2, H), "s5": (2, P, GN)}
    out = {k: nc.dram_tensor("out_" + k, s, F32, kind="ExternalOutput").ap() for k, s in shapes.items()}
    program(nc, ar, out)
    r = run_bass_kernel_spmd(nc, [{k + "_dram": a for k, a in arrays.items()}], core_ids=[0]).results[0]
    y = np.asarray(r["out_yT"]).transpose(2, 1, 0).reshape(TOK, D)
    Cn = np.asarray(r["out_Cn"])
    s5 = np.asarray(r["out_s5"]).reshape(2, 2, SP_, GN).transpose(0, 1, 3, 2)
    full = lambda a: np.ascontiguousarray(a)[None, None]
    return (np.ascontiguousarray(y[LAT:])[None], np.ascontiguousarray(y[:LAT])[None], full(Cn[..., :DH]),
            full(Cn[..., DH]), full(np.asarray(r["out_m"])), full(s5[0]), full(s5[1]))
```
